# Optimizing a Trainium2 kernel written in Bass

```python
import math
import jax, jax.numpy as jnp
from jax import lax
import numpy as np

D_MODEL = 1024
BATCH = 1
SEQ = 512
DEPTH = 1

CHUNK = 64
HEAD_DIM = 64
D_A = 384
HEADS_A = D_A // HEAD_DIM
D_B = 256
HEADS_B = D_B // HEAD_DIM
D_C = 384
HEADS_C = D_C // HEAD_DIM
D_MIX = D_A + D_B + D_C
IN_COLS = 2 * D_A + 3 * D_B + 2 * D_C
CONV_A_WIDTH = 31
CONV_B_WIDTH = 3
SG_BLOCK = 128
PEER_HEADS = 8
D_KEY = 256
N_KEYS = 128
N_EXPERTS = N_KEYS * N_KEYS
TOPK = 16
PEER_BLOCK = 128
PLE_DIM = 256
EPS = 1e-6


def rmsnorm(x, g):
    xf = x.astype(jnp.float32)
    y = xf * lax.rsqrt(jnp.mean(xf * xf, axis=-1, keepdims=True) + EPS)
    return (y * g.astype(jnp.float32)).astype(x.dtype)

def group_layernorm(x, g, b, heads):
    shp = x.shape
    xf = x.astype(jnp.float32).reshape(shp[:-1] + (heads, shp[-1] // heads))
    m = jnp.mean(xf, axis=-1, keepdims=True)
    var = jnp.mean(jnp.square(xf - m), axis=-1, keepdims=True)
    y = ((xf - m) * lax.rsqrt(var + EPS)).reshape(shp)
    return (y * g.astype(jnp.float32) + b.astype(jnp.float32)).astype(x.dtype)

def causal_dwconv(x, w):
    k = w.shape[0]
    return lax.conv_general_dilated(
        x, w.astype(x.dtype)[:, None, :], window_strides=(1,), padding=[(k - 1, 0)],
        dimension_numbers=("NWC", "WIO", "NWC"), feature_group_count=x.shape[-1])

def conformer_conv(za, conv_w, conv_b, ln_g, ln_b):
    val, gate = jnp.split(za, 2, axis=-1)
    y = val * jax.nn.sigmoid(gate)
    y = causal_dwconv(y, conv_w) + conv_b.astype(y.dtype)
    y = group_layernorm(y, ln_g, ln_b, HEADS_A)
    return jax.nn.silu(y)

def short_gated_conv(zb, conv_w):
    bg, cg, xb = jnp.split(zb, 3, axis=-1)
    return bg * causal_dwconv(cg * xb, conv_w)

def spatial_gating(zc, ln_g, ln_b, w_s, b_s):
    u, v = jnp.split(zc, 2, axis=-1)
    bsz, s, _ = v.shape
    v = group_layernorm(v, ln_g, ln_b, HEADS_C)
    vb = v.reshape(bsz, s // SG_BLOCK, SG_BLOCK, HEADS_C, HEAD_DIM)
    pos = jnp.arange(SG_BLOCK)
    mask = (pos[None, :] // CHUNK) <= (pos[:, None] // CHUNK)
    ws = jnp.where(mask[None], w_s, 0).astype(v.dtype)
    mixed = jnp.einsum("hij,bnjhc->bnihc", ws, vb) + b_s.T.astype(v.dtype)[None, None, :, :, None]
    return u * mixed.reshape(bsz, s, D_C)

def peer(n, w_q, sub_keys, expert_u, expert_v):
    bsz, s, d = n.shape
    t = bsz * s
    nf = n.reshape(t, d)
    q = (nf @ w_q).reshape(t, PEER_HEADS, D_KEY)
    q1, q2 = q[..., : D_KEY // 2], q[..., D_KEY // 2:]
    s1 = jnp.einsum("thd,hkd->thk", q1, sub_keys[:, 0])
    s2 = jnp.einsum("thd,hkd->thk", q2, sub_keys[:, 1])
    v1, i1 = lax.top_k(s1, TOPK)
    v2, i2 = lax.top_k(s2, TOPK)
    cand = (v1[..., :, None] + v2[..., None, :]).reshape(t, PEER_HEADS, TOPK * TOPK)
    vals, ci = lax.top_k(cand, TOPK)
    e1 = jnp.take_along_axis(i1, ci // TOPK, axis=-1)
    e2 = jnp.take_along_axis(i2, ci % TOPK, axis=-1)
    idx = (e1 * N_KEYS + e2).reshape(t, PEER_HEADS * TOPK)
    gates = jax.nn.softmax(vals.astype(jnp.float32), axis=-1).astype(n.dtype)
    gates = gates.reshape(t, PEER_HEADS * TOPK)
    nblk = t // PEER_BLOCK

    def block(args):
        xb, ib, gb = args
        ug = expert_u[ib]
        act = jax.nn.gelu(jnp.einsum("td,tkd->tk", xb, ug)) * gb
        vg = expert_v[ib]
        return jnp.einsum("tk,tkd->td", act, vg)

    out = lax.map(block, (nf.reshape(nblk, PEER_BLOCK, d),
                          idx.reshape(nblk, PEER_BLOCK, PEER_HEADS * TOPK),
                          gates.reshape(nblk, PEER_BLOCK, PEER_HEADS * TOPK)))
    return out.reshape(bsz, s, d)

def first_inputs(seed: int = 0) -> dict:
    key = jax.random.key(seed)
    ks = jax.random.split(key, 24)
    L, D = DEPTH, D_MODEL
    nrm = lambda k, shp, sc: jax.random.normal(k, shp, jnp.float32) * sc
    gain = lambda k, shp: 1.0 + 0.05 * jax.random.normal(k, shp, jnp.float32)
    return {
        "x": nrm(ks[0], (BATCH, SEQ, D), 1.0),
        "p": nrm(ks[1], (DEPTH, BATCH, SEQ, PLE_DIM), 1.0),
        "g_mix": gain(ks[2], (L, D)),
        "w_in": nrm(ks[3], (L, D, IN_COLS), D ** -0.5),
        "conv_a_w": nrm(ks[4], (L, CONV_A_WIDTH, D_A), CONV_A_WIDTH ** -0.5),
        "conv_a_b": nrm(ks[5], (L, D_A), 0.02),
        "ln_a_g": gain(ks[6], (L, D_A)),
        "ln_a_b": nrm(ks[7], (L, D_A), 0.02),
        "conv_b_w": nrm(ks[8], (L, CONV_B_WIDTH, D_B), CONV_B_WIDTH ** -0.5),
        "ln_c_g": gain(ks[9], (L, D_C)),
        "ln_c_b": nrm(ks[10], (L, D_C), 0.02),
        "w_s": nrm(ks[11], (L, HEADS_C, SG_BLOCK, SG_BLOCK), 0.5 * SG_BLOCK ** -0.5),
        "b_s": gain(ks[12], (L, HEADS_C, SG_BLOCK)),
        "w_out": nrm(ks[13], (L, D_MIX, D), D_MIX ** -0.5),
        "g_ffn": gain(ks[14], (L, D)),
        "w_q": nrm(ks[15], (L, D, PEER_HEADS * D_KEY), D ** -0.5),
        "sub_keys": nrm(ks[16], (L, PEER_HEADS, 2, N_KEYS, D_KEY // 2), (D_KEY // 2) ** -0.5),
        "expert_u": nrm(ks[17], (L, N_EXPERTS, D), D ** -0.5),
        "expert_v": nrm(ks[18], (L, N_EXPERTS, D), 0.1),
        "g_ple": gain(ks[19], (L, D)),
        "w_pe": nrm(ks[20], (L, PLE_DIM, D), PLE_DIM ** -0.5),
        "w_pg": nrm(ks[21], (L, D, D), D ** -0.5),
        "g_final": gain(ks[22], (D,)),
    }

def first_block(x, p, g_mix, w_in, conv_a_w, conv_a_b, ln_a_g, ln_a_b, conv_b_w, ln_c_g, ln_c_b,
              w_s, b_s, w_out, g_ffn, w_q, sub_keys, expert_u, expert_v, g_ple, w_pe, w_pg,
              g_final):
    h = x
    for i in range(DEPTH):
        a = rmsnorm(h, g_mix[i])
        z = a @ w_in[i]
        za = z[..., : 2 * D_A]
        zb = z[..., 2 * D_A: 2 * D_A + 3 * D_B]
        zc = z[..., 2 * D_A + 3 * D_B:]
        ya = conformer_conv(za, conv_a_w[i], conv_a_b[i], ln_a_g[i], ln_a_b[i])
        yb = short_gated_conv(zb, conv_b_w[i])
        yc = spatial_gating(zc, ln_c_g[i], ln_c_b[i], w_s[i], b_s[i])
        h = h + jnp.concatenate([ya, yb, yc], axis=-1) @ w_out[i]
        h = h + peer(rmsnorm(h, g_ffn[i]), w_q[i], sub_keys[i], expert_u[i], expert_v[i])
        gate = jax.nn.sigmoid(rmsnorm(h, g_ple[i]) @ w_pg[i])
        h = h + (p[i] @ w_pe[i]) * gate
    return rmsnorm(h, g_final)


DEPTH_2 = 2

N_MIXERS = 2
N_GLA = (DEPTH_2 + 1) // 2
N_MLA = DEPTH_2 // 2

GLA_HEADS = 4
GLA_DK = D_MODEL // 2 // GLA_HEADS
GLA_DV = D_MODEL // GLA_HEADS
GLA_GATE_RANK = 16
GLA_TAU = 16.0
GLA_CHUNK = 64

MLA_HEADS = 8
MLA_NOPE = 128
MLA_ROPE = 64
MLA_VDIM = 128
MLA_Q_RANK = 384
MLA_KV_RANK = 256
ROPE_THETA = 10000.0
Q_BLOCK = 128

D_FF = -(-8 * D_MODEL // (3 * 256)) * 256


def rmsnorm_2(t, g):
    tf = t.astype(jnp.float32)
    y = tf * lax.rsqrt(jnp.mean(tf * tf, axis=-1, keepdims=True) + EPS)
    return (y * g.astype(jnp.float32)).astype(t.dtype)

def modulate(t, g, shift, scale):
    return rmsnorm_2(t, g) * (1.0 + scale[:, None, :]) + shift[:, None, :]

def gla_chunked(q, k, v, log_a):
    B, S, H, DK = q.shape
    DV = v.shape[-1]
    C = GLA_CHUNK
    n = S // C

    def to_chunks(t):
        return t.astype(jnp.float32).reshape(B, n, C, H, t.shape[-1]).transpose(1, 0, 3, 2, 4)

    qc, kc, vc, gc = to_chunks(q), to_chunks(k), to_chunks(v), to_chunks(log_a)
    causal = jnp.tril(jnp.ones((C, C), dtype=bool))[:, :, None]

    def step(state, inp):
        qi, ki, vi, gi = inp
        b = jnp.cumsum(gi, axis=-2)
        o_inter = jnp.einsum('bhck,bhkv->bhcv', qi * jnp.exp(b), state)
        diff = b[:, :, :, None, :] - b[:, :, None, :, :]
        decay = jnp.exp(jnp.where(causal, diff, -jnp.inf))
        attn = jnp.einsum('bhik,bhjk,bhijk->bhij', qi, ki, decay)
        o_intra = jnp.einsum('bhij,bhjv->bhiv', attn, vi)
        b_last = b[:, :, -1:, :]
        new_state = state * jnp.exp(b_last[:, :, 0, :])[..., None] + jnp.einsum(
            'bhck,bhcv->bhkv', ki * jnp.exp(b_last - b), vi)
        return new_state, o_inter + o_intra

    state0 = jnp.zeros((B, H, DK, DV), jnp.float32)
    _, o = lax.scan(step, state0, (qc, kc, vc, gc))
    return o.transpose(1, 0, 3, 2, 4).reshape(B, S, H, DV)

def gla_mixer(h, w_in, w_gate, b_gate, g_out, w_out):
    B, S, _ = h.shape
    H, DK, DV = GLA_HEADS, GLA_DK, GLA_DV
    proj = h @ w_in
    q, k, v, r, glr = jnp.split(proj, [H * DK, 2 * H * DK, 2 * H * DK + H * DV,
                                       2 * H * DK + 2 * H * DV], axis=-1)
    q = q.reshape(B, S, H, DK) * (DK ** -0.5)
    k = k.reshape(B, S, H, DK)
    v = v.reshape(B, S, H, DV)
    r = r.reshape(B, S, H, DV)
    log_a = jax.nn.log_sigmoid((glr @ w_gate + b_gate).astype(jnp.float32)) / GLA_TAU
    o = gla_chunked(q, k, v, log_a.reshape(B, S, H, DK)).astype(h.dtype)
    o = rmsnorm_2(o, g_out) * jax.nn.silu(r)
    return o.reshape(B, S, H * DV) @ w_out

def apply_rope(t, cos, sin):
    tf = t.astype(jnp.float32).reshape(*t.shape[:-1], -1, 2)
    t1, t2 = tf[..., 0], tf[..., 1]
    out = jnp.stack([t1 * cos - t2 * sin, t1 * sin + t2 * cos], axis=-1).reshape(t.shape)
    return out.astype(t.dtype)

def mla_mixer(h, cos, sin, w_in, g_q, w_q_up, g_kv, w_kv_up, w_out):
    B, S, _ = h.shape
    H = MLA_HEADS
    proj = h @ w_in
    cq, ckv, k_rope = jnp.split(proj, [MLA_Q_RANK, MLA_Q_RANK + MLA_KV_RANK], axis=-1)
    q = (rmsnorm_2(cq, g_q) @ w_q_up).reshape(B, S, H, MLA_NOPE + MLA_ROPE)
    q_nope, q_rope = jnp.split(q, [MLA_NOPE], axis=-1)
    kv = (rmsnorm_2(ckv, g_kv) @ w_kv_up).reshape(B, S, H, MLA_NOPE + MLA_VDIM)
    k_nope, v = jnp.split(kv, [MLA_NOPE], axis=-1)
    q_rope = apply_rope(q_rope, cos, sin)
    k_rope = apply_rope(k_rope[:, :, None, :], cos, sin)[:, :, 0, :]

    scale = (MLA_NOPE + MLA_ROPE) ** -0.5
    nb = S // Q_BLOCK
    qn = q_nope.reshape(B, nb, Q_BLOCK, H, MLA_NOPE).transpose(1, 0, 2, 3, 4)
    qr = q_rope.reshape(B, nb, Q_BLOCK, H, MLA_ROPE).transpose(1, 0, 2, 3, 4)
    kpos = jnp.arange(S)

    def block(args):
        qn_b, qr_b, idx = args
        s = (jnp.einsum('bqhd,bkhd->bhqk', qn_b, k_nope)
             + jnp.einsum('bqhd,bkd->bhqk', qr_b, k_rope)).astype(jnp.float32) * scale
        qpos = idx * Q_BLOCK + jnp.arange(Q_BLOCK)
        mask = kpos[None, :] <= qpos[:, None]
        p = jax.nn.softmax(jnp.where(mask, s, -jnp.inf), axis=-1)
        return jnp.einsum('bhqk,bkhd->bqhd', p.astype(v.dtype), v)

    o = lax.map(block, (qn, qr, jnp.arange(nb)))
    o = o.transpose(1, 0, 2, 3, 4).reshape(B, S, H * MLA_VDIM)
    return o @ w_out

def swiglu(h, w_in, w_out):
    gate, up = jnp.split(h @ w_in, 2, axis=-1)
    return (jax.nn.silu(gate) * up) @ w_out

def second_inputs(seed: int = 0) -> dict:
    key = jax.random.key(seed)
    ks = jax.random.split(key, 24)
    D = D_MODEL
    f32 = jnp.float32

    def w(k, shape, fan_in):
        return jax.random.normal(k, shape, f32) * (fan_in ** -0.5)

    def gain(k, shape):
        return 1.0 + 0.02 * jax.random.normal(k, shape, f32)

    x = jax.random.normal(ks[0], (BATCH, SEQ, D), f32)
    c = jax.random.normal(ks[1], (BATCH, D), f32)
    offsets = jax.random.randint(ks[2], (BATCH, 1), 0, 4096, dtype=jnp.int32)
    positions = offsets + jnp.arange(SEQ, dtype=jnp.int32)[None, :]

    gla_in = 2 * GLA_HEADS * GLA_DK + 2 * GLA_HEADS * GLA_DV + GLA_GATE_RANK
    mla_in = MLA_Q_RANK + MLA_KV_RANK + MLA_ROPE
    return {
        "x": x,
        "c": c,
        "positions": positions,
        "ada_w": w(ks[3], (DEPTH_2, D, 6 * D), D),
        "ada_b": 0.02 * jax.random.normal(ks[4], (DEPTH_2, 6 * D), f32),
        "norm_mix": gain(ks[5], (DEPTH_2, D)),
        "norm_ffn": gain(ks[6], (DEPTH_2, D)),
        "gla_w_in": w(ks[7], (N_GLA, D, gla_in), D),
        "gla_w_gate": w(ks[8], (N_GLA, GLA_GATE_RANK, GLA_HEADS * GLA_DK), GLA_GATE_RANK),
        "gla_b_gate": 0.1 * jax.random.normal(ks[9], (N_GLA, GLA_HEADS * GLA_DK), f32),
        "gla_g_out": gain(ks[10], (N_GLA, GLA_DV)),
        "gla_w_out": w(ks[11], (N_GLA, GLA_HEADS * GLA_DV, D), GLA_HEADS * GLA_DV),
        "mla_w_in": w(ks[12], (N_MLA, D, mla_in), D),
        "mla_g_q": gain(ks[13], (N_MLA, MLA_Q_RANK)),
        "mla_w_q_up": w(ks[14], (N_MLA, MLA_Q_RANK, MLA_HEADS * (MLA_NOPE + MLA_ROPE)), MLA_Q_RANK),
        "mla_g_kv": gain(ks[15], (N_MLA, MLA_KV_RANK)),
        "mla_w_kv_up": w(ks[16], (N_MLA, MLA_KV_RANK, MLA_HEADS * (MLA_NOPE + MLA_VDIM)), MLA_KV_RANK),
        "mla_w_out": w(ks[17], (N_MLA, MLA_HEADS * MLA_VDIM, D), MLA_HEADS * MLA_VDIM),
        "ffn_w_in": w(ks[18], (DEPTH_2, D, 2 * D_FF), D),
        "ffn_w_out": w(ks[19], (DEPTH_2, D_FF, D), D_FF),
        "final_norm": gain(ks[20], (D,)),
    }

def second_block(x, c, positions, ada_w, ada_b, norm_mix, norm_ffn,
              gla_w_in, gla_w_gate, gla_b_gate, gla_g_out, gla_w_out,
              mla_w_in, mla_g_q, mla_w_q_up, mla_g_kv, mla_w_kv_up, mla_w_out,
              ffn_w_in, ffn_w_out, final_norm):
    inv_freq = ROPE_THETA ** (-jnp.arange(0, MLA_ROPE, 2, dtype=jnp.float32) / MLA_ROPE)
    ang = positions.astype(jnp.float32)[..., None] * inv_freq
    cos = jnp.cos(ang)[:, :, None, :]
    sin = jnp.sin(ang)[:, :, None, :]
    c_act = jax.nn.silu(c)

    for i in range(DEPTH_2):
        mod = c_act @ ada_w[i] + ada_b[i]
        sh1, sc1, g1, sh2, sc2, g2 = jnp.split(mod, 6, axis=-1)
        h = modulate(x, norm_mix[i], sh1, sc1)
        j = i // N_MIXERS
        if i % N_MIXERS == 0:
            y = gla_mixer(h, gla_w_in[j], gla_w_gate[j], gla_b_gate[j], gla_g_out[j], gla_w_out[j])
        else:
            y = mla_mixer(h, cos, sin, mla_w_in[j], mla_g_q[j], mla_w_q_up[j],
                          mla_g_kv[j], mla_w_kv_up[j], mla_w_out[j])
        x = x + g1[:, None, :] * y
        h = modulate(x, norm_ffn[i], sh2, sc2)
        x = x + g2[:, None, :] * swiglu(h, ffn_w_in[i], ffn_w_out[i])

    return rmsnorm_2(x, final_norm)


def setup_inputs(seed=0):
    out = dict(first_inputs(seed))
    for name, value in second_inputs(seed + 1).items():
        if name != "x":
            out[name + "_2"] = value
    return out


def reference(
    x, p, g_mix, w_in, conv_a_w, conv_a_b, ln_a_g, ln_a_b, conv_b_w, ln_c_g, ln_c_b, w_s, b_s,
    w_out, g_ffn, w_q, sub_keys, expert_u, expert_v, g_ple, w_pe, w_pg, g_final, c_2,
    positions_2, ada_w_2, ada_b_2, norm_mix_2, norm_ffn_2, gla_w_in_2, gla_w_gate_2,
    gla_b_gate_2, gla_g_out_2, gla_w_out_2, mla_w_in_2, mla_g_q_2, mla_w_q_up_2, mla_g_kv_2,
    mla_w_kv_up_2, mla_w_out_2, ffn_w_in_2, ffn_w_out_2, final_norm_2,
):
    x = first_block(
        x, p, g_mix, w_in, conv_a_w, conv_a_b, ln_a_g, ln_a_b, conv_b_w, ln_c_g, ln_c_b, w_s,
        b_s, w_out, g_ffn, w_q, sub_keys, expert_u, expert_v, g_ple, w_pe, w_pg, g_final,
    )
    return second_block(
        x, c_2, positions_2, ada_w_2, ada_b_2, norm_mix_2, norm_ffn_2, gla_w_in_2, gla_w_gate_2,
        gla_b_gate_2, gla_g_out_2, gla_w_out_2, mla_w_in_2, mla_g_q_2, mla_w_q_up_2, mla_g_kv_2,
        mla_w_kv_up_2, mla_w_out_2, ffn_w_in_2, ffn_w_out_2, final_norm_2,
    )


_drawn_inputs = setup_inputs


def setup_inputs(seed=0):
    import zlib

    import numpy as np

    out = dict(_drawn_inputs(seed))
    spreads = {}
    factors = {'conv_a_b': 2.802,
     'ln_a_b': 6.004,
     'ln_c_g': 4.249,
     'ln_c_b': 8.0,
     'g_ffn': 4.868,
     'g_ple': 5.77,
     'norm_mix_2': 2.954,
     'norm_ffn_2': 3.144,
     'gla_g_out_2': 5.14,
     'mla_g_q_2': 8.0,
     'mla_g_kv_2': 8.0,
     'final_norm_2': 2.829}
    for name, (base, spread) in spreads.items():
        noise = np.random.default_rng([zlib.crc32(name.encode()), seed]).standard_normal(out[name].shape)
        drawn = base * np.exp(spread * noise) if base else spread * noise
        out[name] = __import__('jax').numpy.asarray(drawn.astype(out[name].dtype))
    for name, factor in factors.items():
        out[name] = (out[name] * factor).astype(out[name].dtype)
    return out
```

```python
from contextlib import ExitStack, contextmanager

import concourse.bass as bass
import numpy as np
from concourse import mybir

ALU = mybir.AluOpType
ACT = mybir.ActivationFunctionType
F32 = mybir.dt.float32
U32 = mybir.dt.uint32
I32 = mybir.dt.int32
AX = mybir.AxisListType
P = 128
EPS = 1e-6

T = 512
D = 1024
DC = D // P
TT = T // P
MIX_A, MIX_B, MIX_C = 384, 256, 384
TAPS_A, TAPS_B = 31, 3
HEADS, KEYS, TOPK = 8, 128, 16
UNITS = TT * HEADS
AHEAD = 2
RING = 16
GLA_H, GLA_DK, GLA_DV, GLA_SUB = 4, 128, 256, 16
GLA_G = GLA_H * TT
MLA_H, NOPE, ROPE, VDIM = 8, 128, 64, 128
D_FF = 2816
FC = D_FF // P
FH = FC // 2
UNIT = 256
SLOT = FH * UNIT
MASKED = -1e30
ROUND = 1.5 * 2.0 ** 23
PI2_A, PI2_B, PI2_C = 6.28125, 0.0019350051879882812, 3.0199159819567e-07
PI_IN = 3.1415925


class Count:

    def __init__(self, sem, start=0):
        self.sem, self.at, self.dyn = sem, start, None

    def value(self, back=0):
        n = self.at - back
        return n if self.dyn is None else self.dyn + n

    def add(self, n=1):
        self.at += n


@contextmanager
def loop(eng, trips, counts):
    starts = [c.at for c, _ in counts]
    outer = [c.dyn for c, _ in counts]
    with eng.Fori(0, trips) as i:
        for c, per in counts:
            c.dyn = i * per if c.dyn is None else c.dyn + i * per
        yield i
        for (c, per), s in zip(counts, starts):
            assert c.at - s == per, (c.sem, c.at - s, per)
    for (c, per), s, o in zip(counts, starts, outer):
        c.at, c.dyn = s + per * trips, o


SEMS = ("x_in params_in ws_in bs_in keys_in ptok_in wgate_in pos_in wglr_in xtok_t hT_in params_t params_c "
        "chunk_done act_evac dve_evac consts sq_ready ms_ready var_ready std_ready norm_ready norm_full "
        "v_ch v_shift pool_step vector_step a_ch pl_ch gl_src gl_mean gl_cen gl_var gl_veps gl_std gl_norm mix_scaled mix_ready ws_t ws_ready vt_t vt_ready "
        "sg_done h_ready ntok_t ntok_ready keys_t keysT_ready sc_done sc_ready hs_ready hs_read cand_max gexp "
        "gates_ready idx_ready idx_copied consumed x_ready u_read dots_ready gelu_ready coef_ready acc_ready "
        "acc_t acc_added ada_done mod_ready cT_ready pT_t pT_ready sig_ready pe_used "
        "glr_ready glog_in glog_a glog_v glog_l scan_ready dq_ready dq_exp q_sub dk_ready dk_exp k_sub amat_done amat_read "
        "a_ready ew_ready ew_exp ew_done kw_ready kw_t kw_tok s_upd s_new o_done o_evac osq_done "
        "rope_src rot_done rope_read rope_ready angle_ready trig_ready cnorm_ready att_s att_m att_p att_n att_t att_pt att_o "
        "att_oe fin_t fin_ready out_done ada_in glr_in gla_r shift_ready hid_ready").split()


def build(nc, A, out):
    with ExitStack() as ctx:
        S = {n: ctx.enter_context(nc.semaphore(n)) for n in SEMS}
        w_landed = [ctx.enter_context(nc.semaphore(f"w_landed{i}")) for i in range(2)]
        row_landed = [ctx.enter_context(nc.semaphore(f"row_landed{i}")) for i in range(RING)]

        def sb(name, *shape, dt=F32):
            return ctx.enter_context(nc.sbuf_tensor(name, [P, *shape], dt))

        hT = sb("hT", DC, T)
        nT = sb("nT", DC, T)
        work = sb("work", DC, T)
        wring = sb("wring", 2, SLOT)
        row = sb("row", 3, T)
        var, std, rstd = row[:, 0, :], row[:, 1, :], row[:, 2, :]
        ident = sb("ident", P)
        ones = sb("ones", P)
        bdiag = sb("bdiag", P)
        rotm = sb("rotm", P)
        par_rows = sb("par_rows", 3, P)
        par = sb("par", 3, P)
        mod = sb("mod", 96)
        gmod = sb("gmod", 4, DC)
        cT = sb("cT", DC)
        arena = sb("arena", 31232)

        class Region:
            def __init__(self, start=0):
                self.at = start

            def take(self, *shape, dt=None):
                n = int(np.prod(shape))
                ap = arena[:, self.at:self.at + n]
                self.at += n
                assert self.at <= 31232, self.at
                if dt is not None:
                    ap = ap.bitcast(dt)
                if len(shape) == 2:
                    ap = ap.rearrange("p (a b) -> p a b", a=shape[0])
                if len(shape) == 3:
                    ap = ap.rearrange("p (a b c) -> p a b c", a=shape[0], b=shape[1])
                return ap

        ps = ctx.enter_context(nc.psum_tensor("ps", [P, 8, 512], F32))

        vectors, at = {}, [0, 0, 0]

        def vec(name, ap, tile):
            n = ap.shape[0]
            vectors[name] = (ap, tile, at[tile], n)
            at[tile] += n

        def rows(ap):
            return ap.rearrange("(c p) -> c p", p=P)

        for name in ("g_mix", "conv_a_b", "ln_a_g", "ln_a_b", "ln_c_g", "ln_c_b", "g_ffn", "g_ple", "gla_b_gate_2",
                     "gla_g_out_2", "mla_g_q_2", "mla_g_kv_2", "c_2"):
            vec(name, rows(A[name][0, :]), 0)
        vec("g_final", rows(A["g_final"]), 0)
        vec("final_norm_2", rows(A["final_norm_2"]), 0)
        vec("norm_mix_2", A["norm_mix_2"].rearrange("l (c p) -> (l c) p", p=P), 0)
        vec("norm_ffn_2", A["norm_ffn_2"].rearrange("l (c p) -> (l c) p", p=P), 0)
        vec("ada_b_2", A["ada_b_2"].rearrange("l (c p) -> (l c) p", p=P), 1)
        vec("inv_freq", A["inv_freq"], 1)
        vec("conv_b_w", A["conv_b_w"][0].rearrange("k (c p) -> (k c) p", p=P), 1)
        vec("conv_a_w", A["conv_a_w"][0].rearrange("k (c p) -> (k c) p", p=P), 2)

        def col(name, k=0, n=1):
            _, tile, r0, _ = vectors[name]
            return par[:, tile, r0 + k:r0 + k + n]

        R = Region()
        z = R.take(18, T)
        padA = R.take(3, TAPS_A - 1 + T)
        padB = R.take(2, TAPS_B - 1 + T)
        cvA = R.take(3, T)
        gvar = R.take(3, T)
        ws_in = R.take(6, P)
        wsT = R.take(6, P)
        bsb = R.take(3, P)
        vtok = R.take(TT, MIX_C)
        mixT = R.take(DC, T)
        x_tok = nT[:, :, :].rearrange("p (t c) k -> p t (c k)", t=TT)

        R = Region()
        score = R.take(UNITS + AHEAD, 2 * KEYS)
        ring = R.take(RING, D)
        R2 = Region((UNITS + AHEAD) * 2 * KEYS)
        qT = R2.take(2 * HEADS, T)
        keys_in = R2.take(2 * HEADS, P)
        keysT = R2.take(2 * HEADS, P)
        junk = R.take(D)
        acc_sb = R.take(D)
        hs = R.take(2, KEYS)
        cand = R.take(TOPK, TOPK)
        onehot = R.take(TOPK, TOPK)
        iota16 = R.take(TOPK)
        top_v = R.take(3, TOPK)
        top_i = R.take(3, TOPK, dt=U32)
        pick_i = R.take(2, TOPK, dt=U32)
        pick_f = R.take(2, TOPK)
        top_f = R.take(2, TOPK)
        ek = R.take(3, TOPK)
        gcur = R.take(TOPK)
        small = R.take(8)
        idx = R.take(UNITS + AHEAD, TOPK, dt=U32)
        idx_flat = idx.rearrange("p n k -> p (n k)")
        gates = R.take(UNITS + AHEAD, TOPK)
        cur = R.take(RING, dt=U32)
        dots = R.take(TOPK)
        gdots = R.take(TOPK)
        coef = R.take(TOPK)
        ntok = work[:, :, :].rearrange("p (t c) k -> p t (c k)", t=TT)

        R = Region()
        p_tok = R.take(TT, UNIT)
        pT = R.take(2, T)
        peT = R.take(DC, T)
        sgT = R.take(DC, T)

        R = Region()
        gq = R.take(GLA_H, T)
        gk = R.take(GLA_H, T)
        gvt = R.take(TT, D)
        gr = R.take(DC, T)
        wglr = R.take(DC, 16)
        glrT = R.take(T)
        wgate = R.take(T)
        gb = R.take(GLA_H, T)
        gtmp = R.take(GLA_H, T)
        gtmp2 = R.take(GLA_H, T)
        qsub = R.take(GLA_H, T)
        reset = R.take(T)
        amat = R.take(GLA_G, P)
        kwt = R.take(GLA_G, P)
        state = R.take(GLA_H, GLA_DV)
        elast = R.take(GLA_G)
        keep = R.take(P)
        kd = work[:, :, :].rearrange("p (a c) k -> p a (c k)", a=2)
        goT = nT

        R = Region()
        cT6 = R.take(6, T)
        qn = R.take(MLA_H, T)
        qr = R.take(MLA_H // 2, T)
        kn = R.take(MLA_H, T)
        vt = R.take(TT, D)
        ang = R.take(T)
        tri = R.take(2, T)
        rtmp = R.take(2, T)
        pos_i = R.take(T, dt=I32)
        pp = R.take(2, T)
        pTt = R.take(TT, T)
        cmask = R.take(P)
        attsm = R.take(2, 4)
        oT = nT

        R = Region()
        hid = R.take(FC, T)
        gsil = R.take(2, T)

        R = Region()
        o_tok = R.take(TT, D)

        def gsubs(x):
            return x.rearrange("p h (t k) -> p (h t) k", k=P)

        def kd_g(a):
            return kd[:, a, :].rearrange("p (g k) -> p g k", g=GLA_G)

        IN = {n: A[n] for n in A}
        w_in, w_out, w_q = IN["w_in"][0], IN["w_out"][0], IN["w_q"][0]
        gla_in = IN["gla_w_in_2"][0]
        mla_in = IN["mla_w_in_2"][0]

        block = ctx.enter_context(nc.Block())

        @block.sync
        def _(e):
            c = {n: Count(s) for n, s in S.items()}
            landed = [Count(s) for s in w_landed]
            done = c["chunk_done"]
            state_ = {"u": 0, "ends": []}

            def unit(W, col0, kc, k0=0, width=UNIT, chunks=2, back=None, extra=None):
                u = state_["u"]
                v = done.value(back) if back is not None else (
                    state_["ends"][-2] if len(state_["ends"]) >= 2 else None)
                if v is not None:
                    e.wait_ge(done.sem, v)
                dst = wring[:, u % 2, 0:kc * width].rearrange("p (k n) -> p k n", n=width)
                wide = width - (extra or 0)
                src = W[k0 * P:(k0 + kc) * P, bass.ds(col0, wide)].rearrange("(k p) n -> p k n", p=P)
                n = 16
                e.dma_start(dst[:, :, 0:wide], src).then_inc(landed[u % 2].sem, 16)
                if extra:
                    e.dma_start(dst[:, :, wide:width],
                                W[k0 * P:(k0 + kc) * P, bass.ds(col0 + wide - extra, extra)]
                                .rearrange("(k p) n -> p k n", p=P)).then_inc(landed[u % 2].sem, 16)
                done.add(chunks)
                state_["u"] += 1
                if back is None:
                    state_["ends"].append(done.at)

            def units(W, col0, n, kc):
                pairs = n // 2
                if pairs > 1:
                    with loop(e, pairs, [(done, 4)]) as i:
                        for j in range(2):
                            unit(W, i * (2 * UNIT) + (col0 + j * UNIT), kc, back=2)
                    state_["ends"] += [done.at - 2, done.at]
                else:
                    for j in range(2 * pairs):
                        unit(W, col0 + j * UNIT, kc)
                if n % 2:
                    unit(W, col0 + 2 * pairs * UNIT, kc)

            e.dma_start(x_tok, IN["x"][0].rearrange("(t p) d -> p t d", p=P)).then_inc(S["x_in"], 16)
            e.wait_ge(S["consts"], 1)
            for name, (ap, tile, r0, n) in vectors.items():
                e.dma_start(par_rows[r0:r0 + n, tile, :], ap).then_inc(S["params_in"], 16)
            e.dma_start(ws_in, IN["w_s"][0].rearrange("h i j -> i h j")).then_inc(S["ws_in"], 16)
            for h in range(6):
                e.dma_start(bsb[64 * (h % 2):64 * (h % 2) + 64, h // 2, :],
                            IN["b_s"][0, h:h + 1, :].to_broadcast([64, P])).then_inc(S["bs_in"], 16)
            units(w_in, 0, 3, DC)
            units(w_in, 2 * MIX_A, 6, DC)
            units(w_out, 0, 4, DC)
            units(w_q, 0, 8, DC)
            e.wait_ge(S["norm_full"], 2)
            e.dma_start(keys_in, IN["sub_keys"][0].rearrange("h s k d -> k (h s) d")).then_inc(S["keys_in"], 16)
            for b in range(TT):
                layer, half = divmod(b, 2)
                units(IN["ada_w_2"][layer], half * 3 * D, 12, DC)
            e.wait_ge(S["h_ready"], 2)
            e.dma_start(p_tok, IN["p"][0, 0].rearrange("(t p) d -> p t d", p=P)).then_inc(S["ptok_in"], 16)
            units(IN["w_pe"][0], 0, 4, 2)
            units(IN["w_pg"][0], 0, 4, DC)
            e.wait_ge(S["h_ready"], 4)
            e.dma_start(wglr, gla_in[:, 3072:3088].rearrange("(k p) n -> p k n", p=P)).then_inc(S["glr_in"], 16)
            e.dma_start(wgate[0:16, :], IN["gla_w_gate_2"][0]).then_inc(S["glr_in"], 16)
            units(gla_in, 0, 4, DC)
            units(gla_in, 1024, 4, DC)
            units(gla_in, 2048, 4, DC)
            units(IN["gla_w_out_2"][0], 0, 4, DC)

            def ffn(layer):
                W = IN["ffn_w_in_2"][layer]
                with loop(e, FH, [(done, 4)]) as i:
                    unit(W, i * UNIT, DC, back=2)
                    unit(W, i * UNIT + D_FF, DC, back=2)
                state_["ends"] += [done.at - 2, done.at]
                W = IN["ffn_w_out_2"][layer]
                with loop(e, 2, [(done, 8)]) as i:
                    for half in range(2):
                        for k in range(2):
                            unit(W, i * (2 * UNIT) + half * UNIT, FH, k0=k * FH, back=2)
                state_["ends"] += [done.at - 2, done.at]

            ffn(0)
            e.wait_ge(S["h_ready"], 6)
            e.dma_start(pos_i, IN["positions_2"][0:1, :].to_broadcast([P, T])).then_inc(S["pos_in"], 16)
            unit(mla_in, 0, DC)
            unit(mla_in, 256, DC)
            unit(mla_in, 512, DC, extra=ROPE)
            for m in range(4):
                u = state_["u"]
                e.wait_ge(done.sem, state_["ends"][-2])
                dst = wring[:, u % 2, 0:3 * 384].rearrange("p (k n) -> p k n", n=384)
                W = IN["mla_w_q_up_2"][0].rearrange("(k p) n -> p k n", p=P)
                for to, frm, n in ((0, 0, NOPE), (NOPE, 192, NOPE), (256, NOPE, ROPE), (320, 320, ROPE)):
                    e.dma_start(dst[:, :, to:to + n], W[:, :, 384 * m + frm:384 * m + frm + n]
                                ).then_inc(landed[u % 2].sem, 16)
                done.add(3)
                state_["u"] += 1
                state_["ends"].append(done.at)
            units(IN["mla_w_kv_up_2"][0], 0, 8, 2)
            units(IN["mla_w_out_2"][0], 0, 4, DC)
            ffn(1)
            e.wait_ge(S["fin_ready"], 2 * TT)
            e.dma_start(out[0].rearrange("(t p) d -> p t d", p=P), o_tok).then_inc(S["out_done"], 16)
            e.wait_ge(S["out_done"], 16)

        @block.gpsimd
        def _(e):
            k = Count(S["pl_ch"])

            def chain(ins):
                ins.then_inc(k.sem, 1)
                k.add()
                e.wait_ge(k.sem, k.value())

            chain(e.memset(ident[:], 0.0))
            chain(e.affine_select(out=ident[:], in_=ident[:], compare_op=ALU.not_equal, fill=1.0, base=0,
                                  pattern=[[-1, P]], channel_multiplier=1))
            chain(e.memset(ones[:], 1.0))
            chain(e.memset(bdiag[:], 0.0))
            for q in range(2):
                chain(e.memset(bdiag[64 * q:64 * q + 64, 64 * q:64 * q + 64], 1.0 / 64))
            chain(e.memset(rotm[:], 0.0))
            pairs = rotm[:].rearrange("p (i two) -> p i two", two=2)
            chain(e.affine_select(out=pairs[:, :, 0], in_=pairs[:, :, 0], compare_op=ALU.not_equal, fill=-1.0,
                                  base=-1, pattern=[[-2, 64]], channel_multiplier=1))
            chain(e.affine_select(out=pairs[:, :, 1], in_=pairs[:, :, 1], compare_op=ALU.not_equal, fill=1.0,
                                  base=0, pattern=[[-2, 64]], channel_multiplier=1))
            chain(e.memset(padA[:, :, 0:TAPS_A - 1], 0.0))
            chain(e.memset(padB[:, :, 0:TAPS_B - 1], 0.0))
            e.memset(par_rows[:], 0.0).then_inc(S["consts"], 1)

            e.wait_ge(S["sc_done"], 4 * TT)
            chain(e.iota(iota16, [[1, TOPK]], base=0, channel_multiplier=0, allow_small_or_imprecise_dtypes=True))
            e.memset(small[:, 0:1], 0.0).then_inc(S["consts"], 1)
            copied = Count(S["idx_copied"])
            slots = Count(S["consumed"])
            landed = [Count(s) for s in row_landed]
            ready = Count(S["idx_ready"])
            expert_u, expert_v = IN["expert_u"][0], IN["expert_v"][0]

            def gather(g, tables, parts):
                slots.add(4)
                e.wait_ge(slots.sem, slots.value())
                for dst, src in parts:
                    e.tensor_copy(dst, src).then_inc(copied.sem, 1)
                    copied.add()
                e.wait_ge(copied.sem, copied.value())
                e.sem_inc(S["pool_step"], 1)
                for s, table in zip(range(g, g + 4), tables):
                    e.indirect_dma_start(ring[:, s, :], None, table,
                                         bass.IndirectOffsetOnAxis(ap=cur[:, s:s + 1], axis=0)
                                         ).then_inc(landed[s].sem, 16)

            def gather_one(table, base):
                for g in range(0, RING, 4):
                    gather(g, [table] * 4, [(cur[:, g:g + 4], idx_flat[:, bass.ds(base + g, 4)])])

            PER_BLOCK = HEADS * TOPK
            with loop(e, TT, [(copied, 4 + 7 * 16 + 4), (slots, 16 * RING), (ready, HEADS)]) as b:
                ready.add()
                e.wait_ge(ready.sem, ready.value())
                gather_one(expert_u, b * PER_BLOCK)
                with loop(e, HEADS - 1, [(copied, 16), (slots, 2 * RING), (ready, 1)]) as h:
                    ready.add()
                    e.wait_ge(ready.sem, ready.value())
                    for half in range(2):
                        for g in range(0, RING, 4):
                            v0 = b * PER_BLOCK + h * TOPK + (half * 8 + g // 2)
                            gather(g, [expert_u, expert_v] * 2,
                                   [(cur[:, g:g + 4:2], idx_flat[:, bass.ds(v0 + TOPK, 2)]),
                                    (cur[:, g + 1:g + 4:2], idx_flat[:, bass.ds(v0, 2)])])
                gather_one(expert_v, b * PER_BLOCK + (HEADS - 1) * TOPK)
            e.wait_ge(S["norm_full"], 5)
            chain(e.memset(keep, 1.0))
            chain(e.affine_select(out=keep, in_=keep, compare_op=ALU.is_ge, fill=0.0, base=0,
                                  pattern=[[1, P]], channel_multiplier=-1))
            chain(e.memset(reset, 1.0))
            for t in range(TT):
                chain(e.memset(reset[:, t * P:t * P + 1], 0.0))
            e.memset(kd, 0.0).then_inc(S["consts"], 1)
            e.wait_ge(S["h_ready"], 6)
            chain(e.memset(cmask, 0.0))
            e.affine_select(out=cmask, in_=cmask, compare_op=ALU.is_ge, fill=MASKED, base=0,
                            pattern=[[-1, P]], channel_multiplier=1).then_inc(S["consts"], 1)

        @block.tensor
        def _(e):
            c = {n: Count(s) for n, s in S.items()}
            landed = [Count(s) for s in w_landed]
            done, act, dve = c["chunk_done"], Count(S["act_evac"], 4), Count(S["dve_evac"], 4)
            st = {"u": 0}

            def need(name, n):
                c[name].at = max(c[name].at, n)
                e.wait_ge(S[name], n)

            def inc(ins, name, n=1):
                ins.then_inc(S[name], n)
                c[name].add(n)

            def settle():
                e.wait_ge(act.sem, act.value())
                e.wait_ge(dve.sem, dve.value())

            def slot(kc, width=UNIT, n=16):
                u = st["u"]
                st["u"] += 1
                landed[u % 2].add(n)
                e.wait_ge(landed[u % 2].sem, landed[u % 2].value())
                return wring[:, u % 2, 0:kc * width].rearrange("p (k n) -> p k n", n=width)

            def unit(kc, rhs, evac, n=16):
                w = slot(kc, n=n)
                for j in range(2):
                    b = 2 * ((st["u"] - 1) % 2) + j
                    e.wait_ge(evac.sem, evac.value(3))
                    for k in range(kc):
                        mm = e.matmul(ps[:, b, :], w[:, k, j * P:(j + 1) * P], rhs(k), start=(k == 0),
                                      stop=(k == kc - 1))
                    inc(mm, "chunk_done")
                    evac.add()

            def unit_tok(w, src, evac, st_bank):
                for j in range(2):
                    e.wait_ge(evac.sem, evac.value(3))
                    for q in range(2):
                        for k in range(DC):
                            mm = e.matmul(ps[:, st_bank + j, q * UNIT:(q + 1) * UNIT],
                                          src[:, k, (2 * j + q) * P:(2 * j + q + 1) * P], w[:, k, :],
                                          start=(k == 0), stop=(k == DC - 1))
                    inc(mm, "chunk_done")
                    evac.add()

            def pairs_of(n, body, evac, nland=16):
                if n // 2 > 1:
                    u0 = st["u"]
                    with loop(e, n // 2, [(done, 4), (evac, 4), (landed[0], nland), (landed[1], nland)]):
                        body()
                        body()
                    st["u"] = u0 + 2 * (n // 2)
                else:
                    for _ in range(2 * (n // 2)):
                        body()
                if n % 2:
                    body()

            def linear(n, kc, rhs, evac):
                settle()
                pairs_of(n, lambda: unit(kc, rhs, evac), evac)

            def squares(n, bank, groups=1):
                if c["var_ready"].at:
                    need("var_ready", c["var_ready"].at)
                per = n // groups
                for g in range(groups):
                    for k in range(per):
                        need("sq_ready", c["sq_ready"].at + 1)
                        mm = e.matmul(ps[:, bank + g, :], ones[:], work[:, g * per + k, :], start=(k == 0),
                                      stop=(k == per - 1))
                inc(mm, "ms_ready")
                c["var_ready"].at += 1

            def nrhs(k):
                return nT[:, k, :]

            need("consts", 1)
            need("x_in", 16)
            for k in range(DC):
                if k >= 4:
                    need("hT_in", k - 3)
                for t in range(TT):
                    mm = e.transpose(ps[:, 4 + k % 4, t * P:(t + 1) * P], x_tok[:, t, k * P:(k + 1) * P], ident[:])
                inc(mm, "xtok_t")
            need("hT_in", 5)
            need("params_in", 16 * len(vectors))
            for k in range(3):
                mm = e.transpose(ps[:, 4, k * P:(k + 1) * P], par_rows[:, k, :], ident[:])
            inc(mm, "params_t")
            need("hT_in", 7)
            need("ws_in", 16)
            for h in range(6):
                mm = e.transpose(ps[:, 5 + h // 4, (h % 4) * P:(h % 4 + 1) * P], ws_in[:, h, :], ident[:])
            inc(mm, "ws_t")
            need("params_c", 1)
            need("ws_ready", 1)
            squares(DC, 4)
            need("norm_full", 1)
            linear(3, DC, nrhs, act)
            linear(6, DC, nrhs, act)

            def head_stats(src):
                if c["gl_veps"].at:
                    need("gl_veps", c["gl_veps"].at)
                need("gl_src", c["gl_src"].at + 1)
                for k in range(3):
                    mm = e.matmul(ps[:, 5 + k, :], bdiag[:], src[:, k, :], start=True, stop=True)
                inc(mm, "gl_mean")
                for k in range(3):
                    need("sq_ready", c["sq_ready"].at + 1)
                    mm = e.matmul(ps[:, 5 + k, :], bdiag[:], work[:, k, :], start=True, stop=True)
                inc(mm, "gl_var")
                c["gl_veps"].at += 1

            head_stats(cvA)
            head_stats(z[:, 15:18, :])
            need("gl_norm", 2)
            for t in range(TT):
                b = 5 + t % 3
                if t >= 3:
                    need("vt_ready", t - 2)
                for k in range(3):
                    mm = e.transpose(ps[:, b, k * P:(k + 1) * P], z[:, 15 + k, t * P:(t + 1) * P], ident[:])
                inc(mm, "vt_t")
            need("vt_ready", TT)
            for k in range(3):
                if k:
                    need("sg_done", k)
                for par_ in range(2):
                    for b in range(TT):
                        mm = e.matmul(ps[:, 5 + par_, b * P:(b + 1) * P], vtok[:, b, k * P:(k + 1) * P],
                                      wsT[:, 2 * k + par_, :], start=True, stop=True)
                inc(mm, "mix_ready")
            need("sg_done", 3)
            linear(4, DC, lambda k: mixT[:, k, :], dve)

            squares(DC, 4)
            need("norm_full", 2)
            for t in range(TT):
                for half in range(2):
                    if t or half:
                        need("ntok_ready", 2 * t + half)
                    for k in range(4):
                        kk = half * 4 + k
                        mm = e.transpose(ps[:, 5 + (2 * t + half) % 2, k * P:(k + 1) * P],
                                         nT[:, kk, t * P:(t + 1) * P], ident[:])
                    inc(mm, "ntok_t")
            linear(8, DC, nrhs, act)
            need("keys_in", 16)
            need("ntok_ready", 2 * TT)
            for q in range(4):
                for k in range(4):
                    mm = e.transpose(ps[:, 4 + q, k * P:(k + 1) * P], keys_in[:, 4 * q + k, :], ident[:])
                inc(mm, "keys_t")
            settle()
            need("keysT_ready", 4)
            for t in range(TT):
                for q in range(4):
                    b = 4 * (t % 2) + q
                    if t >= 2:
                        need("sc_ready", 4 * (t - 2) + q + 1)
                    for k in range(4):
                        mm = e.matmul(ps[:, b, k * P:(k + 1) * P], qT[:, 4 * q + k, t * P:(t + 1) * P],
                                      keysT[:, 4 * q + k, :], start=True, stop=True)
                    inc(mm, "sc_done")
            need("sc_ready", 4 * TT)
            need("cT_ready", 1)
            for b in range(TT):
                u0 = st["u"]
                with loop(e, 6, [(done, 4), (landed[0], 16), (landed[1], 16)]) as i:
                    for p in range(2):
                        w = slot(DC)
                        for j in range(2):
                            m = i * 4 + (24 * b + 2 * p + j)
                            for k in range(DC):
                                mm = e.matmul(ps[:, 0, bass.ds(m, 1)], w[:, k, j * P:(j + 1) * P], cT[:, k:k + 1],
                                              start=(k == 0), stop=(k == DC - 1))
                            inc(mm, "chunk_done")
                st["u"] = u0 + 12
                need("acc_ready", b + 1)
                if b:
                    need("acc_added", b)
                for k in range(DC):
                    mm = e.transpose(ps[:, 2 + k // 4, (k % 4) * P:(k % 4 + 1) * P], acc_sb[:, k * P:(k + 1) * P],
                                     ident[:])
                inc(mm, "acc_t")

            need("ptok_in", 16)
            need("mod_ready", 1)
            need("acc_added", TT)
            for k in range(2):
                for t in range(TT):
                    mm = e.transpose(ps[:, 6 + k, t * P:(t + 1) * P], p_tok[:, t, k * P:(k + 1) * P], ident[:])
            inc(mm, "pT_t")
            need("pT_ready", 1)
            linear(4, 2, lambda k: pT[:, k, :], act)
            squares(DC, 4)
            need("norm_full", 3)
            linear(4, DC, nrhs, act)
            squares(DC, 4)
            squares(DC, 4)

            need("norm_full", 5)
            need("glr_in", 32)
            for k in range(DC):
                mm = e.matmul(ps[0:16, 5, :], wglr[:, k, :], nT[:, k, :], start=(k == 0), stop=(k == DC - 1))
            inc(mm, "glr_ready")
            need("glog_in", 1)
            for h in range(GLA_H):
                mm = e.matmul(ps[:, 4 + h, :], wgate[0:16, h * P:(h + 1) * P], glrT[0:16, :], start=True, stop=True)
                inc(mm, "glog_a")
            linear(4, DC, nrhs, act)
            settle()
            u0 = st["u"]
            with loop(e, 2, [(done, 4), (act, 4), (landed[0], 16), (landed[1], 16)]):
                for p in range(2):
                    unit_tok(slot(DC), nT, act, 2 * p)
            st["u"] = u0 + 4
            linear(4, DC, nrhs, act)
            need("glog_v", GLA_H)
            need("q_sub", 1)
            for i in range(8):
                need("k_sub", i + 1)
                for g in range(GLA_G):
                    mm = e.matmul(ps[:, 4 + g // 4, (g % 4) * P + 16 * i:(g % 4) * P + 16 * i + 16],
                                  kd_g(i % 2)[:, g, :], gsubs(qsub)[:, g, 16 * i:16 * i + 16], start=True, stop=True)
                inc(mm, "amat_done")
            need("kw_ready", 1)
            for h in range(GLA_H):
                need("a_ready", h + 1)
                for t in range(TT):
                    mm = e.transpose(ps[:, 4 + h, t * P:(t + 1) * P], gtmp2[:, h, t * P:(t + 1) * P], ident[:])
                inc(mm, "kw_t")
            need("ew_done", 1)
            for t in range(TT):
                for h in range(GLA_H):
                    i = t * GLA_H + h
                    g = h * TT + t
                    b = 4 + i % 4
                    if i < 4:
                        need("kw_tok", h + 1)
                    else:
                        need("o_evac", i - 3)
                        need("s_new", i - 3)
                    for v in range(2):
                        mm = e.matmul(ps[:, b, v * P:(v + 1) * P],
                                      gvt[:, t, h * GLA_DV + v * P:h * GLA_DV + (v + 1) * P], amat[:, g, :],
                                      start=True, stop=(t == 0))
                        if t:
                            mm = e.matmul(ps[:, b, v * P:(v + 1) * P], state[:, h, v * P:(v + 1) * P],
                                          gq[:, h, t * P:(t + 1) * P], start=False, stop=True)
                    if t < TT - 1:
                        mm = e.matmul(ps[:, b, 2 * P:4 * P], kwt[:, g, :], gvt[:, t, h * GLA_DV:(h + 1) * GLA_DV],
                                      start=True, stop=True)
                    inc(mm, "o_done")
            need("o_evac", 16)
            squares(DC, 4, groups=4)
            need("gla_r", 1)
            linear(4, DC, nrhs, dve)

            def ffn():
                squares(DC, 4)
                need("norm_full", c["norm_full"].at + 1)
                settle()
                with loop(e, FH, [(done, 4), (act, 2), (dve, 2), (landed[0], 16), (landed[1], 16)]):
                    for p, evac in enumerate((act, dve)):
                        w = slot(DC)
                        for j in range(2):
                            e.wait_ge(evac.sem, evac.value(1))
                            for k in range(DC):
                                mm = e.matmul(ps[:, 2 * p + j, :], w[:, k, j * P:(j + 1) * P], nrhs(k),
                                              start=(k == 0), stop=(k == DC - 1))
                            inc(mm, "chunk_done")
                            evac.add()
                st["u"] += 2 * (FH - 1)
                settle()
                with loop(e, 2, [(done, 8), (dve, 4), (landed[0], 32), (landed[1], 32)]):
                    for half in range(2):
                        for kh in range(2):
                            w = slot(FH)
                            for j in range(2):
                                if kh == 0:
                                    e.wait_ge(dve.sem, dve.value(3 - j))
                                for k in range(FH):
                                    mm = e.matmul(ps[:, 2 * half + j, :], w[:, k, j * P:(j + 1) * P],
                                                  hid[:, kh * FH + k, :], start=(kh == 0 and k == 0),
                                                  stop=(kh == 1 and k == FH - 1))
                                inc(mm, "chunk_done")
                        dve.add(2)
                st["u"] += 4

            ffn()

            squares(DC, 4)
            need("norm_full", 7)
            settle()
            for n in range(3):
                unit(DC, nrhs, act, n=32 if n == 2 else 16)
            squares(3, 4)
            squares(2, 4)
            need("norm_full", 8)
            settle()
            for m in range(4):
                w = slot(3, width=384, n=64)
                for j in range(3):
                    e.wait_ge(act.sem, act.value(3))
                    for k in range(3):
                        mm = e.matmul(ps[:, (3 * m + j) % 4, :], w[:, k, j * P:(j + 1) * P], cT6[:, k, :], start=(k == 0), stop=(k == 2))
                    inc(mm, "chunk_done")
                    act.add()
            need("norm_full", 9)
            settle()

            def kv_unit():
                w = slot(2)
                b = 2 * ((st["u"] - 1) % 2)
                e.wait_ge(act.sem, act.value(3))
                for k in range(2):
                    mm = e.matmul(ps[:, b, :], w[:, k, 0:NOPE], cT6[:, 3 + k, :], start=(k == 0), stop=(k == 1))
                inc(mm, "chunk_done")
                act.add()
                e.wait_ge(act.sem, act.value(3))
                for t in range(TT):
                    for k in range(2):
                        mm = e.matmul(ps[:, b + 1, t * P:(t + 1) * P], cT6[:, 3 + k, t * P:(t + 1) * P],
                                      w[:, k, NOPE:NOPE + VDIM], start=(k == 0), stop=(k == 1))
                inc(mm, "chunk_done")
                act.add()

            pairs_of(MLA_H, kv_unit, act)
            settle()
            for r in range(5):
                if r >= 4:
                    need("rope_read", r - 3)
                mm = e.matmul(ps[:, 4 + r % 4, :], rotm[:], cT6[:, 5, :] if r == 4 else qr[:, r, :],
                              start=True, stop=True)
                inc(mm, "rot_done")
            need("rope_ready", 5)
            settle()
            ITEMS = MLA_H * TT

            def scores(i):
                h, t = divmod(i, TT)
                if i >= 2:
                    need("att_p", i - 1)
                n = (t + 1) * P
                r0 = 64 * (h % 2)
                e.matmul(ps[:, 4 + i % 2, 0:n], qn[:, h, t * P:(t + 1) * P], kn[:, h, 0:n], start=True, stop=False)
                mm = e.matmul(ps[:, 4 + i % 2, 0:n], qr[r0:r0 + 64, h // 2, t * P:(t + 1) * P],
                              cT6[r0:r0 + 64, 5, 0:n], start=False, stop=True)
                inc(mm, "att_s")

            def turn(i):
                h, t = divmod(i, TT)
                need("att_n", i + 1)
                if i >= 2:
                    need("att_pt", i - 1)
                for q in range(t + 1):
                    mm = e.transpose(ps[:, 2 + i % 2, q * P:(q + 1) * P], pp[:, i % 2, q * P:(q + 1) * P], ident[:])
                inc(mm, "att_t")

            scores(0)
            for i in range(ITEMS):
                if i + 1 < ITEMS:
                    scores(i + 1)
                turn(i)
                h, t = divmod(i, TT)
                if t == TT - 1:
                    need("att_pt", i + 1)
                    if h >= 2:
                        need("att_oe", h - 1)
                    for q in range(TT):
                        mm = e.matmul(ps[:, 6 + h % 2, q * P:T], vt[:, q, h * VDIM:(h + 1) * VDIM],
                                      pTt[:, q, q * P:T], start=(q == 0), stop=(q == TT - 1))
                    inc(mm, "att_o")
            need("att_oe", MLA_H)
            linear(4, DC, nrhs, dve)
            ffn()
            squares(DC, 4)
            need("norm_full", 11)
            for t in range(TT):
                for half in range(2):
                    i = 2 * t + half
                    if i >= 3:
                        need("fin_ready", i - 2)
                    for k in range(4):
                        mm = e.transpose(ps[:, 5 + i % 3, k * P:(k + 1) * P], nT[:, half * 4 + k, t * P:(t + 1) * P],
                                         ident[:])
                    inc(mm, "fin_t")

        @block.scalar
        def _(e):
            c = {n: Count(s) for n, s in S.items()}
            done, evacs = c["chunk_done"], Count(S["act_evac"], 4)
            st = {"u": 0}

            def need(name, n):
                c[name].at = max(c[name].at, n)
                e.wait_ge(S[name], n)

            def inc(ins, name):
                ins.then_inc(S[name], 1)
                c[name].add()

            def own(ins, name):
                inc(ins, name)
                e.wait_ge(S[name], c[name].value())

            def squares(aps):
                for k, ap in enumerate(aps):
                    inc(e.activation(work[:, k, :], ap, ACT.Square), "sq_ready")

            def root(dst, src):
                c["var_ready"].at += 1
                e.wait_ge(S["var_ready"], c["var_ready"].at)
                inc(e.activation(dst, src, ACT.Sqrt), "std_ready")

            def hchunks():
                return [hT[:, k, :] for k in range(DC)]

            def units(n, evac, first=0):
                def one(base):
                    b = 2 * (st["u"] % 2)
                    st["u"] += 1
                    for j in range(2):
                        done.add()
                        e.wait_ge(done.sem, done.value())
                        evac(ps[:, b + j, :], base + j).then_inc(evacs.sem, 1)
                        evacs.add()
                if n // 2 > 1:
                    u0 = st["u"]
                    with loop(e, n // 2, [(done, 4), (evacs, 4)]) as i:
                        one(i * 4 + first)
                        one(i * 4 + (first + 2))
                    st["u"] = u0 + 2 * (n // 2)
                else:
                    for q in range(2 * (n // 2)):
                        one(first + 2 * q)
                if n % 2:
                    one(first + 2 * (n - 1))

            def copy_to(dst, scale=1.0, func=ACT.Copy):
                def evac(src, m):
                    where = dst[:, m, :] if isinstance(m, int) else dst[:, bass.ds(m, 1), :].rearrange("p a k -> p (a k)")
                    return e.activation(where, src, func, scale=scale)
                return evac

            def skip(n):
                done.add(2 * n)
                st["u"] += n

            e.sem_inc(S["act_evac"], 4)
            for k in range(DC):
                need("xtok_t", k + 1)
                inc(e.activation(hT[:, k, :], ps[:, 4 + k % 4, :], ACT.Copy), "hT_in")
            need("hT_in", DC)
            squares(hchunks())
            root(std, var)
            need("params_c", 1)
            own(e.activation(cT[:], col("c_2", 0, DC), ACT.Silu), "cT_ready")
            copy = copy_to(z)
            gate = copy_to(z, func=ACT.Sigmoid)
            units(3, lambda src, m: (copy if m < 3 else gate)(src, m))
            units(6, copy_to(z), first=6)

            def head_norm(src, dst, g, b, func):
                for k in range(3):
                    need("gl_cen", c["gl_cen"].at + 1)
                    inc(e.activation(work[:, k, :], src[:, k, :], ACT.Square), "sq_ready")
                need("gl_veps", c["gl_veps"].at + 1)
                inc(e.activation(gvar, gvar, ACT.Sqrt), "gl_std")
                need("mix_scaled", c["mix_scaled"].at + 1)
                for k in range(3):
                    ins = e.activation(dst[:, k, :], src[:, k, :], func, scale=col(g, k), bias=col(b, k))
                inc(ins, "gl_norm")

            head_norm(cvA, mixT, "ln_a_g", "ln_a_b", ACT.Silu)
            head_norm(z[:, 15:18, :], z[:, 15:18, :], "ln_c_g", "ln_c_b", ACT.Identity)
            for t in range(TT):
                need("vt_t", t + 1)
                inc(e.activation(vtok[:, t, :], ps[:, 5 + t % 3, 0:MIX_C], ACT.Copy), "vt_ready")
            skip(4)
            need("h_ready", 1)
            squares(hchunks())
            root(std, var)
            for i in range(2 * TT):
                need("ntok_t", i + 1)
                inc(e.activation(ntok[:, i // 2, (i % 2) * 512:(i % 2 + 1) * 512], ps[:, 5 + i % 2, :], ACT.Copy),
                    "ntok_ready")
            units(8, copy_to(qT))
            for q in range(4):
                need("keys_t", q + 1)
                inc(e.activation(keysT[:, 4 * q:4 * q + 4, :].rearrange("p a k -> p (a k)"), ps[:, 4 + q, :], ACT.Copy),
                    "keysT_ready")
            for t in range(TT):
                for q in range(4):
                    need("sc_done", 4 * t + q + 1)
                    u = HEADS * t + 2 * q
                    inc(e.activation(score[:, u:u + 2, :].rearrange("p a k -> p (a k)"), ps[:, 4 * (t % 2) + q, :],
                                     ACT.Copy), "sc_ready")
            e.wait_ge(S["sc_ready"], c["sc_ready"].value())
            inc(e.activation(score[:, UNITS:UNITS + AHEAD, :], score[:, 0:AHEAD, :], ACT.Copy), "sc_ready")
            e.wait_ge(S["sc_ready"], c["sc_ready"].value())
            hsr, hst, cmx, gxp = c["hs_read"], c["hs_ready"], c["cand_max"], c["gexp"]
            used, xrd, gel = c["consumed"], c["x_ready"], c["gelu_ready"]
            used.at = RING

            def head_scores(n):
                hst.add()
                if not (isinstance(n, int) and n == 0):
                    e.wait_ge(hsr.sem, hst.value(1))
                src = score[:, n, :] if isinstance(n, int) else score[:, bass.ds(n, 1), :].rearrange("p a k -> p (a k)")
                e.activation(hs.rearrange("p a k -> p (a k)"), src, ACT.Copy).then_inc(hst.sem, 1)

            def gate_exp():
                cmx.add()
                e.wait_ge(cmx.sem, cmx.value())
                e.activation(gcur, top_v[:, 2, :], ACT.Exp, bias=small[:, 1:2], accum_out=small[:, 2:3]).then_inc(gxp.sem, 1)
                gxp.add()

            def hidden():
                e.activation(gdots, dots, ACT.Gelu_apprx_tanh).then_inc(gel.sem, 1)
                gel.add()

            for n in range(AHEAD):
                head_scores(n)
                gate_exp()
            with loop(e, TT, [(hst, 8), (cmx, 8), (gxp, 8), (used, 16 * RING), (xrd, 1), (gel, 8)]) as b:
                e.wait_ge(used.sem, used.value())
                e.activation(ps[:, 4:6, :].rearrange("p a k -> p (a k)"), ntok[:, bass.ds(b, 1), :].rearrange("p a k -> p (a k)"),
                             ACT.Copy).then_inc(xrd.sem, 1)
                xrd.add()
                head_scores(b * HEADS + AHEAD)
                used.add(RING)
                e.wait_ge(used.sem, used.value())
                hidden()
                gate_exp()
                with loop(e, HEADS - 1, [(hst, 1), (cmx, 1), (gxp, 1), (used, 2 * RING), (gel, 1)]) as h:
                    head_scores(b * HEADS + h + (AHEAD + 1))
                    used.add(2 * RING)
                    e.wait_ge(used.sem, used.value(1))
                    hidden()
                    gate_exp()
                used.add(RING)
            done.add(96)
            st["u"] += 48
            need("pT_t", 1)
            inc(e.activation(pT, ps[:, 6:8, :], ACT.Copy), "pT_ready")
            units(4, copy_to(peT))
            need("h_ready", 2)
            squares(hchunks())
            root(std, var)
            units(4, copy_to(sgT, func=ACT.Sigmoid))
            need("h_ready", 3)
            squares(hchunks())
            root(std, var)
            need("h_ready", 4)
            squares(hchunks())
            root(std, var)

            need("glr_ready", 1)
            inc(e.activation(glrT[0:16, :], ps[0:16, 5, :], ACT.Copy), "glog_in")
            for h in range(GLA_H):
                need("glog_a", h + 1)
                own(e.activation(gtmp[:, h, :], ps[:, 4 + h, :], ACT.Abs, bias=col("gla_b_gate_2", h)), "a_ch")
            own(e.activation(gtmp2, gtmp, ACT.Exp, scale=-1.0), "a_ch")
            inc(e.activation(gtmp2, gtmp2, ACT.Ln, bias=1.0), "glog_l")
            q_or_k = (copy_to(gq, scale=GLA_DK ** -0.5), copy_to(gk))
            for q in range(2):
                for p in range(2):
                    for j in range(2):
                        done.add()
                        e.wait_ge(done.sem, done.value())
                        q_or_k[q](ps[:, 2 * (st["u"] % 2) + j, :], 2 * p + j).then_inc(evacs.sem, 1)
                        evacs.add()
                    st["u"] += 1
            need("dq_ready", 1)
            inc(e.activation(qsub, gtmp, ACT.Exp, scale=1.0 / 16), "dq_exp")
            for i in range(2):
                need("dk_ready", i + 1)
                n = 16 * (i + 1)
                inc(e.activation(kd_g(i % 2)[:, :, 0:n], kd_g(i % 2)[:, :, 0:n], ACT.Exp, scale=1.0 / 16), "dk_exp")
            with loop(e, 2, [(done, 4), (evacs, 4)]) as i:
                for p in range(2):
                    for j in range(2):
                        done.add()
                        e.wait_ge(done.sem, done.value())
                        e.activation(gvt[:, 2 * j:2 * j + 2, bass.ds(i * (2 * UNIT) + p * UNIT, UNIT)],
                                     ps[:, 2 * p + j, :].rearrange("p (a k) -> p a k", a=2), ACT.Copy
                                     ).then_inc(evacs.sem, 1)
                        evacs.add()
            st["u"] += 4
            units(4, copy_to(gr, func=ACT.Silu))
            for i in range(2, 8):
                need("dk_ready", i + 1)
                n = 16 * (i + 1)
                inc(e.activation(kd_g(i % 2)[:, :, 0:n], kd_g(i % 2)[:, :, 0:n], ACT.Exp, scale=1.0 / 16), "dk_exp")
            need("ew_ready", 1)
            own(e.activation(gtmp, gb, ACT.Exp, scale=1.0 / 16), "ew_exp")
            own(e.activation(elast, gsubs(gb)[:, :, P - 1], ACT.Exp, scale=1.0 / 16), "ew_exp")
            inc(e.activation(gtmp2, gtmp2, ACT.Exp, scale=1.0 / 16), "ew_exp")
            for h in range(GLA_H):
                need("kw_t", h + 1)
                inc(e.activation(kwt[:, 4 * h:4 * h + 4, :], ps[:, 4 + h, :].rearrange("p (a k) -> p a k", a=4), ACT.Copy),
                    "kw_tok")
            for i in range(16):
                t, h = divmod(i, GLA_H)
                need("o_done", i + 1)
                inc(e.activation(goT[:, 2 * h:2 * h + 2, t * P:(t + 1) * P],
                                 ps[:, 4 + i % 4, 0:2 * P].rearrange("p (a k) -> p a k", a=2), ACT.Copy), "o_evac")
            need("o_evac", 16)
            squares([goT[:, k, :] for k in range(DC)])
            root(gtmp2, gtmp)
            skip(4)

            def ffn(h):
                need("h_ready", h)
                squares(hchunks())
                root(std, var)
                dve = Count(S["dve_evac"], 4)
                dve.at = st["dve"]
                with loop(e, FH, [(done, 4), (evacs, 2), (dve, 2)]):
                    for j in range(2):
                        done.add()
                        e.wait_ge(done.sem, done.value())
                        e.wait_ge(dve.sem, dve.value(1))
                        e.activation(gsil[:, j, :], ps[:, j, :], ACT.Silu).then_inc(evacs.sem, 1)
                        evacs.add()
                        dve.add()
                    done.add(2)
                done.add(16)
                st["dve"] = dve.at + 8

            st["dve"] = 4 + 8 + 8
            ffn(5)
            st["u"] += 22 + 8

            need("h_ready", 6)
            squares(hchunks())
            root(std, var)
            need("pos_in", 16)
            units(3, copy_to(cT6))
            e.wait_ge(evacs.sem, evacs.value())
            squares([cT6[:, k, :] for k in range(3)])
            root(std, var)
            squares([cT6[:, 3 + k, :] for k in range(2)])
            root(std, var)
            for m in range(4):
                for j in range(3):
                    done.add()
                    e.wait_ge(done.sem, done.value())
                    dst = qr[:, m, :] if j == 2 else qn[:, 2 * m + j, :]
                    e.activation(dst, ps[:, (3 * m + j) % 4, :], ACT.Copy).then_inc(evacs.sem, 1)
                    evacs.add()
            st["u"] += 4
            with loop(e, 4, [(done, 4), (evacs, 4)]) as i:
                for p in range(2):
                    b = 2 * ((st["u"] + p) % 2)
                    done.add()
                    e.wait_ge(done.sem, done.value())
                    e.activation(kn[:, bass.ds(i * 2 + p, 1), :].rearrange("p a k -> p (a k)"), ps[:, b, :], ACT.Copy
                                 ).then_inc(evacs.sem, 1)
                    evacs.add()
                    done.add()
                    e.wait_ge(done.sem, done.value())
                    e.activation(vt[:, :, bass.ds(i * 256 + p * VDIM, VDIM)],
                                 ps[:, b + 1, :].rearrange("p (a k) -> p a k", a=TT), ACT.Copy).then_inc(evacs.sem, 1)
                    evacs.add()
            st["u"] += 8
            need("angle_ready", 1)
            inc(e.activation(tri, rtmp, ACT.Sin), "trig_ready")

            SCALE = float(NOPE + ROPE) ** -0.5

            def evac_p(i):
                h, t = divmod(i, TT)
                need("att_t", i + 1)
                if t == 0 and h:
                    need("att_o", h)
                inc(e.activation(pTt[:, 0:t + 1, t * P:(t + 1) * P],
                                 ps[:, 2 + i % 2, 0:(t + 1) * P].rearrange("p (a k) -> p a k", k=P), ACT.Copy), "att_pt")

            for i in range(MLA_H * TT):
                h, t = divmod(i, TT)
                n = (t + 1) * P
                need("att_m", i + 1)
                if i >= 2:
                    need("att_t", i - 1)
                inc(e.activation(pp[:, i % 2, 0:n], ps[:, 4 + i % 2, 0:n], ACT.Exp, scale=SCALE,
                                 bias=attsm[:, i % 2, 1:2], accum_out=attsm[:, i % 2, 2:3]), "att_p")
                if i:
                    evac_p(i - 1)
                    if t == 0:
                        need("att_o", h)
                        inc(e.activation(oT[:, h - 1, :], ps[:, 6 + (h - 1) % 2, :], ACT.Copy), "att_oe")
            evac_p(MLA_H * TT - 1)
            need("att_o", MLA_H)
            inc(e.activation(oT[:, MLA_H - 1, :], ps[:, 6 + (MLA_H - 1) % 2, :], ACT.Copy), "att_oe")
            skip(4)
            st["dve"] += 8
            ffn(7)
            need("h_ready", 8)
            squares(hchunks())
            root(std, var)
            for i in range(2 * TT):
                need("fin_t", i + 1)
                inc(e.activation(o_tok[:, i // 2, (i % 2) * 512:(i % 2 + 1) * 512], ps[:, 5 + i % 3, :], ACT.Copy),
                    "fin_ready")

        @block.vector
        def _(e):
            c = {n: Count(s) for n, s in S.items()}
            done, evacs = c["chunk_done"], Count(S["dve_evac"], 4)
            st = {"u": 0}

            def need(name, n):
                c[name].at = max(c[name].at, n)
                e.wait_ge(S[name], n)

            def inc(ins, name):
                ins.then_inc(S[name], 1)
                c[name].add()

            def own(ins, name="v_ch"):
                inc(ins, name)
                e.wait_ge(S[name], c[name].value())

            def bcast(ap, shape):
                return ap.to_broadcast(shape)

            def variance(dst, src, dim):
                c["ms_ready"].at += 1
                e.wait_ge(S["ms_ready"], c["ms_ready"].at)
                inc(e.tensor_scalar(dst, src, 1.0 / dim, EPS, ALU.mult, ALU.add), "var_ready")

            def rroot(dst, src):
                c["std_ready"].at += 1
                e.wait_ge(S["std_ready"], c["std_ready"].at)
                own(e.reciprocal(dst, src))

            def rms(src, dst, gain, n, dim=D, shift=None, signal="norm_full"):
                variance(var, ps[:, 4, :], dim)
                rroot(rstd, std)
                for k in range(n):
                    ins = e.scalar_tensor_tensor(out=dst[:, k, :], in0=src[:, k, :], scalar=gain(k), in1=rstd,
                                                 op0=ALU.mult, op1=ALU.mult)
                    if shift is None and k == n - 1:
                        own(ins, signal)
                    else:
                        inc(ins, "v_ch")
                if shift is not None:
                    base = c["v_ch"].at - n
                    for k in range(n):
                        e.wait_ge(S["v_ch"], base + k + 1)
                        ins = e.tensor_scalar(dst[:, k, :], dst[:, k, :], shift(k), None, ALU.add)
                        if k < n - 1:
                            ins.then_inc(S["v_shift"], 1)
                        else:
                            own(ins, signal)

            def skip(n):
                done.add(2 * n)
                st["u"] += n

            def residual(units, gate=None):
                with loop(e, units // 2, [(done, 4), (evacs, 4)]) as i:
                    for p in range(2):
                        for j in range(2):
                            done.add()
                            e.wait_ge(done.sem, done.value())
                            m = i * 4 + (2 * p + j)
                            bank = ps[:, 2 * ((st["u"] + p) % 2) + j, :]
                            dst = hT[:, bass.ds(m, 1), :].rearrange("p a k -> p (a k)")
                            if gate is None:
                                ins = e.tensor_tensor(dst, bank, dst, ALU.add)
                            else:
                                ins = e.scalar_tensor_tensor(out=dst, in0=bank, scalar=mod[:, bass.ds(m + gate, 1)],
                                                             in1=dst, op0=ALU.mult, op1=ALU.add)
                            ins.then_inc(evacs.sem, 1)
                            evacs.add()
                st["u"] += units

            def h_done():
                e.wait_ge(evacs.sem, evacs.value())
                own(e.tensor_copy(row[:, 0, 0:1], hT[:, 0, 0:1]), "h_ready")

            e.sem_inc(S["dve_evac"], 4)
            need("hT_in", DC)
            need("params_t", 1)
            own(e.tensor_copy(par[:, :, :].rearrange("p a k -> p (a k)"), ps[:, 4, 0:3 * P]), "params_c")
            need("ws_t", 1)
            own(e.tensor_copy(wsT.rearrange("p a k -> p (a k)")[:, 0:4 * P], ps[:, 5, :]))
            own(e.tensor_copy(wsT.rearrange("p a k -> p (a k)")[:, 4 * P:6 * P], ps[:, 6, 0:2 * P]))
            own(e.memset(wsT[64:128, :, 0:64], 0.0), "ws_ready")
            rms(hT, nT, lambda k: col("g_mix", k), DC)

            e.wait_ge(S["act_evac"], 4 + 6)
            need("consts", 1)
            own(e.tensor_tensor(padA[:, :, TAPS_A - 1:], z[:, 0:3, :], z[:, 3:6, :], ALU.mult))
            for k in range(3):
                inc(e.tensor_scalar(cvA[:, k, :], padA[:, k, 0:T], col("conv_a_w", k), col("conv_a_b", k),
                                    ALU.mult, ALU.add), "v_ch")
            for tap in range(1, TAPS_A):
                for k in range(3):
                    e.wait_ge(S["v_ch"], c["v_ch"].value(2))
                    inc(e.scalar_tensor_tensor(out=cvA[:, k, :], in0=padA[:, k, tap:tap + T],
                                               scalar=col("conv_a_w", 3 * tap + k), in1=cvA[:, k, :],
                                               op0=ALU.mult, op1=ALU.add), "v_ch")
            e.wait_ge(S["v_ch"], c["v_ch"].value())
            own(e.tensor_copy(row[:, 0, 0:1], cvA[:, 0, 0:1]), "gl_src")

            def head_center(src):
                c["gl_mean"].at += 1
                e.wait_ge(S["gl_mean"], c["gl_mean"].at)
                for k in range(3):
                    own(e.tensor_tensor(src[:, k, :], src[:, k, :], ps[:, 5 + k, :], ALU.subtract), "gl_cen")

            def head_scale(src):
                c["gl_var"].at += 1
                e.wait_ge(S["gl_var"], c["gl_var"].at)
                own(e.tensor_scalar(gvar, ps[:, 5:8, :], EPS, None, ALU.add), "gl_veps")
                c["gl_std"].at += 1
                e.wait_ge(S["gl_std"], c["gl_std"].at)
                own(e.reciprocal(gvar, gvar))
                own(e.tensor_tensor(src, src, gvar, ALU.mult), "mix_scaled")

            def short_conv():
                own(e.tensor_tensor(padB[:, :, TAPS_B - 1:], z[:, 8:10, :], z[:, 10:12, :], ALU.mult))
                yb = mixT[:, 3:5, :]
                for k in range(2):
                    own(e.tensor_scalar(yb[:, k, :], padB[:, k, 0:T], col("conv_b_w", k), None, ALU.mult))
                    for tap in range(1, TAPS_B):
                        own(e.scalar_tensor_tensor(out=yb[:, k, :], in0=padB[:, k, tap:tap + T],
                                                   scalar=col("conv_b_w", 2 * tap + k), in1=yb[:, k, :],
                                                   op0=ALU.mult, op1=ALU.add))
                own(e.tensor_tensor(yb, yb, z[:, 6:8, :], ALU.mult))

            head_center(cvA)
            e.wait_ge(S["act_evac"], 4 + 18)
            head_scale(cvA)
            own(e.tensor_copy(row[:, 0, 0:1], z[:, 15, 0:1]), "gl_src")
            head_center(z[:, 15:18, :])
            short_conv()
            head_scale(z[:, 15:18, :])
            skip(9)
            need("bs_in", 96)
            for k in range(3):
                need("mix_ready", k + 1)
                for q in range(2):
                    rows_ = slice(64 * q, 64 * q + 64)
                    own(e.tensor_tensor(work[rows_, 3, :].rearrange("p (b i) -> p b i", b=TT),
                                        ps[rows_, 5 + q, :].rearrange("p (b i) -> p b i", b=TT),
                                        bsb[rows_, k:k + 1, :].to_broadcast([64, TT, P]), ALU.add))
                own(e.tensor_tensor(mixT[:, 5 + k, :], work[:, 3, :], z[:, 12 + k, :], ALU.mult), "sg_done")
            residual(4)
            h_done()

            rms(hT, nT, lambda k: col("g_ffn", k), DC)
            skip(8)
            need("sc_ready", 4 * TT + 1)
            need("consts", 2)
            used = c["consumed"]
            landed = [Count(s) for s in row_landed]
            hst, gxp = c["hs_ready"], c["gexp"]
            vch, mk, rdy = c["v_ch"], c["hs_read"], c["idx_ready"]
            cmx, gel, xrd, gat = c["cand_max"], c["gelu_ready"], c["x_ready"], c["gates_ready"]

            def signal(ins, count):
                ins.then_inc(count.sem, 1)
                count.add()
                e.wait_ge(count.sem, count.value())
                e.sem_inc(S["vector_step"], 1)

            def chain(ins):
                signal(ins, vch)

            def top16(values, a):
                chain(e.max(top_v[:, a, 0:8], values))
                chain(e.max_index(top_i[:, a, 0:8], top_v[:, a, 0:8], values))
                chain(e.match_replace(values, top_v[:, a, 0:8], values, -3e38))
                chain(e.max(top_v[:, a, 8:16], values))

            def topk(n):
                hst.add()
                e.wait_ge(hst.sem, hst.value())
                e.sem_inc(S["vector_step"], 1)
                for a in range(2):
                    top16(hs[:, a, :], a)
                    ins = e.max_index(top_i[:, a, 8:16], top_v[:, a, 8:16], hs[:, a, :])
                    if a == 0:
                        chain(ins)
                    else:
                        signal(ins, mk)
                chain(e.tensor_tensor(cand, top_v[:, 0, :].rearrange("p (a b) -> p a b", b=1).to_broadcast([P, TOPK, TOPK]),
                                      top_v[:, 1:2, :].to_broadcast([P, TOPK, TOPK]), ALU.add))
                flat = cand.rearrange("p a b -> p (a b)")
                top16(flat, 2)
                chain(e.max_index(top_i[:, 2, 8:16], top_v[:, 2, 8:16], flat))
                signal(e.tensor_scalar(small[:, 1:2], top_v[:, 2, 0:1], -1.0, None, ALU.mult), cmx)
                chain(e.tensor_scalar(pick_i[:, 0, :], top_i[:, 2, :], 4, None, ALU.logical_shift_right))
                chain(e.tensor_scalar(pick_i[:, 1, :], top_i[:, 2, :], TOPK - 1, None, ALU.bitwise_and))
                chain(e.tensor_copy(pick_f, pick_i))
                chain(e.tensor_copy(top_f, top_i[:, 0:2, :]))
                for a in range(2):
                    chain(e.tensor_tensor(onehot, pick_f[:, a, :].rearrange("p (a b) -> p a b", b=1).to_broadcast([P, TOPK, TOPK]),
                                          iota16.rearrange("p (a b) -> p a b", a=1).to_broadcast([P, TOPK, TOPK]),
                                          ALU.is_equal))
                    chain(e.tensor_tensor(onehot, onehot, top_f[:, a:a + 1, :].to_broadcast([P, TOPK, TOPK]), ALU.mult))
                    chain(e.tensor_reduce(ek[:, a, :], onehot, AX.X, ALU.add))
                where = bass.ds(n * TOPK, TOPK)
                signal(e.scalar_tensor_tensor(out=idx_flat[:, where], in0=ek[:, 0, :], scalar=float(KEYS), in1=ek[:, 1, :],
                                              op0=ALU.mult, op1=ALU.add), rdy)
                gxp.add()
                e.wait_ge(gxp.sem, gxp.value())
                chain(e.reciprocal(small[:, 3:4], small[:, 2:3]))
                chain(e.tensor_scalar(gates.rearrange("p n k -> p (n k)")[:, where], gcur, small[:, 3:4], None, ALU.mult))

            def u_row(s, k):
                landed[s].add(16)
                e.wait_ge(used.sem, used.value(1) if not first[0] else used.value())
                e.wait_ge(landed[s].sem, landed[s].value())
                e.tensor_tensor_reduce(junk, ring[:, s, :], ps[:, 4:6, :].rearrange("p a k -> p (a k)"), 1.0, 0.0,
                                       ALU.mult, ALU.add, dots[:, k:k + 1]).then_inc(used.sem, 1)
                used.add()

            def v_row(s, k):
                landed[s].add(16)
                e.wait_ge(used.sem, used.value(1) if not first[0] else used.value())
                e.wait_ge(landed[s].sem, landed[s].value())
                acc = ps[:, 6:8, :].rearrange("p a k -> p (a k)")
                e.scalar_tensor_tensor(out=acc, in0=ring[:, s, :], scalar=coef[:, k:k + 1], in1=acc,
                                       op0=ALU.mult, op1=ALU.add).then_inc(used.sem, 1)
                used.add()

            first = [True]

            def coefs(n):
                gel.add()
                e.wait_ge(gel.sem, gel.value())
                e.wait_ge(used.sem, used.value())
                chain(e.tensor_tensor(coef, gdots, gates.rearrange("p n k -> p (n k)")[:, bass.ds(n * TOPK, TOPK)],
                                      ALU.mult))

            e.memset(junk, 0.0).then_inc(used.sem, RING)
            used.at = RING
            e.wait_ge(used.sem, RING)
            v0 = vch.at
            topk(0)
            steps = vch.at - v0
            topk(1)
            per = [(hst, 8), (gxp, 8), (mk, 8), (rdy, 8), (cmx, 8), (gel, 8), (xrd, 1), (used, 16 * RING),
                   (vch, 8 * steps + 8 + 2)] + [(l, 256) for l in landed] + [(c["acc_ready"], 1), (c["acc_t"], 1),
                                                                          (c["acc_added"], 1)]
            with loop(e, TT, per) as b:
                chain(e.memset(ps[:, 6:8, :], 0.0))
                xrd.add()
                e.wait_ge(xrd.sem, xrd.value())
                for s in range(RING):
                    u_row(s, s)
                topk(b * HEADS + AHEAD)
                coefs(b * HEADS)
                with loop(e, HEADS - 1, [(hst, 1), (gxp, 1), (mk, 1), (rdy, 1), (cmx, 1), (gel, 1), (used, 2 * RING),
                                         (vch, steps + 1)] + [(l, 32) for l in landed]) as h:
                    for half in range(2):
                        for q in range(8):
                            u_row(2 * q, half * 8 + q)
                            v_row(2 * q + 1, half * 8 + q)
                    topk(b * HEADS + h + (AHEAD + 1))
                    coefs(b * HEADS + h + 1)
                first[0] = True
                for s in range(RING):
                    v_row(s, s)
                e.wait_ge(used.sem, used.value())
                signal(e.tensor_copy(acc_sb, ps[:, 6:8, :].rearrange("p a k -> p (a k)")), c["acc_ready"])
                c["acc_t"].add()
                e.wait_ge(c["acc_t"].sem, c["acc_t"].value())
                dst = hT[:, :, bass.ds(b * P, P)]
                signal(e.tensor_tensor(dst, ps[:, 2:4, :].rearrange("p a (c k) -> p (a c) k", k=P), dst, ALU.add),
                       c["acc_added"])
                chain(e.memset(small[:, 4:5], 0.0))
            own(e.tensor_copy(row[:, 0, 0:1], hT[:, 0, 0:1]), "h_ready")
            done.add(96)
            st["u"] += 48
            need("chunk_done", done.at)
            own(e.tensor_tensor(mod[:], ps[:, 0, 0:96], col("ada_b_2", 0, 96), ALU.add), "mod_ready")
            for k, (name, off) in enumerate((("norm_mix_2", 8), ("norm_ffn_2", 32))):
                for layer in range(2):
                    own(e.scalar_tensor_tensor(out=gmod[:, 2 * layer + k, :], in0=mod[:, 48 * layer + off:48 * layer + off + 8],
                                               scalar=1.0, in1=col(name, 8 * layer, 8), op0=ALU.add, op1=ALU.mult))
            rms(hT, nT, lambda k: col("g_ple", k), DC)
            for k in range(DC):
                e.wait_ge(S["act_evac"], 4 + 18 + 16 + 8 + k + 1)
                own(e.tensor_tensor(sgT[:, k, :], sgT[:, k, :], peT[:, k, :], ALU.mult))
                ins = e.tensor_tensor(hT[:, k, :], hT[:, k, :], sgT[:, k, :], ALU.add)
                own(ins, "h_ready" if k == DC - 1 else "v_ch")
            skip(8)
            rms(hT, hT, lambda k: col("g_final", k), DC)
            own(e.tensor_copy(row[:, 0, 0:1], hT[:, 0, 0:1]), "h_ready")

            def modulated(layer, k):
                rms(hT, nT, lambda m: gmod[:, 2 * layer + k, m:m + 1], DC,
                    shift=lambda m: mod[:, 48 * layer + 24 * k + m:48 * layer + 24 * k + m + 1])

            modulated(0, 0)
            for h in range(GLA_H):
                need("a_ch", h + 1)
                own(e.tensor_scalar(gb[:, h, :], ps[:, 4 + h, :], col("gla_b_gate_2", h), 0.0, ALU.add, ALU.min), "glog_v")
            need("glog_l", 1)
            need("consts", 3)
            own(e.tensor_tensor(gtmp, gb, gtmp2, ALU.subtract))
            for h in range(GLA_H):
                own(e.tensor_tensor_scan(gb[:, h, :], reset, gtmp[:, h, :], 0.0, ALU.mult, ALU.add))
            runs = gb.rearrange("p h (i s) -> p (h i) s", s=GLA_SUB)
            own(e.tensor_tensor(gtmp.rearrange("p h (i s) -> p (h i) s", s=GLA_SUB), runs,
                                runs[:, :, 8:9].to_broadcast([P, 4 * T // GLA_SUB, GLA_SUB]), ALU.subtract), "dq_ready")
            gbg, gkg = gsubs(gb), gsubs(gk)

            def k_diff(i):
                n = 16 * (i + 1)
                if i >= 2:
                    need("amat_done", i - 1)
                own(e.tensor_tensor(kd_g(i % 2)[:, :, 0:n], gbg[:, :, 16 * i + 8:16 * i + 9].to_broadcast([P, GLA_G, n]),
                                    gbg[:, :, 0:n], ALU.subtract), "dk_ready")

            k_diff(0)
            k_diff(1)
            e.wait_ge(S["act_evac"], 4 + 50)
            need("dq_exp", 1)
            own(e.tensor_tensor(qsub, qsub, gq, ALU.mult), "q_sub")
            for i in range(8):
                n = 16 * (i + 1)
                need("dk_exp", i + 1)
                own(e.tensor_tensor(kd_g(i % 2)[:, :, 0:n], kd_g(i % 2)[:, :, 0:n], gkg[:, :, 0:n], ALU.mult), "k_sub")
                if i + 2 < 8:
                    k_diff(i + 2)
            own(e.tensor_tensor(gsubs(gtmp2), gbg[:, :, P - 1:P].to_broadcast([P, GLA_G, P]), gbg, ALU.subtract), "ew_ready")
            need("ew_exp", 3)
            own(e.tensor_tensor(gq, gq, gtmp, ALU.mult), "ew_done")
            own(e.tensor_tensor(gtmp2, gtmp2, gk, ALU.mult), "kw_ready")
            need("amat_done", 8)
            for h in range(GLA_H):
                own(e.tensor_tensor(amat[:, 4 * h:4 * h + 4, :], ps[:, 4 + h, :].rearrange("p (a k) -> p a k", a=4),
                                    keep.rearrange("p (a k) -> p a k", a=1).to_broadcast([P, 4, P]), ALU.mult), "a_ready")
            for i in range(16):
                t, h = divmod(i, GLA_H)
                need("o_evac", i + 1)
                src = ps[:, 4 + i % 4, 2 * P:4 * P]
                if t == 0:
                    ins = e.tensor_copy(state[:, h, :], src)
                elif t < TT - 1:
                    ins = e.scalar_tensor_tensor(out=state[:, h, :], in0=state[:, h, :],
                                                 scalar=elast[:, h * TT + t:h * TT + t + 1], in1=src,
                                                 op0=ALU.mult, op1=ALU.add)
                else:
                    break
                own(ins, "s_new")
            variance(gtmp, ps[:, 4:8, :], GLA_DV)
            rroot(gtmp2, gtmp2)
            e.wait_ge(S["act_evac"], 4 + 66)
            for k in range(DC):
                own(e.scalar_tensor_tensor(out=goT[:, k, :], in0=goT[:, k, :], scalar=col("gla_g_out_2", k % 2),
                                           in1=gtmp2[:, k // 2, :], op0=ALU.mult, op1=ALU.mult))
            own(e.tensor_tensor(goT[:, :, :], goT[:, :, :], gr, ALU.mult), "gla_r")
            skip(12)
            residual(4, gate=16)
            h_done()

            def ffn(layer):
                modulated(layer, 1)
                act = Count(S["act_evac"], st["act"])
                with loop(e, FH, [(done, 4), (evacs, 2), (act, 2)]) as i:
                    done.add(2)
                    for j in range(2):
                        act.add()
                        e.wait_ge(act.sem, act.value())
                        done.add()
                        e.wait_ge(done.sem, done.value())
                        e.tensor_tensor(hid[:, bass.ds(i * 2 + j, 1), :].rearrange("p a k -> p (a k)"), ps[:, 2 + j, :],
                                        gsil[:, j, :], ALU.mult).then_inc(evacs.sem, 1)
                        evacs.add()
                st["act"] = act.at
                with loop(e, 2, [(done, 8), (evacs, 4)]) as i:
                    for half in range(2):
                        done.add(2)
                        for j in range(2):
                            done.add()
                            e.wait_ge(done.sem, done.value())
                            m = i * 4 + (2 * half + j)
                            dst = hT[:, bass.ds(m, 1), :].rearrange("p a k -> p (a k)")
                            e.scalar_tensor_tensor(out=dst, in0=ps[:, 2 * half + j, :],
                                                   scalar=mod[:, bass.ds(m + (48 * layer + 40), 1)], in1=dst,
                                                   op0=ALU.mult, op1=ALU.add).then_inc(evacs.sem, 1)
                            evacs.add()
                st["u"] += 30
                h_done()

            st["act"] = 4 + 18 + 16 + 16 + 24
            ffn(0)

            modulated(1, 0)
            need("pos_in", 16)
            own(e.tensor_copy(ang, pos_i))
            own(e.tensor_scalar(ang, ang, col("inv_freq"), None, ALU.mult))
            for q, turn in ((0, 0.25), (1, 0.0)):
                n_, r_ = rtmp[:, q, :], tri[:, q, :]
                own(e.tensor_scalar(n_, ang, float(1 / (2 * np.pi)), turn, ALU.mult, ALU.add))
                own(e.tensor_scalar(n_, n_, ROUND, None, ALU.add))
                own(e.tensor_scalar(n_, n_, ROUND, None, ALU.subtract))
                own(e.scalar_tensor_tensor(out=r_, in0=n_, scalar=-PI2_A, in1=ang, op0=ALU.mult, op1=ALU.add))
                own(e.scalar_tensor_tensor(out=r_, in0=n_, scalar=-PI2_B, in1=r_, op0=ALU.mult, op1=ALU.add))
                own(e.scalar_tensor_tensor(out=r_, in0=n_, scalar=-PI2_C, in1=r_, op0=ALU.mult, op1=ALU.add))
                own(e.tensor_scalar(r_, r_, float(turn * 2 * np.pi), PI_IN, ALU.add, ALU.min))
                own(e.tensor_scalar(n_, r_, -PI_IN, None, ALU.max))
            own(e.tensor_copy(row[:, 1, 0:1], ang[:, 0:1]), "angle_ready")
            e.wait_ge(S["act_evac"], st["act"] + 6)
            rms(cT6, cT6, lambda k: col("mla_g_q_2", k), 3, dim=384)
            rms(cT6[:, 3:5, :], cT6[:, 3:5, :], lambda k: col("mla_g_kv_2", k), 2, dim=256)
            e.wait_ge(S["act_evac"], st["act"] + 6 + 12 + 16)
            st["act"] += 34
            need("trig_ready", 1)
            for r in range(5):
                x = cT6[:, 5, :] if r == 4 else qr[:, r, :]
                need("rot_done", r + 1)
                own(e.tensor_tensor(rtmp[:, 0, :], ps[:, 4 + r % 4, :], tri[:, 1, :], ALU.mult), "rope_read")
                own(e.tensor_tensor(x, x, tri[:, 0, :], ALU.mult))
                own(e.tensor_tensor(x, x, rtmp[:, 0, :], ALU.add), "rope_ready")
            need("consts", 4)
            SCALE = float(NOPE + ROPE) ** -0.5

            def peak(i):
                t = i % TT
                n = (t + 1) * P
                b = ps[:, 4 + i % 2, :]
                need("att_s", i + 1)
                own(e.tensor_tensor(b[:, t * P:n], b[:, t * P:n], cmask, ALU.add))
                own(e.tensor_reduce(attsm[:, i % 2, 0:1], b[:, 0:n], AX.X, ALU.max))
                own(e.tensor_scalar(attsm[:, i % 2, 1:2], attsm[:, i % 2, 0:1], -SCALE, None, ALU.mult), "att_m")

            peak(0)
            for i in range(MLA_H * TT):
                if i + 1 < MLA_H * TT:
                    peak(i + 1)
                n = (i % TT + 1) * P
                need("att_p", i + 1)
                own(e.reciprocal(attsm[:, i % 2, 3:4], attsm[:, i % 2, 2:3]))
                own(e.tensor_scalar(pp[:, i % 2, 0:n], pp[:, i % 2, 0:n], attsm[:, i % 2, 3:4], None, ALU.mult), "att_n")
            skip(3 + 4 + 8)
            done.add(4)
            residual(4, gate=48 + 16)
            h_done()
            ffn(1)
            rms(hT, nT, lambda k: col("final_norm_2", k), DC)


_INS = ["x", "p", "g_mix", "w_in", "conv_a_w", "conv_a_b", "ln_a_g", "ln_a_b", "conv_b_w", "ln_c_g", "ln_c_b", "w_s",
        "b_s", "w_out", "g_ffn", "w_q", "sub_keys", "expert_u", "expert_v", "g_ple", "w_pe", "w_pg", "g_final",
        "c_2", "positions_2", "ada_w_2", "ada_b_2", "norm_mix_2", "norm_ffn_2", "gla_w_in_2", "gla_w_gate_2",
        "gla_b_gate_2", "gla_g_out_2", "gla_w_out_2", "mla_w_in_2", "mla_g_q_2", "mla_w_q_up_2", "mla_g_kv_2",
        "mla_w_kv_up_2", "mla_w_out_2", "ffn_w_in_2", "ffn_w_out_2", "final_norm_2"]


def kernel(**inputs):
    import numpy as _np
    import concourse.bacc as _bacc
    from concourse import mybir as _mybir
    from concourse.bass_utils import run_bass_kernel_spmd as _run

    nc = _bacc.Bacc("TRN2", target_bir_lowering=False, num_devices=1)
    given = {name: _np.ascontiguousarray(inputs[name]) for name in _INS}
    freq = _np.float32(10000.0) ** (-_np.arange(0, ROPE, 2, dtype=_np.float32) / _np.float32(ROPE))
    given["inv_freq"] = _np.tile(_np.repeat(freq, 2), 2).astype(_np.float32).reshape(1, P)
    arrays, args = {}, {}
    for name, a in given.items():
        arrays[f"in_{name}_dram"] = a
        args[name] = nc.dram_tensor(f"in_{name}_dram", a.shape, _mybir.dt.from_np(a.dtype), kind="ExternalInput").ap()
    out = nc.dram_tensor("out_0_dram", (1, T, D), F32, kind="ExternalOutput").ap()
    build(nc, args, out)
    r = _run(nc, [arrays], core_ids=[0])
    return r.results[0]["out_0_dram"]
```

```python
from contextlib import ExitStack, contextmanager

import concourse.bass as bass
import numpy as np
from concourse import mybir

ALU = mybir.AluOpType
ACT = mybir.ActivationFunctionType
F32 = mybir.dt.float32
U32 = mybir.dt.uint32
I32 = mybir.dt.int32
F32R = mybir.dt.float32r
AX = mybir.AxisListType
P = 128
EPS = 1e-6

T = 512
D = 1024
DC = D // P
TT = T // P
MIX_A, MIX_B, MIX_C = 384, 256, 384
TAPS_A, TAPS_B = 31, 3
HEADS, KEYS, TOPK = 8, 128, 16
UNITS = TT * HEADS
AHEAD = 2
RING = 16
GLA_H, GLA_DK, GLA_DV, GLA_SUB = 4, 128, 256, 16
GLA_G = GLA_H * TT
PER_BLOCK = HEADS * TOPK
MLA_H, NOPE, ROPE, VDIM = 8, 128, 64, 128
D_FF = 2816
FC = D_FF // P
FH = FC // 2
UNIT = 256
SLOT = FH * UNIT
ARENA = 32256
MASKED = -1e30
ROUND = 1.5 * 2.0 ** 23
PI2_A, PI2_B, PI2_C = 6.28125, 0.0019350051879882812, 3.0199159819567e-07
PI_IN = 3.1415925


class Count:

    def __init__(self, sem, start=0):
        self.sem, self.at, self.dyn = sem, start, None

    def value(self, back=0):
        n = self.at - back
        return n if self.dyn is None else self.dyn + n

    def add(self, n=1):
        self.at += n


@contextmanager
def loop(eng, trips, counts):
    starts = [c.at for c, _ in counts]
    outer = [c.dyn for c, _ in counts]
    with eng.Fori(0, trips) as i:
        for c, per in counts:
            c.dyn = i * per if c.dyn is None else c.dyn + i * per
        yield i
        for (c, per), s in zip(counts, starts):
            assert c.at - s == per, (c.sem, c.at - s, per)
    for (c, per), s, o in zip(counts, starts, outer):
        c.at, c.dyn = s + per * trips, o


SEMS = ("x_in params_in ws_in bs_in keys_in ptok_in wgate_in pos_in wglr_in xtok_t hT_in params_t params_c "
        "chunk_done act_evac dve_evac consts consts_v sq_ready ms_ready var_ready std_ready norm_ready norm_full norm_scaled "
        "v_ch v_shift pool_step vector_step a_ch pl_ch gl_src gl_mean gl_cen gl_var gl_veps gl_std gl_norm mix_scaled mix_ready ws_t ws_ready vt_t vt_ready "
        "sg_done h_ready ntok_t ntok_ready keys_t keysT_ready sc_done sc_ready hs_ready hs_read cand_max gexp "
        "gates_ready idx_ready idx_copied u_used v_used diag_ready x_ready u_read dots_ready gelu_ready coef_ready acc_ready "
        "acc_t acc_added ada_done mod_ready cT_ready pT_t pT_ready sig_ready pe_used "
        "glr_ready glog_in glog_a glog_v glog_l scan_ready dq_ready dq_exp q_sub dk_ready dk_exp k_sub amat_done amat_read "
        "a_ready ew_ready ew_exp ew_done kw_ready kw_t kw_tok s_upd s_new o_done o_evac osq_done "
        "rope_src rot_done rope_read rope_ready angle_ready trig_ready cnorm_ready att_s att_m att_p att_n att_t att_pt att_o "
        "att_oe fin_t fin_ready out_done ada_in glr_in shift_ready hid_ready ada_ch ada_cols gr_ready go_chunk norm_chunk nhi_ready nlo_ready w_hi w_lo hid_raw hid_hi_ready").split()


def build(nc, A, out):
    with ExitStack() as ctx:
        S = {n: ctx.enter_context(nc.semaphore(n)) for n in SEMS}
        w_landed = [ctx.enter_context(nc.semaphore(f"w_landed{i}")) for i in range(2)]
        ada_landed = [ctx.enter_context(nc.semaphore(f"ada_landed{i}")) for i in range(2)]
        row_landed = [ctx.enter_context(nc.semaphore(f"row_landed{i}")) for i in range(RING)]

        def sb(name, *shape, dt=F32):
            return ctx.enter_context(nc.sbuf_tensor(name, [P, *shape], dt))

        hT = sb("hT", DC, T)
        row = sb("row", 3, T)
        var, std, rstd = row[:, 0, :], row[:, 1, :], row[:, 2, :]
        ident = sb("ident", P)
        ones = sb("ones", P)
        bdiag = sb("bdiag", P)
        rotm = sb("rotm", P)
        par_rows = sb("par_rows", 3, P)
        par = sb("par", 3, P)
        mod = sb("mod", 96)
        gmod = sb("gmod", 4, DC)
        cT = sb("cT", DC)
        def two_names(name, other, *shape):
            with nc.sbuf_tensor(name, [P, *shape], F32) as plain:
                pass
            return plain, sb(other, *shape, dt=F32R)

        nT, n_lo = two_names("nT", "n_lo", DC, T)
        work, n_hi = two_names("work", "n_hi", DC, T)
        wring, wlo = two_names("wring", "wlo", 2, SLOT)
        with nc.sbuf_tensor("arena", [P, ARENA], F32) as arena:
            pass
        hid_l = sb("hid_l", FC, T, dt=F32R)
        sb("beside_gates", 2, T)
        whi = sb("whi", 2, SLOT, dt=F32R)
        hid_h = sb("hid_h", FC, T, dt=F32R)

        class Region:
            def __init__(self, start=0):
                self.at = start

            def take(self, *shape, dt=None):
                n = int(np.prod(shape))
                ap = arena[:, self.at:self.at + n]
                self.at += n
                assert self.at <= ARENA, self.at
                if dt is not None:
                    ap = ap.bitcast(dt)
                if len(shape) == 2:
                    ap = ap.rearrange("p (a b) -> p a b", a=shape[0])
                if len(shape) == 3:
                    ap = ap.rearrange("p (a b c) -> p a b c", a=shape[0], b=shape[1])
                return ap

        ps = ctx.enter_context(nc.psum_tensor("ps", [P, 8, 512], F32))

        vectors, at = {}, [0, 0, 0]

        def vec(name, ap, tile):
            n = ap.shape[0]
            vectors[name] = (ap, tile, at[tile], n)
            at[tile] += n

        def rows(ap):
            return ap.rearrange("(c p) -> c p", p=P)

        for name in ("g_mix", "conv_a_b", "ln_a_g", "ln_a_b", "ln_c_g", "ln_c_b", "g_ffn", "g_ple", "gla_b_gate_2",
                     "gla_g_out_2", "mla_g_q_2", "mla_g_kv_2", "c_2"):
            vec(name, rows(A[name][0, :]), 0)
        vec("g_final", rows(A["g_final"]), 0)
        vec("final_norm_2", rows(A["final_norm_2"]), 0)
        vec("norm_mix_2", A["norm_mix_2"].rearrange("l (c p) -> (l c) p", p=P), 0)
        vec("norm_ffn_2", A["norm_ffn_2"].rearrange("l (c p) -> (l c) p", p=P), 0)
        vec("ada_b_2", A["ada_b_2"].rearrange("l (c p) -> (l c) p", p=P), 1)
        vec("inv_freq", A["inv_freq"], 1)
        vec("conv_b_w", A["conv_b_w"][0].rearrange("k (c p) -> (k c) p", p=P), 1)
        vec("conv_a_w", A["conv_a_w"][0].rearrange("k (c p) -> (k c) p", p=P), 2)

        def col(name, k=0, n=1):
            _, tile, r0, _ = vectors[name]
            return par[:, tile, r0 + k:r0 + k + n]

        R = Region()
        z = R.take(18, T)
        padA = R.take(3, TAPS_A - 1 + T)
        padB = R.take(2, TAPS_B - 1 + T)
        cvA = R.take(3, T)
        gvar = R.take(3, T)
        ws_in = R.take(6, P)
        wsT = R.take(6, P)
        bsb = R.take(3, P)
        vtok = R.take(TT, MIX_C)
        mixT = R.take(DC, T)
        x_tok = nT[:, :, :].rearrange("p (t c) k -> p t (c k)", t=TT)

        R = Region()
        score = R.take(UNITS + AHEAD, 2 * KEYS)
        ring = R.take(RING, D)
        R2 = Region((UNITS + AHEAD) * 2 * KEYS)
        qT = R2.take(2 * HEADS, T)
        keys_in = R2.take(2 * HEADS, P)
        keysT = R2.take(2 * HEADS, P)
        junk = R.take(D)
        acc_sb = R.take(D)
        hs = R.take(2, KEYS)
        cand = R.take(TOPK, TOPK)
        onehot = R.take(TOPK, TOPK)
        iota16 = R.take(TOPK)
        top_v = R.take(3, TOPK)
        top_i = R.take(3, TOPK, dt=U32)
        pick_i = R.take(2, TOPK, dt=U32)
        pick_f = R.take(2, TOPK)
        top_f = R.take(2, TOPK)
        ek = R.take(3, TOPK)
        gcur = R.take(TOPK)
        small = R.take(8)
        idx = R.take(UNITS + AHEAD, TOPK, dt=U32)
        idx_flat = idx.rearrange("p n k -> p (n k)")
        gates = R.take(UNITS + AHEAD, TOPK)
        cur = R.take(RING, dt=U32)
        dots = R.take(TOPK)
        gdots = R.take(TOPK)
        coef = R.take(TOPK)
        diag = nT[:, 0:4, :].rearrange("p a (b k) -> p (a b) k", k=P)
        zero = nT[:, 4, 0:P]
        ntok = work[:, :, :].rearrange("p (t c) k -> p t (c k)", t=TT)

        R = Region()
        p_tok = R.take(TT, UNIT)
        pT = R.take(2, T)
        peT = R.take(DC, T)
        sgT = R.take(DC, T)

        R = Region()
        gq = R.take(GLA_H, T)
        gk = R.take(GLA_H, T)
        gvt = R.take(TT, D)
        gr = R.take(DC, T)
        wglr = R.take(DC, 16)
        glrT = R.take(T)
        wgate = R.take(T)
        gb = R.take(GLA_H, T)
        gtmp = R.take(GLA_H, T)
        gtmp2 = R.take(GLA_H, T)
        qsub = R.take(GLA_H, T)
        reset = R.take(T)
        keep = R.take(P)
        elast = R.take(GLA_G)
        amat = R.take(GLA_G, P)
        kwt = R.take(GLA_G, P)
        state = R.take(GLA_H, GLA_DV)
        kd = work[:, :, :].rearrange("p (a c) k -> p a (c k)", a=2)
        goT = nT

        R = Region()
        cT6 = R.take(6, T)
        qn = R.take(MLA_H, T)
        qr = R.take(MLA_H // 2, T)
        kn = R.take(MLA_H, T)
        vt = R.take(TT, D)
        ang = R.take(T)
        tri = R.take(2, T)
        rtmp = R.take(2, T)
        pos_i = R.take(T, dt=I32)
        pp = R.take(4, T)
        pTt = R.take(TT, T)
        cmask = R.take(P)
        attsm = R.take(4, 4)
        oT = nT

        R = Region()
        hid = R.take(FC, T)
        gsil = R.take(2, T)

        R = Region(ARENA - 2 * DC * UNIT - 3 * D)
        aslot = R.take(2, DC, UNIT)
        asum = R.take(3 * D)

        R = Region()
        o_tok = R.take(TT, D)

        def gsubs(x):
            return x.rearrange("p h (t k) -> p (h t) k", k=P)

        def kd_g(a):
            return kd[:, a, :].rearrange("p (g k) -> p g k", g=GLA_G)

        marks = {}

        def sbank(i, n):
            return ps[:, (4, 5, 0, 1)[i % 4], 0:n]

        IN = {n: A[n] for n in A}
        w_in, w_out, w_q = IN["w_in"][0], IN["w_out"][0], IN["w_q"][0]
        gla_in = IN["gla_w_in_2"][0]
        mla_in = IN["mla_w_in_2"][0]

        block = ctx.enter_context(nc.Block())

        @block.sync
        def _(e):
            c = {n: Count(s) for n, s in S.items()}
            landed = [Count(s) for s in w_landed]
            done = c["chunk_done"]
            state_ = {"u": 0, "ends": []}

            def unit(W, col0, kc, k0=0, width=UNIT, chunks=2, back=None, extra=None):
                u = state_["u"]
                v = done.value(back) if back is not None else (
                    state_["ends"][-2] if len(state_["ends"]) >= 2 else None)
                if v is not None:
                    e.wait_ge(done.sem, v)
                dst = wring[:, u % 2, 0:kc * width].rearrange("p (k n) -> p k n", n=width)
                wide = width - (extra or 0)
                src = W[k0 * P:(k0 + kc) * P, bass.ds(col0, wide)].rearrange("(k p) n -> p k n", p=P)
                n = 16
                e.dma_start(dst[:, :, 0:wide], src).then_inc(landed[u % 2].sem, 16)
                if extra:
                    e.dma_start(dst[:, :, wide:width],
                                W[k0 * P:(k0 + kc) * P, bass.ds(col0 + wide - extra, extra)]
                                .rearrange("(k p) n -> p k n", p=P)).then_inc(landed[u % 2].sem, 16)
                done.add(chunks)
                state_["u"] += 1
                if back is None:
                    state_["ends"].append(done.at)

            def units(W, col0, n, kc):
                pairs = n // 2
                if pairs > 1:
                    with loop(e, pairs, [(done, 4)]) as i:
                        for j in range(2):
                            unit(W, i * (2 * UNIT) + (col0 + j * UNIT), kc, back=2)
                    state_["ends"] += [done.at - 2, done.at]
                else:
                    for j in range(2 * pairs):
                        unit(W, col0 + j * UNIT, kc)
                if n % 2:
                    unit(W, col0 + 2 * pairs * UNIT, kc)

            e.dma_start(x_tok, IN["x"][0].rearrange("(t p) d -> p t d", p=P)).then_inc(S["x_in"], 16)
            e.wait_ge(S["consts"], 1)
            for name, (ap, tile, r0, n) in vectors.items():
                e.dma_start(par_rows[r0:r0 + n, tile, :], ap).then_inc(S["params_in"], 16)
            e.dma_start(ws_in, IN["w_s"][0].rearrange("h i j -> i h j")).then_inc(S["ws_in"], 16)
            for h in range(6):
                e.dma_start(bsb[64 * (h % 2):64 * (h % 2) + 64, h // 2, :],
                            IN["b_s"][0, h:h + 1, :].to_broadcast([64, P])).then_inc(S["bs_in"], 16)
            units(w_in, 0, 3, DC)
            units(w_in, 2 * MIX_A, 6, DC)
            units(w_out, 0, 4, DC)
            units(w_q, 0, 8, DC)
            e.wait_ge(S["norm_full"], 2)
            e.dma_start(keys_in, IN["sub_keys"][0].rearrange("h s k d -> k (h s) d")).then_inc(S["keys_in"], 16)
            e.wait_ge(S["h_ready"], 2)
            e.dma_start(p_tok, IN["p"][0, 0].rearrange("(t p) d -> p t d", p=P)).then_inc(S["ptok_in"], 16)
            units(IN["w_pe"][0], 0, 4, 2)
            units(IN["w_pg"][0], 0, 4, DC)
            e.wait_ge(S["h_ready"], 4)
            e.dma_start(wglr, gla_in[:, 3072:3088].rearrange("(k p) n -> p k n", p=P)).then_inc(S["glr_in"], 16)
            e.dma_start(wgate[0:16, :], IN["gla_w_gate_2"][0]).then_inc(S["glr_in"], 16)
            units(gla_in, 0, 4, DC)
            units(gla_in, 1024, 4, DC)
            units(gla_in, 2048, 4, DC)
            units(IN["gla_w_out_2"][0], 0, 4, DC)

            def ffn(layer):
                W = IN["ffn_w_in_2"][layer]
                with loop(e, FH, [(done, 4)]) as i:
                    unit(W, i * UNIT, DC, back=2)
                    unit(W, i * UNIT + D_FF, DC, back=2)
                state_["ends"] += [done.at - 2, done.at]
                W = IN["ffn_w_out_2"][layer]
                with loop(e, 2, [(done, 8)]) as i:
                    for half in range(2):
                        for k in range(2):
                            unit(W, i * (2 * UNIT) + half * UNIT, FH, k0=k * FH, back=2)
                state_["ends"] += [done.at - 2, done.at]

            ffn(0)
            e.wait_ge(S["h_ready"], 6)
            e.dma_start(pos_i, IN["positions_2"][0:1, :].to_broadcast([P, T])).then_inc(S["pos_in"], 16)
            unit(mla_in, 0, DC)
            unit(mla_in, 256, DC)
            unit(mla_in, 512, DC, extra=ROPE)
            for m in range(4):
                u = state_["u"]
                e.wait_ge(done.sem, state_["ends"][-2])
                dst = wring[:, u % 2, 0:3 * 384].rearrange("p (k n) -> p k n", n=384)
                W = IN["mla_w_q_up_2"][0].rearrange("(k p) n -> p k n", p=P)
                for to, frm, n in ((0, 0, NOPE), (NOPE, 192, NOPE), (256, NOPE, ROPE), (320, 320, ROPE)):
                    e.dma_start(dst[:, :, to:to + n], W[:, :, 384 * m + frm:384 * m + frm + n]
                                ).then_inc(landed[u % 2].sem, 16)
                done.add(3)
                state_["u"] += 1
                state_["ends"].append(done.at)
            units(IN["mla_w_kv_up_2"][0], 0, 8, 2)
            units(IN["mla_w_out_2"][0], 0, 4, DC)
            ffn(1)
            e.wait_ge(S["fin_ready"], 2 * TT)
            e.dma_start(out[0].rearrange("(t p) d -> p t d", p=P), o_tok).then_inc(S["out_done"], 16)
            e.wait_ge(S["out_done"], 16)

        @block.tensor
        def _(e):
            c = {n: Count(s) for n, s in S.items()}
            landed = [Count(s) for s in w_landed]
            done, act, dve = c["chunk_done"], Count(S["act_evac"], 4), Count(S["dve_evac"], 4)
            st = {"u": 0}

            def need(name, n):
                c[name].at = max(c[name].at, n)
                e.wait_ge(S[name], n)

            def inc(ins, name, n=1):
                ins.then_inc(S[name], n)
                c[name].add(n)

            def settle():
                e.wait_ge(act.sem, act.value())
                e.wait_ge(dve.sem, dve.value())

            def slot(kc, width=UNIT, n=16):
                u = st["u"]
                st["u"] += 1
                landed[u % 2].add(n)
                e.wait_ge(landed[u % 2].sem, landed[u % 2].value())
                return wring[:, u % 2, 0:kc * width].rearrange("p (k n) -> p k n", n=width)

            def norm_chunks(full):
                sizes = [DC] * 6 + [3, 2, DC]
                base = sum(sizes[:full - 1]) - (full - 1)

                def wait(k):
                    if k < sizes[full - 1] - 1:
                        e.wait_ge(S["norm_chunk"], base + k + 1)
                    else:
                        e.wait_ge(S["norm_full"], full)
                return wait

            def unit(kc, rhs, evac, n=16, ready=None):
                w = slot(kc, n=n)
                for j in range(2):
                    b = 2 * ((st["u"] - 1) % 2) + j
                    e.wait_ge(evac.sem, evac.value(3))
                    for k in range(kc):
                        if ready and j == 0:
                            ready(k)
                        mm = e.matmul(ps[:, b, :], w[:, k, j * P:(j + 1) * P], rhs(k), start=(k == 0),
                                      stop=(k == kc - 1))
                    inc(mm, "chunk_done")
                    evac.add()

            def unit_tok(w, src, evac, st_bank):
                for j in range(2):
                    e.wait_ge(evac.sem, evac.value(3))
                    for q in range(2):
                        for k in range(DC):
                            mm = e.matmul(ps[:, st_bank + j, q * UNIT:(q + 1) * UNIT],
                                          src[:, k, (2 * j + q) * P:(2 * j + q + 1) * P], w[:, k, :],
                                          start=(k == 0), stop=(k == DC - 1))
                    inc(mm, "chunk_done")
                    evac.add()

            def pairs_of(n, body, evac, nland=16):
                if n // 2 > 1:
                    u0 = st["u"]
                    with loop(e, n // 2, [(done, 4), (evac, 4), (landed[0], nland), (landed[1], nland)]):
                        body()
                        body()
                    st["u"] = u0 + 2 * (n // 2)
                else:
                    for _ in range(2 * (n // 2)):
                        body()
                if n % 2:
                    body()

            def linear(n, kc, rhs, evac, ready=None):
                settle()
                pairs_of(n, lambda: unit(kc, rhs, evac, ready=ready), evac)

            def squares(n, bank, groups=1):
                if c["var_ready"].at:
                    need("var_ready", c["var_ready"].at)
                per = n // groups
                for g in range(groups):
                    for k in range(per):
                        need("sq_ready", c["sq_ready"].at + 1)
                        mm = e.matmul(ps[:, bank + g, :], ones[:], work[:, g * per + k, :], start=(k == 0),
                                      stop=(k == per - 1))
                inc(mm, "ms_ready")
                c["var_ready"].at += 1

            def nrhs(k):
                return nT[:, k, :]

            need("consts", 1)
            need("x_in", 16)
            for k in range(DC):
                if k >= 4:
                    need("hT_in", k - 3)
                for t in range(TT):
                    mm = e.transpose(ps[:, 4 + k % 4, t * P:(t + 1) * P], x_tok[:, t, k * P:(k + 1) * P], ident[:])
                inc(mm, "xtok_t")
            need("hT_in", 5)
            need("params_in", 16 * len(vectors))
            for k in range(3):
                mm = e.transpose(ps[:, 4, k * P:(k + 1) * P], par_rows[:, k, :], ident[:])
            inc(mm, "params_t")
            need("hT_in", 7)
            need("ws_in", 16)
            for h in range(6):
                mm = e.transpose(ps[:, 5 + h // 4, (h % 4) * P:(h % 4 + 1) * P], ws_in[:, h, :], ident[:])
            inc(mm, "ws_t")
            need("params_c", 1)
            need("ws_ready", 1)
            squares(DC, 4)
            linear(3, DC, nrhs, act, norm_chunks(1))
            linear(6, DC, nrhs, act)

            def ada(part, bank):
                need("ada_done", part + 1)
                for m in range(24):
                    mm = e.matmul(ps[:, bank, m:m + 1], asum[:, m * P:(m + 1) * P], ones[:, 0:1], start=True, stop=True)
                inc(mm, "ada_cols")

            def head_stats(src):
                if c["gl_veps"].at:
                    need("gl_veps", c["gl_veps"].at)
                need("gl_src", c["gl_src"].at + 1)
                for k in range(3):
                    mm = e.matmul(ps[:, 5 + k, :], bdiag[:], src[:, k, :], start=True, stop=True)
                inc(mm, "gl_mean")
                for k in range(3):
                    need("sq_ready", c["sq_ready"].at + 1)
                    mm = e.matmul(ps[:, 5 + k, :], bdiag[:], work[:, k, :], start=True, stop=True)
                inc(mm, "gl_var")
                c["gl_veps"].at += 1

            head_stats(cvA)
            head_stats(z[:, 15:18, :])
            settle()
            ada(0, 0)
            need("gl_norm", 2)
            for t in range(TT):
                b = 5 + t % 3
                if t >= 3:
                    need("vt_ready", t - 2)
                for k in range(3):
                    mm = e.transpose(ps[:, b, k * P:(k + 1) * P], z[:, 15 + k, t * P:(t + 1) * P], ident[:])
                inc(mm, "vt_t")
            need("vt_ready", TT)
            for k in range(3):
                if k:
                    need("sg_done", k)
                for par_ in range(2):
                    for b in range(TT):
                        mm = e.matmul(ps[:, 5 + par_, b * P:(b + 1) * P], vtok[:, b, k * P:(k + 1) * P],
                                      wsT[:, 2 * k + par_, :], start=True, stop=True)
                inc(mm, "mix_ready")
            need("sg_done", 3)
            need("mod_ready", 1)
            linear(4, DC, lambda k: mixT[:, k, :], dve)

            squares(DC, 4)
            need("norm_full", 2)
            for t in range(TT):
                for half in range(2):
                    if t or half:
                        need("ntok_ready", 2 * t + half)
                    for k in range(4):
                        kk = half * 4 + k
                        mm = e.transpose(ps[:, 5 + (2 * t + half) % 2, k * P:(k + 1) * P],
                                         nT[:, kk, t * P:(t + 1) * P], ident[:])
                    inc(mm, "ntok_t")
            linear(8, DC, nrhs, act)
            need("keys_in", 16)
            need("ntok_ready", 2 * TT)
            for q in range(4):
                for k in range(4):
                    mm = e.transpose(ps[:, 4 + q, k * P:(k + 1) * P], keys_in[:, 4 * q + k, :], ident[:])
                inc(mm, "keys_t")
            settle()
            need("keysT_ready", 4)
            for t in range(TT):
                for q in range(4):
                    b = 4 * (t % 2) + q
                    if t >= 2:
                        need("sc_ready", 4 * (t - 2) + q + 1)
                    for k in range(4):
                        mm = e.matmul(ps[:, b, k * P:(k + 1) * P], qT[:, 4 * q + k, t * P:(t + 1) * P],
                                      keysT[:, 4 * q + k, :], start=True, stop=True)
                    inc(mm, "sc_done")
            need("sc_ready", 4 * TT)
            vrow = [Count(s) for s in row_landed]
            dgr, vus = Count(S["diag_ready"]), Count(S["v_used"], RING)
            axr, aad = Count(S["acc_ready"]), Count(S["acc_added"])

            def v_row(s, k, stop=False):
                vrow[s].add(16)
                e.wait_ge(vrow[s].sem, vrow[s].value())
                dgr.add()
                e.wait_ge(dgr.sem, dgr.value())
                for q in range(2):
                    mm = e.matmul(ps[:, 6 + q, :], diag[:, k, :], ring[:, s, q * 512:(q + 1) * 512], start=False,
                                  stop=stop)
                mm.then_inc(vus.sem, 1)
                vus.add()

            need("consts_v", 1)
            with loop(e, TT, [(dgr, HEADS * TOPK), (vus, HEADS * TOPK), (axr, 1), (aad, 1)]
                      + [(l, 256) for l in vrow]):
                e.wait_ge(S["hT_in"], 1)
                e.wait_ge(aad.sem, aad.value())
                for q in range(8):
                    e.matmul(ps[:, 6 + q // 4, (q % 4) * P:(q % 4 + 1) * P], zero, ident[:], start=(q % 4 == 0), stop=False)
                for l in vrow:
                    l.add(16)
                with loop(e, HEADS - 1, [(dgr, TOPK), (vus, TOPK)] + [(l, 32) for l in vrow]):
                    for half in range(2):
                        for q in range(8):
                            vrow[2 * q].add(16)
                            v_row(2 * q + 1, half * 8 + q)
                for s in range(RING):
                    v_row(s, s, stop=(s == RING - 1))
                axr.add()
                e.wait_ge(axr.sem, axr.value())
                for k in range(DC):
                    mm = e.transpose(ps[:, 2 + k // 4, (k % 4) * P:(k % 4 + 1) * P], acc_sb[:, k * P:(k + 1) * P],
                                     ident[:])
                inc(mm, "acc_t")
                aad.add()

            need("ptok_in", 16)
            need("acc_added", TT)
            for k in range(2):
                for t in range(TT):
                    mm = e.transpose(ps[:, 6 + k, t * P:(t + 1) * P], p_tok[:, t, k * P:(k + 1) * P], ident[:])
            inc(mm, "pT_t")
            need("pT_ready", 1)
            linear(4, 2, lambda k: pT[:, k, :], act)
            settle()
            squares(DC, 4)
            linear(4, DC, nrhs, act, norm_chunks(3))
            squares(DC, 4)
            squares(DC, 4)

            need("glr_in", 32)
            for k in range(DC):
                norm_chunks(5)(k)
                mm = e.matmul(ps[0:16, 5, :], wglr[:, k, :], nT[:, k, :], start=(k == 0), stop=(k == DC - 1))
            inc(mm, "glr_ready")
            need("glog_in", 1)
            for h in range(GLA_H):
                mm = e.matmul(ps[:, 4 + h, :], wgate[0:16, h * P:(h + 1) * P], glrT[0:16, :], start=True, stop=True)
                inc(mm, "glog_a")
            settle()
            ada(1, 0)
            need("mod_ready", 2)
            linear(4, DC, nrhs, act)
            settle()
            u0 = st["u"]
            with loop(e, 2, [(done, 4), (act, 4), (landed[0], 16), (landed[1], 16)]):
                for p in range(2):
                    unit_tok(slot(DC), nT, act, 2 * p)
            st["u"] = u0 + 4
            settle()
            need("glog_v", GLA_H)
            need("q_sub", 1)
            r_first = st["u"]
            for i in range(8):
                need("k_sub", i + 1)
                for g in range(GLA_G):
                    mm = e.matmul(ps[:, 4 + g // 4, (g % 4) * P + 16 * i:(g % 4) * P + 16 * i + 16],
                                  kd_g(i % 2)[:, g, :], gsubs(qsub)[:, g, 16 * i:16 * i + 16], start=True, stop=True)
                inc(mm, "amat_done")
                j = i % 2
                if j == 0:
                    w = slot(DC)
                e.wait_ge(act.sem, act.value(3))
                for k in range(DC):
                    mm = e.matmul(ps[:, 2 * ((i // 2 + r_first) % 2) + j, :], w[:, k, j * P:(j + 1) * P], nrhs(k),
                                  start=(k == 0), stop=(k == DC - 1))
                inc(mm, "chunk_done")
                act.add()
            settle()
            need("kw_ready", 1)
            for h in range(GLA_H):
                need("a_ready", h + 1)
                for t in range(TT):
                    mm = e.transpose(ps[:, 4 + h, t * P:(t + 1) * P], gtmp2[:, h, t * P:(t + 1) * P], ident[:])
                inc(mm, "kw_t")
            need("ew_done", 1)
            for t in range(TT):
                for h in range(GLA_H):
                    i = t * GLA_H + h
                    g = h * TT + t
                    b = 4 + i % 4
                    if i < 4:
                        need("kw_tok", h + 1)
                    else:
                        need("o_evac", i - 3)
                        need("s_new", i - 3)
                    for v in range(2):
                        mm = e.matmul(ps[:, b, v * P:(v + 1) * P],
                                      gvt[:, t, h * GLA_DV + v * P:h * GLA_DV + (v + 1) * P], amat[:, g, :],
                                      start=True, stop=(t == 0))
                        if t:
                            mm = e.matmul(ps[:, b, v * P:(v + 1) * P], state[:, h, v * P:(v + 1) * P],
                                          gq[:, h, t * P:(t + 1) * P], start=False, stop=True)
                    if t < TT - 1:
                        mm = e.matmul(ps[:, b, 2 * P:4 * P], kwt[:, g, :], gvt[:, t, h * GLA_DV:(h + 1) * GLA_DV],
                                      start=True, stop=True)
                    inc(mm, "o_done")
            ada(2, 0)
            need("o_evac", 16)
            squares(DC, 4, groups=4)
            need("mod_ready", 3)
            linear(4, DC, nrhs, dve, lambda k: e.wait_ge(S["go_chunk"], k + 1))

            def split_unit(kc):
                slot(kc)
                w_hi.add()
                w_lo.add()
                q = (st["u"] - 1) % 2
                return [x[:, q, 0:kc * UNIT].rearrange("p (k n) -> p k n", n=UNIT) for x in (whi, wlo)]

            def split_product(bank, w, j, kc, hi, lo, start, stop, ready=None):
                wh, wl = w
                cols = slice(j * P, (j + 1) * P)
                e.wait_ge(w_hi.sem, w_hi.value())
                for k in range(kc):
                    if ready:
                        e.wait_ge(ready[0].sem, ready[0].at + k + 1)
                    e.matmul(bank, wh[:, k, cols], hi(k), start=(start and k == 0), stop=False)
                e.wait_ge(w_lo.sem, w_lo.value())
                for k in range(kc):
                    e.matmul(bank, wl[:, k, cols], hi(k), start=False, stop=False)
                for k in range(kc):
                    if ready:
                        e.wait_ge(ready[1].sem, ready[1].at + k + 1)
                    mm = e.matmul(bank, wh[:, k, cols], lo(k), start=False, stop=(stop and k == kc - 1))
                inc(mm, "chunk_done")

            w_hi, w_lo = c["w_hi"], c["w_lo"]

            def ffn(layer):
                squares(DC, 4)
                marks[f"ffn{layer}"] = (st["u"], [l.at for l in landed])
                settle()
                counts = [(landed[0], 16), (landed[1], 16), (w_hi, 2), (w_lo, 2)]
                with loop(e, FH, [(done, 4), (act, 2), (dve, 2)] + counts):
                    for p, evac in enumerate((act, dve)):
                        w = split_unit(DC)
                        for j in range(2):
                            e.wait_ge(evac.sem, evac.value(1))
                            split_product(ps[:, 2 * p + j, :], w, j, DC, lambda k: n_hi[:, k, :], lambda k: n_lo[:, k, :],
                                          True, True, (c["nhi_ready"], c["nlo_ready"]) if (p, j) == (0, 0) else None)
                            evac.add()
                st["u"] += 2 * (FH - 1)
                c["nhi_ready"].add(DC)
                c["nlo_ready"].add(DC)
                settle()
                need("hid_ready", c["hid_ready"].at + FC)
                with loop(e, 2, [(done, 8), (dve, 4), (landed[0], 32), (landed[1], 32), (w_hi, 4), (w_lo, 4)]):
                    for half in range(2):
                        for kh in range(2):
                            w = split_unit(FH)
                            for j in range(2):
                                if kh == 0:
                                    e.wait_ge(dve.sem, dve.value(3 - j))
                                split_product(ps[:, 2 * half + j, :], w, j, FH, lambda k: hid_h[:, kh * FH + k, :],
                                              lambda k: hid_l[:, kh * FH + k, :], kh == 0, kh == 1)
                        dve.add(2)
                st["u"] += 4

            ffn(0)

            squares(DC, 4)
            settle()
            for n in range(3):
                unit(DC, nrhs, act, n=32 if n == 2 else 16, ready=norm_chunks(6))
            squares(3, 4)
            squares(2, 4)
            need("norm_full", 7)
            settle()
            for m in range(4):
                w = slot(3, width=384, n=64)
                for j in range(3):
                    e.wait_ge(act.sem, act.value(3))
                    for k in range(3):
                        mm = e.matmul(ps[:, (3 * m + j) % 4, :], w[:, k, j * P:(j + 1) * P], cT6[:, k, :], start=(k == 0), stop=(k == 2))
                    inc(mm, "chunk_done")
                    act.add()
            need("norm_full", 8)
            settle()

            def kv_unit():
                w = slot(2)
                b = 2 * ((st["u"] - 1) % 2)
                e.wait_ge(act.sem, act.value(3))
                for k in range(2):
                    mm = e.matmul(ps[:, b, :], w[:, k, 0:NOPE], cT6[:, 3 + k, :], start=(k == 0), stop=(k == 1))
                inc(mm, "chunk_done")
                act.add()
                e.wait_ge(act.sem, act.value(3))
                for t in range(TT):
                    for k in range(2):
                        mm = e.matmul(ps[:, b + 1, t * P:(t + 1) * P], cT6[:, 3 + k, t * P:(t + 1) * P],
                                      w[:, k, NOPE:NOPE + VDIM], start=(k == 0), stop=(k == 1))
                inc(mm, "chunk_done")
                act.add()

            pairs_of(MLA_H, kv_unit, act)
            settle()
            for r in range(5):
                if r >= 4:
                    need("rope_read", r - 3)
                mm = e.matmul(ps[:, 4 + r % 4, :], rotm[:], cT6[:, 5, :] if r == 4 else qr[:, r, :],
                              start=True, stop=True)
                inc(mm, "rot_done")
            need("rope_ready", 5)
            settle()
            ITEMS = MLA_H * TT

            def scores(i):
                h, t = divmod(i, TT)
                if i >= 4:
                    need("att_p", i - 3)
                n = (t + 1) * P
                r0 = 64 * (h % 2)
                e.matmul(sbank(i, n), qn[:, h, t * P:(t + 1) * P], kn[:, h, 0:n], start=True, stop=False)
                mm = e.matmul(sbank(i, n), qr[r0:r0 + 64, h // 2, t * P:(t + 1) * P],
                              cT6[r0:r0 + 64, 5, 0:n], start=False, stop=True)
                inc(mm, "att_s")

            def turn(i):
                h, t = divmod(i, TT)
                need("att_n", i + 1)
                if i >= 2:
                    need("att_pt", i - 1)
                for q in range(t + 1):
                    mm = e.transpose(ps[:, 2 + i % 2, q * P:(q + 1) * P], pp[:, i % 4, q * P:(q + 1) * P], ident[:])
                inc(mm, "att_t")

            def head_out(h):
                need("att_pt", TT * (h + 1))
                if h >= 2:
                    need("att_oe", h - 1)
                for q in range(TT):
                    mm = e.matmul(ps[:, 6 + h % 2, q * P:T], vt[:, q, h * VDIM:(h + 1) * VDIM],
                                  pTt[:, q, q * P:T], start=(q == 0), stop=(q == TT - 1))
                inc(mm, "att_o")

            for i in range(3):
                scores(i)
            for i in range(ITEMS):
                if i + 3 < ITEMS:
                    scores(i + 3)
                turn(i)
                if i and i % TT == 0:
                    head_out(i // TT - 1)
            head_out(MLA_H - 1)
            need("att_oe", MLA_H)
            ada(3, 0)
            need("mod_ready", 4)
            linear(4, DC, nrhs, dve)
            ffn(1)
            squares(DC, 4)
            need("norm_full", 9)
            for t in range(TT):
                for half in range(2):
                    i = 2 * t + half
                    if i >= 3:
                        need("fin_ready", i - 2)
                    for k in range(4):
                        mm = e.transpose(ps[:, 5 + i % 3, k * P:(k + 1) * P], nT[:, half * 4 + k, t * P:(t + 1) * P],
                                         ident[:])
                    inc(mm, "fin_t")

        @block.gpsimd
        def _(e):
            k = Count(S["pl_ch"])

            def chain(ins):
                ins.then_inc(k.sem, 1)
                k.add()
                e.wait_ge(k.sem, k.value())

            chain(e.memset(ident[:], 0.0))
            chain(e.affine_select(out=ident[:], in_=ident[:], compare_op=ALU.not_equal, fill=1.0, base=0,
                                  pattern=[[-1, P]], channel_multiplier=1))
            chain(e.memset(ones[:], 1.0))
            chain(e.memset(bdiag[:], 0.0))
            for q in range(2):
                chain(e.memset(bdiag[64 * q:64 * q + 64, 64 * q:64 * q + 64], 1.0 / 64))
            chain(e.memset(rotm[:], 0.0))
            pairs = rotm[:].rearrange("p (i two) -> p i two", two=2)
            chain(e.affine_select(out=pairs[:, :, 0], in_=pairs[:, :, 0], compare_op=ALU.not_equal, fill=-1.0,
                                  base=-1, pattern=[[-2, 64]], channel_multiplier=1))
            chain(e.affine_select(out=pairs[:, :, 1], in_=pairs[:, :, 1], compare_op=ALU.not_equal, fill=1.0,
                                  base=0, pattern=[[-2, 64]], channel_multiplier=1))
            chain(e.memset(padA[:, :, 0:TAPS_A - 1], 0.0))
            chain(e.memset(padB[:, :, 0:TAPS_B - 1], 0.0))
            e.memset(par_rows[:], 0.0).then_inc(S["consts"], 1)
            ach = Count(S["ada_ch"])
            alanded = [Count(x) for x in ada_landed]

            def ada(part):
                W = IN["ada_w_2"][part // 2]

                def fetch(unit_, p):
                    e.dma_start(aslot[:, p, :, :],
                                W[:, bass.ds(unit_ * UNIT + (part % 2) * 3 * D, UNIT)].rearrange("(k p) n -> p k n", p=P)
                                ).then_inc(ada_landed[p], 16)

                def product(unit_, p):
                    def stage(ins):
                        ins.then_inc(ach.sem, 1)
                        ach.add()
                        e.wait_ge(ach.sem, ach.value())

                    alanded[p].add(16)
                    e.wait_ge(alanded[p].sem, alanded[p].value())
                    w = aslot[:, p, :, :]
                    stage(e.tensor_tensor(w, w, cT[:, :].rearrange("p (k n) -> p k n", n=1).to_broadcast([P, DC, UNIT]),
                                          ALU.mult))
                    for half in (4, 2):
                        stage(e.tensor_tensor(w[:, 0:half, :], w[:, 0:half, :], w[:, half:2 * half, :], ALU.add))
                    stage(e.tensor_tensor(asum[:, bass.ds(unit_ * UNIT, UNIT)], w[:, 0, :], w[:, 1, :], ALU.add))

                fetch(0, 0)
                fetch(1, 1)
                with loop(e, 5, [(ach, 8), (alanded[0], 16), (alanded[1], 16)]) as i:
                    for p in range(2):
                        product(i * 2 + p, p)
                        fetch(i * 2 + (2 + p), p)
                for p in range(2):
                    product(10 + p, p)
                e.sem_inc(S["ada_done"], 1)

            e.wait_ge(S["cT_ready"], 1)
            ada(0)

            e.wait_ge(S["sc_done"], 4 * TT)
            chain(e.iota(iota16, [[1, TOPK]], base=0, channel_multiplier=0, allow_small_or_imprecise_dtypes=True))
            e.memset(small[:, 0:1], 0.0).then_inc(S["consts"], 1)
            copied = Count(S["idx_copied"])
            landed = [Count(s) for s in row_landed]
            ready = Count(S["idx_ready"])
            us, vs = Count(S["u_used"]), Count(S["v_used"], RING)
            expert_u, expert_v = IN["expert_u"][0], IN["expert_v"][0]

            def gather(g, tables, parts):
                for dst, src in parts:
                    e.tensor_copy(dst, src).then_inc(copied.sem, 1)
                    copied.add()
                e.wait_ge(copied.sem, copied.value())
                e.sem_inc(S["pool_step"], 1)
                for s, table in zip(range(g, g + 4), tables):
                    e.indirect_dma_start(ring[:, s, :], None, table,
                                         bass.IndirectOffsetOnAxis(ap=cur[:, s:s + 1], axis=0)
                                         ).then_inc(landed[s].sem, 16)

            def after_mixed(g):
                e.wait_ge(us.sem, us.value(8 - (g // 2 + 2)))
                e.wait_ge(vs.sem, vs.value(8 - (g // 2 + 2)))

            with loop(e, TT, [(copied, 4 + 7 * 16 + 4), (us, PER_BLOCK), (vs, PER_BLOCK), (ready, HEADS)]) as b:
                ready.add()
                e.wait_ge(ready.sem, ready.value())
                for g in range(0, RING, 4):
                    e.wait_ge(vs.sem, vs.value(RING - (g + 4)))
                    gather(g, [expert_u] * 4, [(cur[:, g:g + 4], idx_flat[:, bass.ds(b * PER_BLOCK + g, 4)])])
                us.add(RING)
                with loop(e, HEADS - 1, [(copied, 16), (us, RING), (vs, RING), (ready, 1)]) as h:
                    ready.add()
                    e.wait_ge(ready.sem, ready.value())
                    for half in range(2):
                        for g in range(0, RING, 4):
                            after_mixed(g)
                            v0 = b * PER_BLOCK + h * TOPK + (half * 8 + g // 2)
                            gather(g, [expert_u, expert_v] * 2,
                                   [(cur[:, g:g + 4:2], idx_flat[:, bass.ds(v0 + TOPK, 2)]),
                                    (cur[:, g + 1:g + 4:2], idx_flat[:, bass.ds(v0, 2)])])
                        us.add(RING // 2)
                        vs.add(RING // 2)
                for g in range(0, RING, 4):
                    after_mixed(g)
                    gather(g, [expert_v] * 4,
                           [(cur[:, g:g + 4], idx_flat[:, bass.ds(b * PER_BLOCK + ((HEADS - 1) * TOPK + g), 4)])])
                vs.add(RING)
            e.wait_ge(S["h_ready"], 2)
            ada(1)
            e.wait_ge(S["norm_full"], 5)
            chain(e.memset(keep, 1.0))
            chain(e.affine_select(out=keep, in_=keep, compare_op=ALU.is_ge, fill=0.0, base=0,
                                  pattern=[[1, P]], channel_multiplier=-1))
            chain(e.memset(reset, 1.0))
            for t in range(TT):
                chain(e.memset(reset[:, t * P:t * P + 1], 0.0))
            e.memset(kd, 0.0).then_inc(S["consts"], 1)
            e.wait_ge(S["ada_cols"], 2)
            ada(2)

            def split(u, kc, landed_, w_split):
                q = u % 2
                landed_[q].add(16)
                e.wait_ge(landed_[q].sem, landed_[q].value())
                e.sem_inc(S["pool_step"], 1)
                n = kc * UNIT
                e.tensor_scalar(whi[:, q, 0:n], wring[:, q, 0:n], 1.0, 0.0, ALU.mult, ALU.add
                                ).then_inc(w_split.sem, 1)
                w_split.add()
                e.wait_ge(w_split.sem, w_split.value())
                e.sem_inc(S["pool_step"], 1)
                e.tensor_tensor(wlo[:, q, 0:n], wring[:, q, 0:n], whi[:, q, 0:n].bitcast(F32), ALU.subtract
                                ).then_inc(S["w_lo"], 1)

            w_split = Count(S["w_hi"])

            def split_ffn(layer):
                u, at = marks[f"ffn{layer}"]
                landed_ = [Count(x, n) for x, n in zip(w_landed, at)]
                e.wait_ge(S["h_ready"], (5, 7)[layer])
                for trips, kc in ((FH, DC), (4, FH)):
                    with loop(e, trips, [(w_split, 2), (landed_[0], 16), (landed_[1], 16)]):
                        for p in range(2):
                            split(u + p, kc, landed_, w_split)

            split_ffn(0)
            e.wait_ge(S["h_ready"], 6)
            chain(e.memset(cmask, 0.0))
            e.affine_select(out=cmask, in_=cmask, compare_op=ALU.is_ge, fill=MASKED, base=0,
                            pattern=[[-1, P]], channel_multiplier=1).then_inc(S["consts"], 1)
            ada(3)
            split_ffn(1)

        @block.scalar
        def _(e):
            c = {n: Count(s) for n, s in S.items()}
            done, evacs = c["chunk_done"], Count(S["act_evac"], 4)
            st = {"u": 0}

            def need(name, n):
                c[name].at = max(c[name].at, n)
                e.wait_ge(S[name], n)

            def inc(ins, name):
                ins.then_inc(S[name], 1)
                c[name].add()

            def own(ins, name):
                inc(ins, name)
                e.wait_ge(S[name], c[name].value())

            def squares(aps):
                for k, ap in enumerate(aps):
                    inc(e.activation(work[:, k, :], ap, ACT.Square), "sq_ready")

            def root(dst, src):
                c["var_ready"].at += 1
                e.wait_ge(S["var_ready"], c["var_ready"].at)
                inc(e.activation(dst, src, ACT.Sqrt), "std_ready")

            def hchunks():
                return [hT[:, k, :] for k in range(DC)]

            def units(n, evac, first=0):
                def one(base):
                    b = 2 * (st["u"] % 2)
                    st["u"] += 1
                    for j in range(2):
                        done.add()
                        e.wait_ge(done.sem, done.value())
                        evac(ps[:, b + j, :], base + j).then_inc(evacs.sem, 1)
                        evacs.add()
                if n // 2 > 1:
                    u0 = st["u"]
                    with loop(e, n // 2, [(done, 4), (evacs, 4)]) as i:
                        one(i * 4 + first)
                        one(i * 4 + (first + 2))
                    st["u"] = u0 + 2 * (n // 2)
                else:
                    for q in range(2 * (n // 2)):
                        one(first + 2 * q)
                if n % 2:
                    one(first + 2 * (n - 1))

            def copy_to(dst, scale=1.0, func=ACT.Copy):
                def evac(src, m):
                    where = dst[:, m, :] if isinstance(m, int) else dst[:, bass.ds(m, 1), :].rearrange("p a k -> p (a k)")
                    return e.activation(where, src, func, scale=scale)
                return evac

            def skip(n):
                done.add(2 * n)
                st["u"] += n

            e.sem_inc(S["act_evac"], 4)
            for k in range(DC):
                need("xtok_t", k + 1)
                inc(e.activation(hT[:, k, :], ps[:, 4 + k % 4, :], ACT.Copy), "hT_in")
            need("hT_in", DC)
            squares(hchunks())
            root(std, var)
            need("params_c", 1)
            own(e.activation(cT[:], col("c_2", 0, DC), ACT.Silu), "cT_ready")
            copy = copy_to(z)
            gate = copy_to(z, func=ACT.Sigmoid)
            units(3, lambda src, m: (copy if m < 3 else gate)(src, m))
            units(6, copy_to(z), first=6)

            def head_norm(src, dst, g, b, func):
                for k in range(3):
                    need("gl_cen", c["gl_cen"].at + 1)
                    inc(e.activation(work[:, k, :], src[:, k, :], ACT.Square), "sq_ready")
                need("gl_veps", c["gl_veps"].at + 1)
                inc(e.activation(gvar, gvar, ACT.Sqrt), "gl_std")
                need("mix_scaled", c["mix_scaled"].at + 1)
                for k in range(3):
                    ins = e.activation(dst[:, k, :], src[:, k, :], func, scale=col(g, k), bias=col(b, k))
                inc(ins, "gl_norm")

            head_norm(cvA, mixT, "ln_a_g", "ln_a_b", ACT.Silu)
            head_norm(z[:, 15:18, :], z[:, 15:18, :], "ln_c_g", "ln_c_b", ACT.Identity)
            for t in range(TT):
                need("vt_t", t + 1)
                inc(e.activation(vtok[:, t, :], ps[:, 5 + t % 3, 0:MIX_C], ACT.Copy), "vt_ready")
            skip(4)
            need("h_ready", 1)
            squares(hchunks())
            root(std, var)
            for i in range(2 * TT):
                need("ntok_t", i + 1)
                inc(e.activation(ntok[:, i // 2, (i % 2) * 512:(i % 2 + 1) * 512], ps[:, 5 + i % 2, :], ACT.Copy),
                    "ntok_ready")
            units(8, copy_to(qT))
            for q in range(4):
                need("keys_t", q + 1)
                inc(e.activation(keysT[:, 4 * q:4 * q + 4, :].rearrange("p a k -> p (a k)"), ps[:, 4 + q, :], ACT.Copy),
                    "keysT_ready")
            for t in range(TT):
                for q in range(4):
                    need("sc_done", 4 * t + q + 1)
                    u = HEADS * t + 2 * q
                    inc(e.activation(score[:, u:u + 2, :].rearrange("p a k -> p (a k)"), ps[:, 4 * (t % 2) + q, :],
                                     ACT.Copy), "sc_ready")
            e.wait_ge(S["sc_ready"], c["sc_ready"].value())
            inc(e.activation(score[:, UNITS:UNITS + AHEAD, :], score[:, 0:AHEAD, :], ACT.Copy), "sc_ready")
            e.wait_ge(S["sc_ready"], c["sc_ready"].value())
            hsr, hst, cmx, gxp = c["hs_read"], c["hs_ready"], c["cand_max"], c["gexp"]
            used, xrd, gel = c["u_used"], c["x_ready"], c["gelu_ready"]
            cof, dgr, vus, axr = c["coef_ready"], c["diag_ready"], c["v_used"], c["acc_ready"]
            vus.at = RING
            e.sem_inc(S["v_used"], RING)

            def diagonals():
                cof.add()
                e.wait_ge(cof.sem, cof.value())
                for k in range(TOPK):
                    e.wait_ge(vus.sem, vus.value(TOPK - 1 - k))
                    e.activation(diag[:, k, :], ident[:], ACT.Copy, scale=coef[:, k:k + 1]).then_inc(dgr.sem, 1)
                    dgr.add()
                vus.add(TOPK)

            def head_scores(n):
                hst.add()
                if not (isinstance(n, int) and n == 0):
                    e.wait_ge(hsr.sem, hst.value(1))
                src = score[:, n, :] if isinstance(n, int) else score[:, bass.ds(n, 1), :].rearrange("p a k -> p (a k)")
                e.activation(hs.rearrange("p a k -> p (a k)"), src, ACT.Copy).then_inc(hst.sem, 1)

            def gate_exp():
                cmx.add()
                e.wait_ge(cmx.sem, cmx.value())
                e.activation(gcur, top_v[:, 2, :], ACT.Exp, bias=small[:, 1:2], accum_out=small[:, 2:3]).then_inc(gxp.sem, 1)
                gxp.add()

            def hidden():
                e.activation(gdots, dots, ACT.Gelu_apprx_tanh).then_inc(gel.sem, 1)
                gel.add()

            for n in range(AHEAD):
                head_scores(n)
                gate_exp()
            with loop(e, TT, [(hst, 8), (cmx, 8), (gxp, 8), (used, PER_BLOCK), (xrd, 1), (gel, 8), (cof, 8),
                              (dgr, PER_BLOCK), (vus, PER_BLOCK), (axr, 1)]) as b:
                e.wait_ge(S["hT_in"], 1)
                e.wait_ge(used.sem, used.value())
                e.activation(ps[:, 4:6, :].rearrange("p a k -> p (a k)"), ntok[:, bass.ds(b, 1), :].rearrange("p a k -> p (a k)"),
                             ACT.Copy).then_inc(xrd.sem, 1)
                xrd.add()
                head_scores(b * HEADS + AHEAD)
                used.add(TOPK)
                e.wait_ge(used.sem, used.value())
                hidden()
                gate_exp()
                diagonals()
                with loop(e, HEADS - 1, [(hst, 1), (cmx, 1), (gxp, 1), (used, TOPK), (gel, 1), (cof, 1), (dgr, TOPK),
                                         (vus, TOPK)]) as h:
                    head_scores(b * HEADS + h + (AHEAD + 1))
                    used.add(TOPK)
                    e.wait_ge(used.sem, used.value())
                    hidden()
                    gate_exp()
                    diagonals()
                e.wait_ge(vus.sem, vus.value())
                e.activation(acc_sb, ps[:, 6:8, :].rearrange("p a k -> p (a k)"), ACT.Copy).then_inc(axr.sem, 1)
                axr.add()
            need("pT_t", 1)
            inc(e.activation(pT, ps[:, 6:8, :], ACT.Copy), "pT_ready")
            units(4, copy_to(peT))
            need("h_ready", 2)
            squares(hchunks())
            root(std, var)
            units(4, copy_to(sgT, func=ACT.Sigmoid))
            need("h_ready", 3)
            squares(hchunks())
            root(std, var)
            need("h_ready", 4)
            squares(hchunks())
            root(std, var)

            need("glr_ready", 1)
            inc(e.activation(glrT[0:16, :], ps[0:16, 5, :], ACT.Copy), "glog_in")
            for h in range(GLA_H):
                need("glog_a", h + 1)
                own(e.activation(gtmp[:, h, :], ps[:, 4 + h, :], ACT.Abs, bias=col("gla_b_gate_2", h)), "a_ch")
            own(e.activation(gtmp2, gtmp, ACT.Exp, scale=-1.0), "a_ch")
            inc(e.activation(gtmp2, gtmp2, ACT.Ln, bias=1.0), "glog_l")
            q_or_k = (copy_to(gq, scale=GLA_DK ** -0.5), copy_to(gk))
            for q in range(2):
                for p in range(2):
                    for j in range(2):
                        done.add()
                        e.wait_ge(done.sem, done.value())
                        q_or_k[q](ps[:, 2 * (st["u"] % 2) + j, :], 2 * p + j).then_inc(evacs.sem, 1)
                        evacs.add()
                    st["u"] += 1
            need("dq_ready", 1)
            inc(e.activation(qsub, gtmp, ACT.Exp, scale=1.0 / 16), "dq_exp")
            for i in range(2):
                need("dk_ready", i + 1)
                n = 16 * (i + 1)
                inc(e.activation(kd_g(i % 2)[:, :, 0:n], kd_g(i % 2)[:, :, 0:n], ACT.Exp, scale=1.0 / 16), "dk_exp")
            with loop(e, 2, [(done, 4), (evacs, 4)]) as i:
                for p in range(2):
                    for j in range(2):
                        done.add()
                        e.wait_ge(done.sem, done.value())
                        e.activation(gvt[:, 2 * j:2 * j + 2, bass.ds(i * (2 * UNIT) + p * UNIT, UNIT)],
                                     ps[:, 2 * p + j, :].rearrange("p (a k) -> p a k", a=2), ACT.Copy
                                     ).then_inc(evacs.sem, 1)
                        evacs.add()
            st["u"] += 4
            for i in range(8):
                if i + 2 < 8:
                    need("dk_ready", i + 3)
                    n = 16 * (i + 3)
                    inc(e.activation(kd_g(i % 2)[:, :, 0:n], kd_g(i % 2)[:, :, 0:n], ACT.Exp, scale=1.0 / 16), "dk_exp")
                done.add()
                e.wait_ge(done.sem, done.value())
                e.activation(gr[:, i, :], ps[:, 2 * ((st["u"] + i // 2) % 2) + i % 2, :], ACT.Copy
                             ).then_inc(evacs.sem, 1)
                evacs.add()
            st["u"] += 4
            need("ew_ready", 1)
            own(e.activation(gtmp, gb, ACT.Exp, scale=1.0 / 16), "ew_exp")
            own(e.activation(elast, gsubs(gb)[:, :, P - 1], ACT.Exp, scale=1.0 / 16), "ew_exp")
            inc(e.activation(gtmp2, gtmp2, ACT.Exp, scale=1.0 / 16), "ew_exp")
            need("ada_done", 3)
            for h in range(GLA_H):
                need("kw_t", h + 1)
                inc(e.activation(kwt[:, 4 * h:4 * h + 4, :], ps[:, 4 + h, :].rearrange("p (a k) -> p a k", a=4), ACT.Copy),
                    "kw_tok")
            for i in range(16):
                t, h = divmod(i, GLA_H)
                need("o_done", i + 1)
                inc(e.activation(goT[:, 2 * h:2 * h + 2, t * P:(t + 1) * P],
                                 ps[:, 4 + i % 4, 0:2 * P].rearrange("p (a k) -> p a k", a=2), ACT.Copy), "o_evac")
                if i == 0:
                    e.wait_ge(evacs.sem, evacs.value())
                    inc(e.activation(gr[:, 0:4, :], gr[:, 0:4, :], ACT.Silu), "gr_ready")
                if i == 4:
                    inc(e.activation(gr[:, 4:8, :], gr[:, 4:8, :], ACT.Silu), "gr_ready")
            need("o_evac", 16)
            squares([goT[:, k, :] for k in range(DC)])
            root(gtmp2, gtmp)
            skip(4)

            def ffn(h):
                need("h_ready", h)
                squares(hchunks())
                root(std, var)
                dve = Count(S["dve_evac"], 4)
                dve.at = st["dve"]
                shift = 48 * (h // 7) + 24
                raw, hh, nsc = c["hid_raw"], c["hid_hi_ready"], c["norm_scaled"]
                for k in range(DC):
                    nsc.add()
                    e.wait_ge(nsc.sem, nsc.at)
                    inc(e.activation(n_hi[:, k, :], nT[:, k, :], ACT.Identity, bias=mod[:, shift + k:shift + k + 1]),
                        "nhi_ready")
                with loop(e, FH, [(done, 4), (evacs, 2), (dve, 2), (raw, 2), (hh, 2)]) as i:
                    for j in range(2):
                        done.add()
                        e.wait_ge(done.sem, done.value())
                        e.wait_ge(dve.sem, dve.value(1))
                        e.activation(gsil[:, j, :], ps[:, j, :], ACT.Silu).then_inc(evacs.sem, 1)
                        evacs.add()
                        dve.add()
                    done.add(2)
                    for j in range(2):
                        raw.add()
                        e.wait_ge(raw.sem, raw.value())
                        m = bass.ds(i * 2 + j, 1)
                        e.activation(hid_h[:, m, :].rearrange("p a k -> p (a k)"), hid[:, m, :].rearrange("p a k -> p (a k)"),
                                     ACT.Copy).then_inc(hh.sem, 1)
                        hh.add()
                done.add(16)
                st["dve"] = dve.at + 8

            st["dve"] = 4 + 8 + 8
            ffn(5)
            st["u"] += 22 + 8

            need("h_ready", 6)
            squares(hchunks())
            root(std, var)
            need("pos_in", 16)
            units(3, copy_to(cT6))
            e.wait_ge(evacs.sem, evacs.value())
            squares([cT6[:, k, :] for k in range(3)])
            root(std, var)
            squares([cT6[:, 3 + k, :] for k in range(2)])
            root(std, var)
            for m in range(4):
                for j in range(3):
                    done.add()
                    e.wait_ge(done.sem, done.value())
                    dst = qr[:, m, :] if j == 2 else qn[:, 2 * m + j, :]
                    e.activation(dst, ps[:, (3 * m + j) % 4, :], ACT.Copy).then_inc(evacs.sem, 1)
                    evacs.add()
            st["u"] += 4
            with loop(e, 4, [(done, 4), (evacs, 4)]) as i:
                for p in range(2):
                    b = 2 * ((st["u"] + p) % 2)
                    done.add()
                    e.wait_ge(done.sem, done.value())
                    e.activation(kn[:, bass.ds(i * 2 + p, 1), :].rearrange("p a k -> p (a k)"), ps[:, b, :], ACT.Copy
                                 ).then_inc(evacs.sem, 1)
                    evacs.add()
                    done.add()
                    e.wait_ge(done.sem, done.value())
                    e.activation(vt[:, :, bass.ds(i * 256 + p * VDIM, VDIM)],
                                 ps[:, b + 1, :].rearrange("p (a k) -> p a k", a=TT), ACT.Copy).then_inc(evacs.sem, 1)
                    evacs.add()
            st["u"] += 8
            need("angle_ready", 1)
            inc(e.activation(tri, rtmp, ACT.Sin), "trig_ready")

            SCALE = float(NOPE + ROPE) ** -0.5

            def evac_p(i):
                h, t = divmod(i, TT)
                need("att_t", i + 1)
                if t == 0 and h:
                    need("att_o", h)
                inc(e.activation(pTt[:, 0:t + 1, t * P:(t + 1) * P],
                                 ps[:, 2 + i % 2, 0:(t + 1) * P].rearrange("p (a k) -> p a k", k=P), ACT.Copy), "att_pt")

            def exp_p(i):
                n = (i % TT + 1) * P
                need("att_m", i + 1)
                if i >= 4:
                    need("att_t", i - 3)
                inc(e.activation(pp[:, i % 4, 0:n], sbank(i, n), ACT.Exp, scale=SCALE,
                                 bias=attsm[:, i % 4, 1:2], accum_out=attsm[:, i % 4, 2:3]), "att_p")

            exp_p(0)
            exp_p(1)
            for i in range(MLA_H * TT):
                if i + 2 < MLA_H * TT:
                    exp_p(i + 2)
                h, t = divmod(i, TT)
                evac_p(i)
                if t == 0 and h:
                    inc(e.activation(oT[:, h - 1, :], ps[:, 6 + (h - 1) % 2, :], ACT.Copy), "att_oe")
            need("att_o", MLA_H)
            inc(e.activation(oT[:, MLA_H - 1, :], ps[:, 6 + (MLA_H - 1) % 2, :], ACT.Copy), "att_oe")
            skip(4)
            st["dve"] += 8
            ffn(7)
            need("h_ready", 8)
            squares(hchunks())
            root(std, var)
            for i in range(2 * TT):
                need("fin_t", i + 1)
                inc(e.activation(o_tok[:, i // 2, (i % 2) * 512:(i % 2 + 1) * 512], ps[:, 5 + i % 3, :], ACT.Copy),
                    "fin_ready")

        @block.vector
        def _(e):
            c = {n: Count(s) for n, s in S.items()}
            done, evacs = c["chunk_done"], Count(S["dve_evac"], 4)
            st = {"u": 0}

            def need(name, n):
                c[name].at = max(c[name].at, n)
                e.wait_ge(S[name], n)

            def inc(ins, name):
                ins.then_inc(S[name], 1)
                c[name].add()

            def own(ins, name="v_ch"):
                inc(ins, name)
                e.wait_ge(S[name], c[name].value())

            def bcast(ap, shape):
                return ap.to_broadcast(shape)

            def variance(dst, src, dim):
                c["ms_ready"].at += 1
                e.wait_ge(S["ms_ready"], c["ms_ready"].at)
                inc(e.tensor_scalar(dst, src, 1.0 / dim, EPS, ALU.mult, ALU.add), "var_ready")

            def rroot(dst, src):
                c["std_ready"].at += 1
                e.wait_ge(S["std_ready"], c["std_ready"].at)
                own(e.reciprocal(dst, src))

            def rms(src, dst, gain, n, dim=D, shift=None, signal="norm_full"):
                variance(var, ps[:, 4, :], dim)
                rroot(rstd, std)
                for k in range(n):
                    ins = e.scalar_tensor_tensor(out=dst[:, k, :], in0=src[:, k, :], scalar=gain(k), in1=rstd,
                                                 op0=ALU.mult, op1=ALU.mult)
                    if shift is None and k == n - 1:
                        own(ins, signal)
                    else:
                        inc(ins, "v_ch" if shift is not None else "norm_chunk")
                if shift is not None:
                    base = c["v_ch"].at - n
                    for k in range(n):
                        e.wait_ge(S["v_ch"], base + k + 1)
                        ins = e.tensor_scalar(dst[:, k, :], dst[:, k, :], shift(k), None, ALU.add)
                        if k < n - 1:
                            inc(ins, "norm_chunk")
                        else:
                            own(ins, signal)

            def skip(n):
                done.add(2 * n)
                st["u"] += n

            def residual(units, gate=None):
                with loop(e, units // 2, [(done, 4), (evacs, 4)]) as i:
                    for p in range(2):
                        for j in range(2):
                            done.add()
                            e.wait_ge(done.sem, done.value())
                            m = i * 4 + (2 * p + j)
                            bank = ps[:, 2 * ((st["u"] + p) % 2) + j, :]
                            dst = hT[:, bass.ds(m, 1), :].rearrange("p a k -> p (a k)")
                            if gate is None:
                                ins = e.tensor_tensor(dst, bank, dst, ALU.add)
                            else:
                                ins = e.scalar_tensor_tensor(out=dst, in0=bank, scalar=mod[:, bass.ds(m + gate, 1)],
                                                             in1=dst, op0=ALU.mult, op1=ALU.add)
                            ins.then_inc(evacs.sem, 1)
                            evacs.add()
                st["u"] += units

            def h_done():
                e.wait_ge(evacs.sem, evacs.value())
                own(e.tensor_copy(row[:, 0, 0:1], hT[:, 0, 0:1]), "h_ready")

            e.sem_inc(S["dve_evac"], 4)
            need("hT_in", DC)
            need("params_t", 1)
            own(e.tensor_copy(par[:, :, :].rearrange("p a k -> p (a k)"), ps[:, 4, 0:3 * P]), "params_c")
            need("ws_t", 1)
            own(e.tensor_copy(wsT.rearrange("p a k -> p (a k)")[:, 0:4 * P], ps[:, 5, :]))
            own(e.tensor_copy(wsT.rearrange("p a k -> p (a k)")[:, 4 * P:6 * P], ps[:, 6, 0:2 * P]))
            own(e.memset(wsT[64:128, :, 0:64], 0.0), "ws_ready")
            rms(hT, nT, lambda k: col("g_mix", k), DC)

            e.wait_ge(S["act_evac"], 4 + 6)
            need("consts", 1)
            own(e.tensor_tensor(padA[:, :, TAPS_A - 1:], z[:, 0:3, :], z[:, 3:6, :], ALU.mult))
            for k in range(3):
                inc(e.tensor_scalar(cvA[:, k, :], padA[:, k, 0:T], col("conv_a_w", k), col("conv_a_b", k),
                                    ALU.mult, ALU.add), "v_ch")
            for tap in range(1, TAPS_A):
                for k in range(3):
                    e.wait_ge(S["v_ch"], c["v_ch"].value(2))
                    inc(e.scalar_tensor_tensor(out=cvA[:, k, :], in0=padA[:, k, tap:tap + T],
                                               scalar=col("conv_a_w", 3 * tap + k), in1=cvA[:, k, :],
                                               op0=ALU.mult, op1=ALU.add), "v_ch")
            e.wait_ge(S["v_ch"], c["v_ch"].value())
            own(e.tensor_copy(row[:, 0, 0:1], cvA[:, 0, 0:1]), "gl_src")

            def head_center(src):
                c["gl_mean"].at += 1
                e.wait_ge(S["gl_mean"], c["gl_mean"].at)
                for k in range(3):
                    own(e.tensor_tensor(src[:, k, :], src[:, k, :], ps[:, 5 + k, :], ALU.subtract), "gl_cen")

            def head_scale(src):
                c["gl_var"].at += 1
                e.wait_ge(S["gl_var"], c["gl_var"].at)
                own(e.tensor_scalar(gvar, ps[:, 5:8, :], EPS, None, ALU.add), "gl_veps")
                c["gl_std"].at += 1
                e.wait_ge(S["gl_std"], c["gl_std"].at)
                own(e.reciprocal(gvar, gvar))
                own(e.tensor_tensor(src, src, gvar, ALU.mult), "mix_scaled")

            def short_conv():
                own(e.tensor_tensor(padB[:, :, TAPS_B - 1:], z[:, 8:10, :], z[:, 10:12, :], ALU.mult))
                yb = mixT[:, 3:5, :]
                for k in range(2):
                    own(e.tensor_scalar(yb[:, k, :], padB[:, k, 0:T], col("conv_b_w", k), None, ALU.mult))
                    for tap in range(1, TAPS_B):
                        own(e.scalar_tensor_tensor(out=yb[:, k, :], in0=padB[:, k, tap:tap + T],
                                                   scalar=col("conv_b_w", 2 * tap + k), in1=yb[:, k, :],
                                                   op0=ALU.mult, op1=ALU.add))
                own(e.tensor_tensor(yb, yb, z[:, 6:8, :], ALU.mult))

            head_center(cvA)
            e.wait_ge(S["act_evac"], 4 + 18)
            head_scale(cvA)
            own(e.tensor_copy(row[:, 0, 0:1], z[:, 15, 0:1]), "gl_src")
            head_center(z[:, 15:18, :])
            short_conv()
            head_scale(z[:, 15:18, :])
            skip(9)
            need("bs_in", 96)
            for k in range(3):
                need("mix_ready", k + 1)
                for q in range(2):
                    rows_ = slice(64 * q, 64 * q + 64)
                    own(e.tensor_tensor(work[rows_, 3, :].rearrange("p (b i) -> p b i", b=TT),
                                        ps[rows_, 5 + q, :].rearrange("p (b i) -> p b i", b=TT),
                                        bsb[rows_, k:k + 1, :].to_broadcast([64, TT, P]), ALU.add))
                own(e.tensor_tensor(mixT[:, 5 + k, :], work[:, 3, :], z[:, 12 + k, :], ALU.mult), "sg_done")

            def modulation(part):
                need("ada_cols", part + 1)
                m = mod[:, 24 * part:24 * part + 24]
                own(e.tensor_tensor(m, ps[:, 0, 0:24], col("ada_b_2", 24 * part, 24), ALU.add), "mod_ready")
                gain = col(("norm_mix_2", "norm_ffn_2")[part % 2], 8 * (part // 2), 8)
                own(e.scalar_tensor_tensor(out=gmod[:, part, :], in0=m[:, 8:16], scalar=1.0, in1=gain,
                                           op0=ALU.add, op1=ALU.mult))

            modulation(0)
            residual(4)
            h_done()

            rms(hT, nT, lambda k: col("g_ffn", k), DC)
            skip(8)
            need("sc_ready", 4 * TT + 1)
            need("consts", 2)
            used = c["u_used"]
            landed = [Count(s) for s in row_landed]
            hst, gxp = c["hs_ready"], c["gexp"]
            vch, mk, rdy = c["v_ch"], c["hs_read"], c["idx_ready"]
            cmx, gel, xrd, gat = c["cand_max"], c["gelu_ready"], c["x_ready"], c["gates_ready"]

            def signal(ins, count):
                ins.then_inc(count.sem, 1)
                count.add()
                e.wait_ge(count.sem, count.value())
                e.sem_inc(S["vector_step"], 1)

            def chain(ins):
                signal(ins, vch)

            def top16(values, a):
                chain(e.max(top_v[:, a, 0:8], values))
                chain(e.max_index(top_i[:, a, 0:8], top_v[:, a, 0:8], values))
                chain(e.match_replace(values, top_v[:, a, 0:8], values, -3e38))
                chain(e.max(top_v[:, a, 8:16], values))

            def topk(n):
                hst.add()
                e.wait_ge(hst.sem, hst.value())
                e.sem_inc(S["vector_step"], 1)
                for a in range(2):
                    top16(hs[:, a, :], a)
                    ins = e.max_index(top_i[:, a, 8:16], top_v[:, a, 8:16], hs[:, a, :])
                    if a == 0:
                        chain(ins)
                    else:
                        signal(ins, mk)
                chain(e.tensor_tensor(cand, top_v[:, 0, :].rearrange("p (a b) -> p a b", b=1).to_broadcast([P, TOPK, TOPK]),
                                      top_v[:, 1:2, :].to_broadcast([P, TOPK, TOPK]), ALU.add))
                flat = cand.rearrange("p a b -> p (a b)")
                top16(flat, 2)
                chain(e.max_index(top_i[:, 2, 8:16], top_v[:, 2, 8:16], flat))
                signal(e.tensor_scalar(small[:, 1:2], top_v[:, 2, 0:1], -1.0, None, ALU.mult), cmx)
                chain(e.tensor_scalar(pick_i[:, 0, :], top_i[:, 2, :], 4, None, ALU.logical_shift_right))
                chain(e.tensor_scalar(pick_i[:, 1, :], top_i[:, 2, :], TOPK - 1, None, ALU.bitwise_and))
                chain(e.tensor_copy(pick_f, pick_i))
                chain(e.tensor_copy(top_f, top_i[:, 0:2, :]))
                for a in range(2):
                    chain(e.tensor_tensor(onehot, pick_f[:, a, :].rearrange("p (a b) -> p a b", b=1).to_broadcast([P, TOPK, TOPK]),
                                          iota16.rearrange("p (a b) -> p a b", a=1).to_broadcast([P, TOPK, TOPK]),
                                          ALU.is_equal))
                    chain(e.tensor_tensor(onehot, onehot, top_f[:, a:a + 1, :].to_broadcast([P, TOPK, TOPK]), ALU.mult))
                    chain(e.tensor_reduce(ek[:, a, :], onehot, AX.X, ALU.add))
                where = bass.ds(n * TOPK, TOPK)
                signal(e.scalar_tensor_tensor(out=idx_flat[:, where], in0=ek[:, 0, :], scalar=float(KEYS), in1=ek[:, 1, :],
                                              op0=ALU.mult, op1=ALU.add), rdy)
                gxp.add()
                e.wait_ge(gxp.sem, gxp.value())
                chain(e.reciprocal(small[:, 3:4], small[:, 2:3]))
                chain(e.tensor_scalar(gates.rearrange("p n k -> p (n k)")[:, where], gcur, small[:, 3:4], None, ALU.mult))

            def u_row(s, k):
                landed[s].add(16)
                e.wait_ge(used.sem, used.value())
                e.wait_ge(landed[s].sem, landed[s].value())
                e.tensor_tensor_reduce(junk, ring[:, s, :], ps[:, 4:6, :].rearrange("p a k -> p (a k)"), 1.0, 0.0,
                                       ALU.mult, ALU.add, dots[:, k:k + 1]).then_inc(used.sem, 1)
                used.add()

            def coefs(n):
                gel.add()
                e.wait_ge(gel.sem, gel.value())
                e.wait_ge(dgr.sem, dgr.value())
                dgr.add(TOPK)
                signal(e.tensor_tensor(coef, gdots, gates.rearrange("p n k -> p (n k)")[:, bass.ds(n * TOPK, TOPK)],
                                       ALU.mult), c["coef_ready"])

            dgr = c["diag_ready"]
            own(e.memset(zero, 0.0), "consts_v")
            v0 = vch.at
            topk(0)
            steps = vch.at - v0
            topk(1)
            with loop(e, TT, [(hst, 8), (gxp, 8), (mk, 8), (rdy, 8), (cmx, 8), (gel, 8), (xrd, 1), (used, PER_BLOCK),
                              (vch, 8 * steps), (dgr, PER_BLOCK), (c["coef_ready"], 8), (c["acc_t"], 1),
                              (c["acc_added"], 1)] + [(l, 256) for l in landed]) as b:
                xrd.add()
                e.wait_ge(xrd.sem, xrd.value())
                for s in range(RING):
                    u_row(s, s)
                topk(b * HEADS + AHEAD)
                coefs(b * HEADS)
                with loop(e, HEADS - 1, [(hst, 1), (gxp, 1), (mk, 1), (rdy, 1), (cmx, 1), (gel, 1), (used, TOPK),
                                         (vch, steps), (dgr, TOPK), (c["coef_ready"], 1)]
                          + [(l, 32) for l in landed]) as h:
                    for half in range(2):
                        for q in range(8):
                            u_row(2 * q, half * 8 + q)
                            landed[2 * q + 1].add(16)
                    topk(b * HEADS + h + (AHEAD + 1))
                    coefs(b * HEADS + h + 1)
                for l in landed:
                    l.add(16)
                c["acc_t"].add()
                e.wait_ge(c["acc_t"].sem, c["acc_t"].value())
                dst = hT[:, :, bass.ds(b * P, P)]
                signal(e.tensor_tensor(dst, ps[:, 2:4, :].rearrange("p a (c k) -> p (a c) k", k=P), dst, ALU.add),
                       c["acc_added"])
            own(e.tensor_copy(row[:, 0, 0:1], hT[:, 0, 0:1]), "h_ready")
            rms(hT, nT, lambda k: col("g_ple", k), DC)
            done.add(8)
            for k in range(DC):
                e.wait_ge(S["act_evac"], 4 + 18 + 16 + 8 + k + 1)
                own(e.tensor_tensor(sgT[:, k, :], sgT[:, k, :], peT[:, k, :], ALU.mult))
                ins = e.tensor_tensor(hT[:, k, :], hT[:, k, :], sgT[:, k, :], ALU.add)
                own(ins, "h_ready" if k == DC - 1 else "v_ch")
            done.add(8)
            rms(hT, hT, lambda k: col("g_final", k), DC)
            own(e.tensor_copy(row[:, 0, 0:1], hT[:, 0, 0:1]), "h_ready")

            def modulated(layer, k):
                rms(hT, nT, lambda m: gmod[:, 2 * layer + k, m:m + 1], DC,
                    shift=lambda m: mod[:, 48 * layer + 24 * k + m:48 * layer + 24 * k + m + 1])

            modulated(0, 0)
            for h in range(GLA_H):
                need("a_ch", h + 1)
                own(e.tensor_scalar(gb[:, h, :], ps[:, 4 + h, :], col("gla_b_gate_2", h), 0.0, ALU.add, ALU.min), "glog_v")
            modulation(1)
            need("glog_l", 1)
            need("consts", 3)
            own(e.tensor_tensor(gtmp, gb, gtmp2, ALU.subtract))
            for h in range(GLA_H):
                own(e.tensor_tensor_scan(gb[:, h, :], reset, gtmp[:, h, :], 0.0, ALU.mult, ALU.add))
            runs = gb.rearrange("p h (i s) -> p (h i) s", s=GLA_SUB)
            own(e.tensor_tensor(gtmp.rearrange("p h (i s) -> p (h i) s", s=GLA_SUB), runs,
                                runs[:, :, 8:9].to_broadcast([P, 4 * T // GLA_SUB, GLA_SUB]), ALU.subtract), "dq_ready")
            gbg, gkg = gsubs(gb), gsubs(gk)

            def k_diff(i):
                n = 16 * (i + 1)
                if i >= 2:
                    need("amat_done", i - 1)
                own(e.tensor_tensor(kd_g(i % 2)[:, :, 0:n], gbg[:, :, 16 * i + 8:16 * i + 9].to_broadcast([P, GLA_G, n]),
                                    gbg[:, :, 0:n], ALU.subtract), "dk_ready")

            k_diff(0)
            k_diff(1)
            e.wait_ge(S["act_evac"], 4 + 50)
            need("dq_exp", 1)
            own(e.tensor_tensor(qsub, qsub, gq, ALU.mult), "q_sub")
            for i in range(8):
                n = 16 * (i + 1)
                need("dk_exp", i + 1)
                own(e.tensor_tensor(kd_g(i % 2)[:, :, 0:n], kd_g(i % 2)[:, :, 0:n], gkg[:, :, 0:n], ALU.mult), "k_sub")
                if i + 2 < 8:
                    k_diff(i + 2)
            skip(12)
            own(e.tensor_tensor(gsubs(gtmp2), gbg[:, :, P - 1:P].to_broadcast([P, GLA_G, P]), gbg, ALU.subtract), "ew_ready")
            need("ew_exp", 3)
            own(e.tensor_tensor(gq, gq, gtmp, ALU.mult), "ew_done")
            own(e.tensor_tensor(gtmp2, gtmp2, gk, ALU.mult), "kw_ready")
            need("amat_done", 8)
            for h in range(GLA_H):
                own(e.tensor_tensor(amat[:, 4 * h:4 * h + 4, :], ps[:, 4 + h, :].rearrange("p (a k) -> p a k", a=4),
                                    keep.rearrange("p (a k) -> p a k", a=1).to_broadcast([P, 4, P]), ALU.mult), "a_ready")
            for i in range(16):
                t, h = divmod(i, GLA_H)
                need("o_evac", i + 1)
                src = ps[:, 4 + i % 4, 2 * P:4 * P]
                if t == 0:
                    ins = e.tensor_copy(state[:, h, :], src)
                elif t < TT - 1:
                    ins = e.scalar_tensor_tensor(out=state[:, h, :], in0=state[:, h, :],
                                                 scalar=elast[:, h * TT + t:h * TT + t + 1], in1=src,
                                                 op0=ALU.mult, op1=ALU.add)
                else:
                    break
                own(ins, "s_new")
            modulation(2)
            variance(gtmp, ps[:, 4:8, :], GLA_DV)
            need("gr_ready", 2)
            for k in range(DC):
                inc(e.scalar_tensor_tensor(out=goT[:, k, :], in0=goT[:, k, :], scalar=col("gla_g_out_2", k % 2),
                                           in1=gr[:, k, :], op0=ALU.mult, op1=ALU.mult), "v_ch")
            for h in range(GLA_H):
                if h == 0:
                    c["std_ready"].at += 1
                    e.wait_ge(S["std_ready"], c["std_ready"].at)
                own(e.reciprocal(gtmp2[:, h, :], gtmp2[:, h, :]))
                e.wait_ge(S["v_ch"], c["v_ch"].at)
                for k in (2 * h, 2 * h + 1):
                    inc(e.tensor_tensor(goT[:, k, :], goT[:, k, :], gtmp2[:, h, :], ALU.mult), "go_chunk")
            residual(4, gate=16)
            h_done()

            def ffn(layer):
                variance(var, ps[:, 4, :], D)
                rroot(rstd, std)
                for k in range(DC):
                    inc(e.scalar_tensor_tensor(out=nT[:, k, :], in0=hT[:, k, :], scalar=gmod[:, 2 * layer + 1, k:k + 1],
                                               in1=rstd, op0=ALU.mult, op1=ALU.mult), "norm_scaled")
                need("norm_scaled", c["norm_scaled"].at)
                for k in range(DC):
                    need("nhi_ready", c["nhi_ready"].at + 1)
                    s_ = 48 * layer + 24 + k
                    inc(e.scalar_tensor_tensor(out=n_lo[:, k, :], in0=nT[:, k, :], scalar=mod[:, s_:s_ + 1],
                                               in1=n_hi[:, k, :].bitcast(F32), op0=ALU.add, op1=ALU.subtract), "nlo_ready")
                raw, hh = c["hid_raw"], c["hid_hi_ready"]
                act = Count(S["act_evac"], st["act"])
                with loop(e, FH, [(done, 4), (evacs, 2), (act, 2), (raw, 2), (hh, 2)]) as i:
                    done.add(2)
                    for j in range(2):
                        act.add()
                        e.wait_ge(act.sem, act.value())
                        done.add()
                        e.wait_ge(done.sem, done.value())
                        e.tensor_tensor(hid[:, bass.ds(i * 2 + j, 1), :].rearrange("p a k -> p (a k)"), ps[:, 2 + j, :],
                                        gsil[:, j, :], ALU.mult).then_inc(raw.sem, 1)
                        raw.add()
                        e.wait_ge(raw.sem, raw.value())
                        e.sem_inc(evacs.sem, 1)
                        evacs.add()
                    for j in range(2):
                        hh.add()
                        e.wait_ge(hh.sem, hh.value())
                        m = bass.ds(i * 2 + j, 1)
                        e.tensor_tensor(hid_l[:, m, :].rearrange("p a k -> p (a k)"), hid[:, m, :].rearrange("p a k -> p (a k)"),
                                        hid_h[:, m, :].bitcast(F32).rearrange("p a k -> p (a k)"), ALU.subtract
                                        ).then_inc(S["hid_ready"], 1)
                st["act"] = act.at
                with loop(e, 2, [(done, 8), (evacs, 4)]) as i:
                    for half in range(2):
                        done.add(2)
                        for j in range(2):
                            done.add()
                            e.wait_ge(done.sem, done.value())
                            m = i * 4 + (2 * half + j)
                            dst = hT[:, bass.ds(m, 1), :].rearrange("p a k -> p (a k)")
                            e.scalar_tensor_tensor(out=dst, in0=ps[:, 2 * half + j, :],
                                                   scalar=mod[:, bass.ds(m + (48 * layer + 40), 1)], in1=dst,
                                                   op0=ALU.mult, op1=ALU.add).then_inc(evacs.sem, 1)
                            evacs.add()
                st["u"] += 30
                h_done()

            st["act"] = 4 + 18 + 16 + 16 + 24
            ffn(0)

            modulated(1, 0)
            need("pos_in", 16)
            own(e.tensor_copy(ang, pos_i))
            own(e.tensor_scalar(ang, ang, col("inv_freq"), None, ALU.mult))
            for q, turn in ((0, 0.25), (1, 0.0)):
                n_, r_ = rtmp[:, q, :], tri[:, q, :]
                own(e.tensor_scalar(n_, ang, float(1 / (2 * np.pi)), turn, ALU.mult, ALU.add))
                own(e.tensor_scalar(n_, n_, ROUND, None, ALU.add))
                own(e.tensor_scalar(n_, n_, ROUND, None, ALU.subtract))
                own(e.scalar_tensor_tensor(out=r_, in0=n_, scalar=-PI2_A, in1=ang, op0=ALU.mult, op1=ALU.add))
                own(e.scalar_tensor_tensor(out=r_, in0=n_, scalar=-PI2_B, in1=r_, op0=ALU.mult, op1=ALU.add))
                own(e.scalar_tensor_tensor(out=r_, in0=n_, scalar=-PI2_C, in1=r_, op0=ALU.mult, op1=ALU.add))
                own(e.tensor_scalar(r_, r_, float(turn * 2 * np.pi), PI_IN, ALU.add, ALU.min))
                own(e.tensor_scalar(n_, r_, -PI_IN, None, ALU.max))
            own(e.tensor_copy(row[:, 1, 0:1], ang[:, 0:1]), "angle_ready")
            e.wait_ge(S["act_evac"], st["act"] + 6)
            rms(cT6, cT6, lambda k: col("mla_g_q_2", k), 3, dim=384)
            rms(cT6[:, 3:5, :], cT6[:, 3:5, :], lambda k: col("mla_g_kv_2", k), 2, dim=256)
            e.wait_ge(S["act_evac"], st["act"] + 6 + 12 + 16)
            st["act"] += 34
            need("trig_ready", 1)
            for r in range(5):
                x = cT6[:, 5, :] if r == 4 else qr[:, r, :]
                need("rot_done", r + 1)
                own(e.tensor_tensor(rtmp[:, 0, :], ps[:, 4 + r % 4, :], tri[:, 1, :], ALU.mult), "rope_read")
                own(e.tensor_tensor(x, x, tri[:, 0, :], ALU.mult))
                own(e.tensor_tensor(x, x, rtmp[:, 0, :], ALU.add), "rope_ready")
            need("consts", 4)
            SCALE = float(NOPE + ROPE) ** -0.5

            def peak(i):
                t = i % TT
                n = (t + 1) * P
                b = sbank(i, T)
                need("att_s", i + 1)
                own(e.tensor_tensor(b[:, t * P:n], b[:, t * P:n], cmask, ALU.add))
                own(e.tensor_reduce(attsm[:, i % 4, 0:1], b[:, 0:n], AX.X, ALU.max))
                own(e.tensor_scalar(attsm[:, i % 4, 1:2], attsm[:, i % 4, 0:1], -SCALE, None, ALU.mult), "att_m")

            peak(0)
            peak(1)
            for i in range(MLA_H * TT):
                if i + 2 < MLA_H * TT:
                    peak(i + 2)
                n = (i % TT + 1) * P
                need("att_p", i + 1)
                own(e.reciprocal(attsm[:, i % 4, 3:4], attsm[:, i % 4, 2:3]))
                own(e.tensor_scalar(pp[:, i % 4, 0:n], pp[:, i % 4, 0:n], attsm[:, i % 4, 3:4], None, ALU.mult), "att_n")
            skip(3 + 4 + 8)
            modulation(3)
            done.add(4)
            residual(4, gate=48 + 16)
            h_done()
            ffn(1)
            rms(hT, nT, lambda k: col("final_norm_2", k), DC)


_INS = ["x", "p", "g_mix", "w_in", "conv_a_w", "conv_a_b", "ln_a_g", "ln_a_b", "conv_b_w", "ln_c_g", "ln_c_b", "w_s",
        "b_s", "w_out", "g_ffn", "w_q", "sub_keys", "expert_u", "expert_v", "g_ple", "w_pe", "w_pg", "g_final",
        "c_2", "positions_2", "ada_w_2", "ada_b_2", "norm_mix_2", "norm_ffn_2", "gla_w_in_2", "gla_w_gate_2",
        "gla_b_gate_2", "gla_g_out_2", "gla_w_out_2", "mla_w_in_2", "mla_g_q_2", "mla_w_q_up_2", "mla_g_kv_2",
        "mla_w_kv_up_2", "mla_w_out_2", "ffn_w_in_2", "ffn_w_out_2", "final_norm_2"]


def kernel(**inputs):
    import numpy as _np
    import concourse.bacc as _bacc
    from concourse import mybir as _mybir
    from concourse.bass_utils import run_bass_kernel_spmd as _run

    nc = _bacc.Bacc("TRN2", target_bir_lowering=False, num_devices=1)
    given = {name: _np.ascontiguousarray(inputs[name]) for name in _INS}
    freq = _np.float32(10000.0) ** (-_np.arange(0, ROPE, 2, dtype=_np.float32) / _np.float32(ROPE))
    given["inv_freq"] = _np.tile(_np.repeat(freq, 2), 2).astype(_np.float32).reshape(1, P)
    arrays, args = {}, {}
    for name, a in given.items():
        arrays[f"in_{name}_dram"] = a
        args[name] = nc.dram_tensor(f"in_{name}_dram", a.shape, _mybir.dt.from_np(a.dtype), kind="ExternalInput").ap()
    out = nc.dram_tensor("out_0_dram", (1, T, D), F32, kind="ExternalOutput").ap()
    build(nc, args, out)
    r = _run(nc, [arrays], core_ids=[0])
    return r.results[0]["out_0_dram"]
```

```python
from contextlib import ExitStack, contextmanager

import concourse.bass as bass
import numpy as np
from concourse import mybir

ALU = mybir.AluOpType
ACT = mybir.ActivationFunctionType
F32 = mybir.dt.float32
U32 = mybir.dt.uint32
I32 = mybir.dt.int32
F32R = mybir.dt.float32r
AX = mybir.AxisListType
P = 128
EPS = 1e-6

T = 512
D = 1024
DC = D // P
TT = T // P
MIX_A, MIX_B, MIX_C = 384, 256, 384
TAPS_A, TAPS_B = 31, 3
HEADS, KEYS, TOPK = 8, 128, 16
UNITS = TT * HEADS
AHEAD = 2
RING = 16
GLA_H, GLA_DK, GLA_DV, GLA_SUB = 4, 128, 256, 16
GLA_G = GLA_H * TT
PER_BLOCK = HEADS * TOPK
MLA_H, NOPE, ROPE, VDIM = 8, 128, 64, 128
D_FF = 2816
FC = D_FF // P
FH = FC // 2
UNIT = 256
SLOT = FH * UNIT
ARENA = 32256
MASKED = -1e30
ROUND = 1.5 * 2.0 ** 23
PI2_A, PI2_B, PI2_C = 6.28125, 0.0019350051879882812, 3.0199159819567e-07
PI_IN = 3.1415925


class Count:

    def __init__(self, sem, start=0):
        self.sem, self.at, self.dyn = sem, start, None

    def value(self, back=0):
        n = self.at - back
        return n if self.dyn is None else self.dyn + n

    def add(self, n=1):
        self.at += n


@contextmanager
def loop(eng, trips, counts):
    starts = [c.at for c, _ in counts]
    outer = [c.dyn for c, _ in counts]
    with eng.Fori(0, trips) as i:
        for c, per in counts:
            c.dyn = i * per if c.dyn is None else c.dyn + i * per
        yield i
        for (c, per), s in zip(counts, starts):
            assert c.at - s == per, (c.sem, c.at - s, per)
    for (c, per), s, o in zip(counts, starts, outer):
        c.at, c.dyn = s + per * trips, o


SEMS = ("x_in params_in ws_in bs_in keys_in ptok_in pos_in xtok_t hT_in params_t params_c "
        "chunk_done act_evac dve_evac consts consts_v sq_ready ms_ready var_ready std_ready norm_full norm_scaled "
        "v_ch pool_step vector_step a_ch pl_ch gl_src gl_mean gl_cen gl_var gl_veps gl_std gl_norm mix_scaled mix_ready ws_t ws_ready vt_t vt_ready "
        "sg_done h_ready ntok_t ntok_ready keys_t keysT_ready sc_done sc_ready hs_ready hs_read cand_max gexp "
        "gates_ready idx_ready idx_copied u_used v_used diag_ready x_ready gelu_ready coef_ready acc_ready "
        "acc_t block_summed acc_added ada_done mod_ready cT_ready pT_t pT_ready "
        "glr_ready glog_in glog_a glog_v glog_l dq_ready dq_exp q_sub dk_ready dk_exp k_sub amat_done "
        "a_ready ew_ready ew_exp ew_done kw_ready kw_t kw_tok s_new o_done o_evac "
        "rot_done rope_read rope_ready angle_ready trig_ready att_s att_m att_p att_n att_t att_pt  att_o att_oh "
        "att_oe fin_t fin_ready out_done glr_in hid_ready ada_ch ada_cols gr_ready go_chunk norm_chunk nhi_ready nlo_ready w_hi w_lo hid_raw hid_hi_ready").split()


def build(nc, A, out):
    with ExitStack() as ctx:
        S = {n: ctx.enter_context(nc.semaphore(n)) for n in SEMS}
        w_landed = [ctx.enter_context(nc.semaphore(f"w_landed{i}")) for i in range(2)]
        ada_landed = [ctx.enter_context(nc.semaphore(f"ada_landed{i}")) for i in range(2)]
        row_landed = [ctx.enter_context(nc.semaphore(f"row_landed{i}")) for i in range(RING)]

        def sb(name, *shape, dt=F32):
            return ctx.enter_context(nc.sbuf_tensor(name, [P, *shape], dt))

        hT = sb("hT", DC, T)
        row = sb("row", 3, T)
        eps = sb("eps", 1)
        mark = sb("mark", 1)
        ident = sb("ident", P)
        ones = sb("ones", P)
        bdiag = sb("bdiag", P)
        rotm = sb("rotm", P)
        par_rows = sb("par_rows", 3, P)
        par = sb("par", 3, P)
        mod = sb("mod", 96)
        gmod = sb("gmod", 4, DC)
        cT = sb("cT", DC)
        def two_names(name, other, *shape):
            with nc.sbuf_tensor(name, [P, *shape], F32) as plain:
                pass
            return plain, sb(other, *shape, dt=F32R)

        nT, n_lo = two_names("nT", "n_lo", DC, T)
        work, n_hi = two_names("work", "n_hi", DC, T)
        wring, wlo = two_names("wring", "wlo", 2, SLOT)
        with nc.sbuf_tensor("arena", [P, ARENA], F32) as arena:
            pass

        def rounded(name, start, *shape):
            with ExitStack() as below:
                if start:
                    below.enter_context(nc.sbuf_tensor(f"{name}_below", [P, start], F32))
                return below.enter_context(nc.sbuf_tensor(name, [P, *shape], F32R))

        def rounded_pair(name, starts, words):
            return [rounded(f"{name}{i}", x, words) for i, x in enumerate(starts)]


        class Region:
            def __init__(self, start=0):
                self.at = start

            def take(self, *shape, dt=None):
                n = int(np.prod(shape))
                ap = arena[:, self.at:self.at + n]
                self.at += n
                assert self.at <= ARENA, self.at
                if dt is not None:
                    ap = ap.bitcast(dt)
                if len(shape) == 2:
                    ap = ap.rearrange("p (a b) -> p a b", a=shape[0])
                if len(shape) == 3:
                    ap = ap.rearrange("p (a b c) -> p a b c", a=shape[0], b=shape[1])
                return ap

        ps = ctx.enter_context(nc.psum_tensor("ps", [P, 8, 512], F32))

        vectors, at = {}, [0, 0, 0]

        def vec(name, ap, tile):
            n = ap.shape[0]
            vectors[name] = (ap, tile, at[tile], n)
            at[tile] += n

        def rows(ap):
            return ap.rearrange("(c p) -> c p", p=P)

        for name in ("g_mix", "conv_a_b", "ln_a_g", "ln_a_b", "ln_c_g", "ln_c_b", "g_ffn", "g_ple", "gla_b_gate_2",
                     "gla_g_out_2", "mla_g_q_2", "mla_g_kv_2", "c_2"):
            vec(name, rows(A[name][0, :]), 0)
        vec("g_final", rows(A["g_final"]), 0)
        vec("final_norm_2", rows(A["final_norm_2"]), 0)
        vec("norm_mix_2", A["norm_mix_2"].rearrange("l (c p) -> (l c) p", p=P), 0)
        vec("norm_ffn_2", A["norm_ffn_2"].rearrange("l (c p) -> (l c) p", p=P), 0)
        vec("ada_b_2", A["ada_b_2"].rearrange("l (c p) -> (l c) p", p=P), 1)
        vec("inv_freq", A["inv_freq"], 1)
        vec("conv_b_w", A["conv_b_w"][0].rearrange("k (c p) -> (k c) p", p=P), 1)
        vec("conv_a_w", A["conv_a_w"][0].rearrange("k (c p) -> (k c) p", p=P), 2)

        def col(name, k=0, n=1):
            _, tile, r0, _ = vectors[name]
            return par[:, tile, r0 + k:r0 + k + n]

        R = Region()
        z = R.take(18, T)
        padA = R.take(3, TAPS_A - 1 + T)
        padB = R.take(2, TAPS_B - 1 + T)
        cvA = R.take(3, T)
        gvar = R.take(3, T)
        ws_in = R.take(6, P)
        wsT = R.take(6, P)
        bsb = R.take(3, P)
        whi_in = rounded_pair("whi_in", (R.at, R.at + DC * UNIT), DC * UNIT)
        vtok = R.take(TT, MIX_C)
        mixT = R.take(DC, T)
        x_tok = nT[:, :, :].rearrange("p (t c) k -> p t (c k)", t=TT)

        R = Region()
        whi_q = rounded_pair("whi_q", (0, DC * UNIT), DC * UNIT)
        q_hi = rounded("q_hi", 2 * DC * UNIT, DC, T)
        score = R.take(UNITS + AHEAD, 2 * KEYS)
        ring = R.take(RING, D)
        R2 = Region((UNITS + AHEAD) * 2 * KEYS)
        qT = R2.take(2 * HEADS, T)
        keys_in = R2.take(2 * HEADS, P)
        keysT = R2.take(2 * HEADS, P)
        junk = R.take(D)
        acc_sb = R.take(D)
        hs = R.take(2, KEYS)
        cand = R.take(TOPK, TOPK)
        onehot = R.take(TOPK, TOPK)
        iota16 = R.take(TOPK)
        top_v = R.take(3, TOPK)
        top_i = R.take(3, TOPK, dt=U32)
        pick_i = R.take(2, TOPK, dt=U32)
        pick_f = R.take(2, TOPK)
        top_f = R.take(2, TOPK)
        ek = R.take(3, TOPK)
        gcur = R.take(TOPK)
        small = R.take(8)
        idx = R.take(UNITS + AHEAD, TOPK, dt=U32)
        idx_flat = idx.rearrange("p n k -> p (n k)")
        gates = R.take(UNITS + AHEAD, TOPK)
        cur = R.take(RING, dt=U32)
        dots = R.take(TOPK)
        gdots = R.take(TOPK)
        coef = R.take(TOPK)
        diag = nT[:, 0:4, :].rearrange("p a (b k) -> p (a b) k", k=P)
        zero = nT[:, 4, 0:P]
        ntok = work[:, :, :].rearrange("p (t c) k -> p t (c k)", t=TT)

        R = Region()
        p_tok = R.take(TT, UNIT)
        pT = R.take(2, T)
        peT = R.take(DC, T)
        sgT = R.take(DC, T)

        R = Region()
        gq = R.take(GLA_H, T)
        gk = R.take(GLA_H, T)
        gvt = R.take(TT, D)
        gr = R.take(DC, T)
        wglr = R.take(DC, 16)
        glrT = R.take(T)
        wgate = R.take(T)
        gb_at = R.at
        gb = R.take(GLA_H, T)
        gtmp = R.take(GLA_H, T)
        gtmp2 = R.take(GLA_H, T)
        whi_go = rounded_pair("whi_go", (gb_at, R.at), DC * UNIT)
        qsub = R.take(GLA_H, T)
        reset = R.take(T)
        keep = R.take(P)
        elast = R.take(GLA_G)
        amat = R.take(GLA_G, P)
        kwt = R.take(GLA_G, P)
        state = R.take(GLA_H, GLA_DV)
        kd = work[:, :, :].rearrange("p (a c) k -> p a (c k)", a=2)
        goT = nT

        R = Region()
        cT6 = R.take(6, T)
        qn = R.take(MLA_H, T)
        qr = R.take(MLA_H // 2, T)
        kn = R.take(MLA_H, T)
        vt = R.take(TT, D)
        ang = R.take(T)
        tri = R.take(2, T)
        rtmp = R.take(2, T)
        pos_i = R.take(T, dt=I32)
        pp = R.take(4, T)
        pTt = R.take(TT, T)
        cmask = R.take(P)
        attsm = R.take(4, 4)
        whi_m = rounded_pair("whi_m", (R.at, R.at + DC * UNIT), DC * UNIT)

        R = Region()
        hid = R.take(FC, T)
        hid_l = rounded("hid_l", 0, FC, T)
        gsil = R.take(2, T)
        whi_f = rounded_pair("whi_f", (R.at, R.at + SLOT), SLOT)
        hid_h = rounded("hid_h", R.at + 2 * SLOT, FC, T)

        R = Region(ARENA - 2 * DC * UNIT - 3 * D)
        aslot = R.take(2, DC, UNIT)
        asum = R.take(3 * D)

        R = Region()
        o_tok = R.take(TT, D)

        def gsubs(x):
            return x.rearrange("p h (t k) -> p (h t) k", k=P)

        def kd_g(a):
            return kd[:, a, :].rearrange("p (g k) -> p g k", g=GLA_G)

        marks = {}

        def sbank(i, n):
            return ps[:, (4, 5, 0, 1)[i % 4], 0:n]

        IN = {n: A[n] for n in A}
        w_in, w_out, w_q = IN["w_in"][0], IN["w_out"][0], IN["w_q"][0]
        gla_in = IN["gla_w_in_2"][0]
        mla_in = IN["mla_w_in_2"][0]

        block = ctx.enter_context(nc.Block())

        @block.sync
        def _(e):
            c = {n: Count(s) for n, s in S.items()}
            landed = [Count(s) for s in w_landed]
            done = c["chunk_done"]
            state_ = {"u": 0, "ends": []}

            def unit(W, col0, kc, k0=0, width=UNIT, chunks=2, back=None, extra=None):
                u = state_["u"]
                v = done.value(back) if back is not None else (
                    state_["ends"][-2] if len(state_["ends"]) >= 2 else None)
                if v is not None:
                    e.wait_ge(done.sem, v)
                dst = wring[:, u % 2, 0:kc * width].rearrange("p (k n) -> p k n", n=width)
                wide = width - (extra or 0)
                src = W[k0 * P:(k0 + kc) * P, bass.ds(col0, wide)].rearrange("(k p) n -> p k n", p=P)
                n = 16
                e.dma_start(dst[:, :, 0:wide], src).then_inc(landed[u % 2].sem, 16)
                if extra:
                    e.dma_start(dst[:, :, wide:width],
                                W[k0 * P:(k0 + kc) * P, bass.ds(col0 + wide - extra, extra)]
                                .rearrange("(k p) n -> p k n", p=P)).then_inc(landed[u % 2].sem, 16)
                done.add(chunks)
                state_["u"] += 1
                if back is None:
                    state_["ends"].append(done.at)

            def units(W, col0, n, kc):
                pairs = n // 2
                if pairs > 1:
                    with loop(e, pairs, [(done, 4)]) as i:
                        for j in range(2):
                            unit(W, i * (2 * UNIT) + (col0 + j * UNIT), kc, back=2)
                    state_["ends"] += [done.at - 2, done.at]
                else:
                    for j in range(2 * pairs):
                        unit(W, col0 + j * UNIT, kc)
                if n % 2:
                    unit(W, col0 + 2 * pairs * UNIT, kc)

            e.dma_start(x_tok, IN["x"][0].rearrange("(t p) d -> p t d", p=P)).then_inc(S["x_in"], 16)
            e.wait_ge(S["consts"], 1)
            for name, (ap, tile, r0, n) in vectors.items():
                e.dma_start(par_rows[r0:r0 + n, tile, :], ap).then_inc(S["params_in"], 16)
            e.dma_start(ws_in, IN["w_s"][0].rearrange("h i j -> i h j")).then_inc(S["ws_in"], 16)
            for h in range(6):
                e.dma_start(bsb[64 * (h % 2):64 * (h % 2) + 64, h // 2, :],
                            IN["b_s"][0, h:h + 1, :].to_broadcast([64, P])).then_inc(S["bs_in"], 16)
            units(w_in, 0, 3, DC)
            units(w_in, 2 * MIX_A, 6, DC)
            units(w_out, 0, 4, DC)
            units(w_q, 0, 8, DC)
            e.wait_ge(S["norm_full"], 2)
            e.dma_start(keys_in, IN["sub_keys"][0].rearrange("h s k d -> k (h s) d")).then_inc(S["keys_in"], 16)
            e.wait_ge(S["h_ready"], 2)
            e.dma_start(p_tok, IN["p"][0, 0].rearrange("(t p) d -> p t d", p=P)).then_inc(S["ptok_in"], 16)
            units(IN["w_pe"][0], 0, 4, 2)
            units(IN["w_pg"][0], 0, 4, DC)
            e.wait_ge(S["h_ready"], 4)
            e.dma_start(wglr, gla_in[:, 3072:3088].rearrange("(k p) n -> p k n", p=P)).then_inc(S["glr_in"], 16)
            e.dma_start(wgate[0:16, :], IN["gla_w_gate_2"][0]).then_inc(S["glr_in"], 16)
            units(gla_in, 0, 4, DC)
            units(gla_in, 1024, 4, DC)
            units(gla_in, 2048, 4, DC)
            units(IN["gla_w_out_2"][0], 0, 4, DC)

            def ffn(layer):
                W = IN["ffn_w_in_2"][layer]
                with loop(e, FH, [(done, 4)]) as i:
                    unit(W, i * UNIT, DC, back=2)
                    unit(W, i * UNIT + D_FF, DC, back=2)
                state_["ends"] += [done.at - 2, done.at]
                W = IN["ffn_w_out_2"][layer]
                with loop(e, 2, [(done, 8)]) as i:
                    for half in range(2):
                        for k in range(2):
                            unit(W, i * (2 * UNIT) + half * UNIT, FH, k0=k * FH, back=2)
                state_["ends"] += [done.at - 2, done.at]

            ffn(0)
            e.wait_ge(S["h_ready"], 6)
            e.dma_start(pos_i, IN["positions_2"][0:1, :].to_broadcast([P, T])).then_inc(S["pos_in"], 16)
            unit(mla_in, 0, DC)
            unit(mla_in, 256, DC)
            unit(mla_in, 512, DC, extra=ROPE)
            for m in range(4):
                u = state_["u"]
                e.wait_ge(done.sem, state_["ends"][-2])
                dst = wring[:, u % 2, 0:3 * 384].rearrange("p (k n) -> p k n", n=384)
                W = IN["mla_w_q_up_2"][0].rearrange("(k p) n -> p k n", p=P)
                for to, frm, n in ((0, 0, NOPE), (NOPE, 192, NOPE), (256, NOPE, ROPE), (320, 320, ROPE)):
                    e.dma_start(dst[:, :, to:to + n], W[:, :, 384 * m + frm:384 * m + frm + n]
                                ).then_inc(landed[u % 2].sem, 16)
                done.add(3)
                state_["u"] += 1
                state_["ends"].append(done.at)
            units(IN["mla_w_kv_up_2"][0], 0, 8, 2)
            units(IN["mla_w_out_2"][0], 0, 4, DC)
            ffn(1)
            e.wait_ge(S["fin_ready"], 2 * TT)
            e.dma_start(out[0].rearrange("(t p) d -> p t d", p=P), o_tok).then_inc(S["out_done"], 16)
            e.wait_ge(S["out_done"], 16)

        @block.tensor
        def _(e):
            c = {n: Count(s) for n, s in S.items()}
            landed = [Count(s) for s in w_landed]
            done, act, dve = c["chunk_done"], Count(S["act_evac"], 4), Count(S["dve_evac"], 4)
            st = {"u": 0}

            def need(name, n):
                c[name].at = max(c[name].at, n)
                e.wait_ge(S[name], n)

            def inc(ins, name, n=1):
                ins.then_inc(S[name], n)
                c[name].add(n)

            def settle():
                e.wait_ge(act.sem, act.value())
                e.wait_ge(dve.sem, dve.value())

            def slot(kc, width=UNIT, n=16):
                u = st["u"]
                st["u"] += 1
                landed[u % 2].add(n)
                e.wait_ge(landed[u % 2].sem, landed[u % 2].value())
                return wring[:, u % 2, 0:kc * width].rearrange("p (k n) -> p k n", n=width)

            def norm_chunks(full):
                sizes = [DC] * 5 + [3, 2, DC]
                base = sum(sizes[:full - 1]) - (full - 1)

                def wait(k):
                    if k < sizes[full - 1] - 1:
                        e.wait_ge(S["norm_chunk"], base + k + 1)
                    else:
                        e.wait_ge(S["norm_full"], full)
                return wait

            def unit(kc, rhs, evac, n=16, ready=None):
                w = slot(kc, n=n)
                for j in range(2):
                    b = 2 * ((st["u"] - 1) % 2) + j
                    e.wait_ge(evac.sem, evac.value(3))
                    for k in range(kc):
                        if ready and j == 0:
                            ready(k)
                        mm = e.matmul(ps[:, b, :], w[:, k, j * P:(j + 1) * P], rhs(k), start=(k == 0),
                                      stop=(k == kc - 1))
                    inc(mm, "chunk_done")
                    evac.add()

            def unit_tok(w, src, evac, st_bank):
                for j in range(2):
                    e.wait_ge(evac.sem, evac.value(3))
                    for q in range(2):
                        for k in range(DC):
                            mm = e.matmul(ps[:, st_bank + j, q * UNIT:(q + 1) * UNIT],
                                          src[:, k, (2 * j + q) * P:(2 * j + q + 1) * P], w[:, k, :],
                                          start=(k == 0), stop=(k == DC - 1))
                    inc(mm, "chunk_done")
                    evac.add()

            def pairs_of(n, body, evac, nland=16, extra=()):
                if n // 2 > 1:
                    u0 = st["u"]
                    with loop(e, n // 2, [(done, 4), (evac, 4), (landed[0], nland), (landed[1], nland), *extra]):
                        body()
                        body()
                    st["u"] = u0 + 2 * (n // 2)
                else:
                    for _ in range(2 * (n // 2)):
                        body()
                if n % 2:
                    body()

            w_hi, w_lo = c["w_hi"], c["w_lo"]

            def split_unit(kc, high, n=16):
                slot(kc, n=n)
                w_hi.add()
                w_lo.add()
                q = (st["u"] - 1) % 2
                return [x.rearrange("p (k n) -> p k n", n=UNIT) for x in (high[q][:, 0:kc * UNIT], wlo[:, q, 0:kc * UNIT])]

            def split_product(bank, w, j, kc, hi, lo, start, stop, ready=None):
                wh, wl = w
                cols = slice(j * P, (j + 1) * P)
                e.wait_ge(w_hi.sem, w_hi.value())
                for k in range(kc):
                    if ready:
                        e.wait_ge(S["nhi_ready"], ready[0] + k + 1)
                    e.matmul(bank, wh[:, k, cols], hi(k), start=(start and k == 0), stop=False)
                e.wait_ge(w_lo.sem, w_lo.value())
                for k in range(kc):
                    e.matmul(bank, wl[:, k, cols], hi(k), start=False, stop=False)
                for k in range(kc):
                    if ready:
                        e.wait_ge(S["nlo_ready"], ready[1] + k + 1)
                    mm = e.matmul(bank, wh[:, k, cols], lo(k), start=False, stop=(stop and k == kc - 1))
                inc(mm, "chunk_done")

            def split_linear(name, n, high, hi, lo, evac, ready=None, lands=None):
                settle()
                if name:
                    marks[name] = (st["u"], [l.at for l in landed])

                def one(nland=16):
                    w = split_unit(DC, high, nland)
                    b = 2 * ((st["u"] - 1) % 2)
                    for j in range(2):
                        e.wait_ge(evac.sem, evac.value(3))
                        split_product(ps[:, b + j, :], w, j, DC, lambda k: hi[:, k, :], lambda k: lo[:, k, :], True, True,
                                      ready if j == 0 else None)
                        evac.add()
                if lands:
                    for x in lands:
                        one(x)
                else:
                    pairs_of(n, one, evac, extra=[(w_hi, 2), (w_lo, 2)])

            def operand(n=DC):
                at = (c["nhi_ready"].at, c["nlo_ready"].at)
                c["nhi_ready"].add(n)
                c["nlo_ready"].add(n)
                return at

            def linear(n, kc, rhs, evac, ready=None):
                settle()
                pairs_of(n, lambda: unit(kc, rhs, evac, ready=ready), evac)

            def squares(n, bank, groups=1):
                if c["var_ready"].at:
                    need("var_ready", c["var_ready"].at)
                per = n // groups
                for g in range(groups):
                    for k in range(per):
                        need("sq_ready", c["sq_ready"].at + 1)
                        mm = e.matmul(ps[:, bank + g, :], ones[:], work[:, g * per + k, :], start=(k == 0),
                                      stop=(k == per - 1))
                inc(mm, "ms_ready")
                c["var_ready"].at += 1

            def nrhs(k):
                return nT[:, k, :]

            need("consts", 1)
            need("x_in", 16)
            for k in range(DC):
                if k >= 4:
                    need("hT_in", k - 3)
                for t in range(TT):
                    mm = e.transpose(ps[:, 4 + k % 4, t * P:(t + 1) * P], x_tok[:, t, k * P:(k + 1) * P], ident[:])
                inc(mm, "xtok_t")
            need("hT_in", 5)
            need("params_in", 16 * len(vectors))
            for k in range(3):
                mm = e.transpose(ps[:, 4, k * P:(k + 1) * P], par_rows[:, k, :], ident[:])
            inc(mm, "params_t")
            need("hT_in", 7)
            need("ws_in", 16)
            for h in range(6):
                mm = e.transpose(ps[:, 5 + h // 4, (h % 4) * P:(h % 4 + 1) * P], ws_in[:, h, :], ident[:])
            inc(mm, "ws_t")
            need("params_c", 1)
            need("ws_ready", 1)
            squares(DC, 4)
            at = operand()
            split_linear("w_in", 3, whi_in, n_hi, n_lo, act, at)
            split_linear(None, 6, whi_in, n_hi, n_lo, act)

            def ada(part, bank):
                need("ada_done", part + 1)
                for m in range(24):
                    mm = e.matmul(ps[:, bank, m:m + 1], asum[:, m * P:(m + 1) * P], ones[:, 0:1], start=True, stop=True)
                inc(mm, "ada_cols")

            def head_stats(src):
                if c["gl_veps"].at:
                    need("gl_veps", c["gl_veps"].at)
                need("gl_src", c["gl_src"].at + 1)
                for k in range(3):
                    mm = e.matmul(ps[:, 5 + k, :], bdiag[:], src[:, k, :], start=True, stop=True)
                inc(mm, "gl_mean")
                for k in range(3):
                    need("sq_ready", c["sq_ready"].at + 1)
                    mm = e.matmul(ps[:, 5 + k, :], bdiag[:], work[:, k, :], start=True, stop=True)
                inc(mm, "gl_var")
                c["gl_veps"].at += 1

            head_stats(cvA)
            head_stats(z[:, 15:18, :])
            need("gl_norm", 2)
            for t in range(TT):
                b = 5 + t % 3
                if t >= 3:
                    need("vt_ready", t - 2)
                for k in range(3):
                    mm = e.transpose(ps[:, b, k * P:(k + 1) * P], z[:, 15 + k, t * P:(t + 1) * P], ident[:])
                inc(mm, "vt_t")
            need("vt_ready", TT)
            for k in range(3):
                if k:
                    need("sg_done", k)
                for par_ in range(2):
                    for b in range(TT):
                        mm = e.matmul(ps[:, 5 + par_, b * P:(b + 1) * P], vtok[:, b, k * P:(k + 1) * P],
                                      wsT[:, 2 * k + par_, :], start=True, stop=True)
                inc(mm, "mix_ready")
            need("sg_done", 3)
            linear(4, DC, lambda k: mixT[:, k, :], dve)

            squares(DC, 4)
            ada(0, 7)
            need("norm_full", 2)
            for t in range(TT):
                for half in range(2):
                    if t or half:
                        need("ntok_ready", 2 * t + half)
                    for k in range(4):
                        kk = half * 4 + k
                        mm = e.transpose(ps[:, 5 + (2 * t + half) % 2, k * P:(k + 1) * P],
                                         nT[:, kk, t * P:(t + 1) * P], ident[:])
                    inc(mm, "ntok_t")
            split_linear("w_q", 8, whi_q, q_hi, n_lo, act, operand())
            need("keys_in", 16)
            need("ntok_ready", 2 * TT)
            need("mod_ready", 1)
            for q in range(4):
                for k in range(4):
                    mm = e.transpose(ps[:, 4 + q, k * P:(k + 1) * P], keys_in[:, 4 * q + k, :], ident[:])
                inc(mm, "keys_t")
            settle()
            need("keysT_ready", 4)
            for t in range(TT):
                for q in range(4):
                    b = 4 * (t % 2) + q
                    if t >= 2:
                        need("sc_ready", 4 * (t - 2) + q + 1)
                    for k in range(4):
                        mm = e.matmul(ps[:, b, k * P:(k + 1) * P], qT[:, 4 * q + k, t * P:(t + 1) * P],
                                      keysT[:, 4 * q + k, :], start=True, stop=True)
                    inc(mm, "sc_done")
            need("sc_ready", 4 * TT)
            vrow = [Count(s) for s in row_landed]
            dgr, vus = Count(S["diag_ready"]), Count(S["v_used"], RING)
            axr, aad = Count(S["acc_ready"], 1), Count(S["acc_added"], 1)

            def v_row(s, k, stop=False):
                vrow[s].add(16)
                e.wait_ge(vrow[s].sem, vrow[s].value())
                dgr.add()
                e.wait_ge(dgr.sem, dgr.value())
                for q in range(2):
                    mm = e.matmul(ps[:, 6 + q, :], diag[:, k, :], ring[:, s, q * 512:(q + 1) * 512], start=False,
                                  stop=stop)
                mm.then_inc(vus.sem, 1)
                vus.add()

            need("consts_v", 1)
            def v_mixed():
                for half in range(2):
                    for q in range(8):
                        vrow[2 * q].add(16)
                        v_row(2 * q + 1, half * 8 + q)

            def v_block(last):
                e.wait_ge(S["hT_in"], 1)
                e.wait_ge(axr.sem, axr.value())
                for q in range(8):
                    e.matmul(ps[:, 6 + q // 4, (q % 4) * P:(q % 4 + 1) * P], zero, ident[:], start=(q % 4 == 0), stop=False)
                with loop(e, HEADS - 1, [(dgr, TOPK), (vus, TOPK)] + [(l, 32) for l in vrow]):
                    v_mixed()
                if last:
                    for s in range(RING):
                        v_row(s, s)
                else:
                    v_mixed()
                for q in range(8):
                    mm = e.matmul(ps[:, 6 + q // 4, (q % 4) * P:(q % 4 + 1) * P], zero, ident[:], start=False, stop=(q % 4 == 3))
                inc(mm, "block_summed")
                axr.add()
                e.wait_ge(axr.sem, axr.value())
                e.wait_ge(aad.sem, aad.value())
                for k in range(DC):
                    mm = e.transpose(ps[:, 2 + k // 4, (k % 4) * P:(k % 4 + 1) * P], acc_sb[:, k * P:(k + 1) * P],
                                     ident[:])
                inc(mm, "acc_t")
                aad.add()

            for l in vrow:
                l.add(16)
            with loop(e, TT - 1, [(dgr, HEADS * TOPK), (vus, HEADS * TOPK), (axr, 1), (aad, 1)]
                      + [(l, 256) for l in vrow]):
                v_block(False)
            v_block(True)

            need("ptok_in", 16)
            need("acc_added", TT + 1)
            for k in range(2):
                for t in range(TT):
                    mm = e.transpose(ps[:, 6 + k, t * P:(t + 1) * P], p_tok[:, t, k * P:(k + 1) * P], ident[:])
            inc(mm, "pT_t")
            need("pT_ready", 1)
            linear(4, 2, lambda k: pT[:, k, :], act)
            settle()
            squares(DC, 4)
            linear(4, DC, nrhs, act, norm_chunks(3))
            squares(DC, 4)
            squares(DC, 4)

            settle()
            ada(1, 0)
            need("glr_in", 32)
            for k in range(DC):
                norm_chunks(5)(k)
                mm = e.matmul(ps[0:16, 5, :], wglr[:, k, :], nT[:, k, :], start=(k == 0), stop=(k == DC - 1))
            inc(mm, "glr_ready")
            need("glog_in", 1)
            for h in range(GLA_H):
                mm = e.matmul(ps[:, 4 + h, :], wgate[0:16, h * P:(h + 1) * P], glrT[0:16, :], start=True, stop=True)
                inc(mm, "glog_a")
            need("mod_ready", 2)
            linear(4, DC, nrhs, act)
            settle()
            u0 = st["u"]
            with loop(e, 2, [(done, 4), (act, 4), (landed[0], 16), (landed[1], 16)]):
                for p in range(2):
                    unit_tok(slot(DC), nT, act, 2 * p)
            st["u"] = u0 + 4
            settle()
            need("glog_v", GLA_H)
            need("q_sub", 1)
            r_first = st["u"]
            for i in range(8):
                need("k_sub", i + 1)
                for g in range(GLA_G):
                    mm = e.matmul(ps[:, 4 + g // 4, (g % 4) * P + 16 * i:(g % 4) * P + 16 * i + 16],
                                  kd_g(i % 2)[:, g, :], gsubs(qsub)[:, g, 16 * i:16 * i + 16], start=True, stop=True)
                inc(mm, "amat_done")
                j = i % 2
                if j == 0:
                    w = slot(DC)
                e.wait_ge(act.sem, act.value(3))
                for k in range(DC):
                    mm = e.matmul(ps[:, 2 * ((i // 2 + r_first) % 2) + j, :], w[:, k, j * P:(j + 1) * P], nrhs(k),
                                  start=(k == 0), stop=(k == DC - 1))
                inc(mm, "chunk_done")
                act.add()
            settle()
            ada(2, 0)
            need("kw_ready", 1)
            for h in range(GLA_H):
                need("a_ready", h + 1)
                for t in range(TT):
                    mm = e.transpose(ps[:, 4 + h, t * P:(t + 1) * P], gtmp2[:, h, t * P:(t + 1) * P], ident[:])
                inc(mm, "kw_t")
            need("ew_done", 1)
            for t in range(TT):
                for h in range(GLA_H):
                    i = t * GLA_H + h
                    g = h * TT + t
                    b = 4 + i % 4
                    if i < 4:
                        need("kw_tok", h + 1)
                    else:
                        need("o_evac", i - 3)
                        need("s_new", i - 3)
                    for v in range(2):
                        mm = e.matmul(ps[:, b, v * P:(v + 1) * P],
                                      gvt[:, t, h * GLA_DV + v * P:h * GLA_DV + (v + 1) * P], amat[:, g, :],
                                      start=True, stop=(t == 0))
                        if t:
                            mm = e.matmul(ps[:, b, v * P:(v + 1) * P], state[:, h, v * P:(v + 1) * P],
                                          gq[:, h, t * P:(t + 1) * P], start=False, stop=True)
                    if t < TT - 1:
                        mm = e.matmul(ps[:, b, 2 * P:4 * P], kwt[:, g, :], gvt[:, t, h * GLA_DV:(h + 1) * GLA_DV],
                                      start=True, stop=True)
                    inc(mm, "o_done")
            need("o_evac", 16)
            squares(DC, 4, groups=4)
            need("mod_ready", 3)
            split_linear("gla_out", 4, whi_go, n_hi, n_lo, dve, operand())

            def ffn(layer):
                squares(DC, 4)
                marks[f"ffn{layer}"] = (st["u"], [l.at for l in landed])
                settle()
                parts = operand()
                counts = [(landed[0], 16), (landed[1], 16), (w_hi, 2), (w_lo, 2)]
                with loop(e, FH, [(done, 4), (act, 2), (dve, 2)] + counts):
                    for p, evac in enumerate((act, dve)):
                        w = split_unit(DC, whi_f)
                        for j in range(2):
                            e.wait_ge(evac.sem, evac.value(1))
                            split_product(ps[:, 2 * p + j, :], w, j, DC, lambda k: n_hi[:, k, :], lambda k: n_lo[:, k, :],
                                          True, True, parts if (p, j) == (0, 0) else None)
                            evac.add()
                st["u"] += 2 * (FH - 1)
                settle()
                need("hid_ready", c["hid_ready"].at + FC)
                with loop(e, 2, [(done, 8), (dve, 4), (landed[0], 32), (landed[1], 32), (w_hi, 4), (w_lo, 4)]):
                    for half in range(2):
                        for kh in range(2):
                            w = split_unit(FH, whi_f)
                            for j in range(2):
                                if kh == 0:
                                    e.wait_ge(dve.sem, dve.value(3 - j))
                                split_product(ps[:, 2 * half + j, :], w, j, FH, lambda k: hid_h[:, kh * FH + k, :],
                                              lambda k: hid_l[:, kh * FH + k, :], kh == 0, kh == 1)
                        dve.add(2)
                st["u"] += 4

            ffn(0)

            squares(DC, 4)
            split_linear("mla_in", 3, whi_m, n_hi, n_lo, act, operand(), lands=(16, 16, 32))
            squares(3, 4)
            squares(2, 4)
            need("norm_full", 6)
            settle()
            for m in range(4):
                w = slot(3, width=384, n=64)
                for j in range(3):
                    e.wait_ge(act.sem, act.value(3))
                    for k in range(3):
                        mm = e.matmul(ps[:, (3 * m + j) % 4, :], w[:, k, j * P:(j + 1) * P], cT6[:, k, :], start=(k == 0), stop=(k == 2))
                    inc(mm, "chunk_done")
                    act.add()
            need("norm_full", 7)
            settle()

            def kv_unit():
                w = slot(2)
                b = 2 * ((st["u"] - 1) % 2)
                e.wait_ge(act.sem, act.value(3))
                for k in range(2):
                    mm = e.matmul(ps[:, b, :], w[:, k, 0:NOPE], cT6[:, 3 + k, :], start=(k == 0), stop=(k == 1))
                inc(mm, "chunk_done")
                act.add()
                e.wait_ge(act.sem, act.value(3))
                for t in range(TT):
                    for k in range(2):
                        mm = e.matmul(ps[:, b + 1, t * P:(t + 1) * P], cT6[:, 3 + k, t * P:(t + 1) * P],
                                      w[:, k, NOPE:NOPE + VDIM], start=(k == 0), stop=(k == 1))
                inc(mm, "chunk_done")
                act.add()

            pairs_of(MLA_H, kv_unit, act)
            settle()
            for r in range(5):
                if r >= 4:
                    need("rope_read", r - 3)
                mm = e.matmul(ps[:, 4 + r % 4, :], rotm[:], cT6[:, 5, :] if r == 4 else qr[:, r, :],
                              start=True, stop=True)
                inc(mm, "rot_done")
            need("rope_ready", 5)
            settle()
            ITEMS = MLA_H * TT

            def scores(i):
                h, t = divmod(i, TT)
                if i >= 4:
                    need("att_p", i - 3)
                n = (t + 1) * P
                r0 = 64 * (h % 2)
                e.matmul(sbank(i, n), qn[:, h, t * P:(t + 1) * P], kn[:, h, 0:n], start=True, stop=False)
                mm = e.matmul(sbank(i, n), qr[r0:r0 + 64, h // 2, t * P:(t + 1) * P],
                              cT6[r0:r0 + 64, 5, 0:n], start=False, stop=True)
                inc(mm, "att_s")

            def turn(i):
                h, t = divmod(i, TT)
                need("att_n", i + 1)
                if i >= 2:
                    need("att_pt", i - 1)
                for q in range(t + 1):
                    mm = e.transpose(ps[:, 2 + i % 2, q * P:(q + 1) * P], pp[:, i % 4, q * P:(q + 1) * P], ident[:])
                inc(mm, "att_t")

            def head_out(h):
                need("att_pt", TT * (h + 1))
                if h >= 2:
                    need("att_oe", h - 1)
                for q in range(TT):
                    mm = e.matmul(ps[:, 6 + h % 2, q * P:T], vt[:, q, h * VDIM:(h + 1) * VDIM],
                                  pTt[:, q, q * P:T], start=(q == 0), stop=(q == TT - 1))
                inc(mm, "att_o")

            for i in range(3):
                scores(i)
            for i in range(ITEMS):
                if i + 3 < ITEMS:
                    scores(i + 3)
                turn(i)
                if i and i % TT == 0:
                    head_out(i // TT - 1)
            head_out(MLA_H - 1)
            need("att_oe", MLA_H)
            ada(3, 0)
            need("mod_ready", 4)
            split_linear("mla_out", 4, whi_m, n_hi, n_lo, dve)
            ffn(1)
            squares(DC, 4)
            need("norm_full", 8)
            for t in range(TT):
                for half in range(2):
                    i = 2 * t + half
                    if i >= 3:
                        need("fin_ready", i - 2)
                    for k in range(4):
                        mm = e.transpose(ps[:, 5 + i % 3, k * P:(k + 1) * P], nT[:, half * 4 + k, t * P:(t + 1) * P],
                                         ident[:])
                    inc(mm, "fin_t")

        @block.gpsimd
        def _(e):
            k = Count(S["pl_ch"])

            def chain(ins):
                ins.then_inc(k.sem, 1)
                k.add()
                e.wait_ge(k.sem, k.value())

            chain(e.memset(eps[:], EPS))
            chain(e.memset(ident[:], 0.0))
            chain(e.affine_select(out=ident[:], in_=ident[:], compare_op=ALU.not_equal, fill=1.0, base=0,
                                  pattern=[[-1, P]], channel_multiplier=1))
            chain(e.memset(ones[:], 1.0))
            chain(e.memset(bdiag[:], 0.0))
            for q in range(2):
                chain(e.memset(bdiag[64 * q:64 * q + 64, 64 * q:64 * q + 64], 1.0 / 64))
            chain(e.memset(rotm[:], 0.0))
            pairs = rotm[:].rearrange("p (i two) -> p i two", two=2)
            chain(e.affine_select(out=pairs[:, :, 0], in_=pairs[:, :, 0], compare_op=ALU.not_equal, fill=-1.0,
                                  base=-1, pattern=[[-2, 64]], channel_multiplier=1))
            chain(e.affine_select(out=pairs[:, :, 1], in_=pairs[:, :, 1], compare_op=ALU.not_equal, fill=1.0,
                                  base=0, pattern=[[-2, 64]], channel_multiplier=1))
            chain(e.memset(padA[:, :, 0:TAPS_A - 1], 0.0))
            chain(e.memset(padB[:, :, 0:TAPS_B - 1], 0.0))
            e.memset(par_rows[:], 0.0).then_inc(S["consts"], 1)
            ach = Count(S["ada_ch"])
            alanded = [Count(x) for x in ada_landed]

            def ada(part):
                W = IN["ada_w_2"][part // 2]

                def fetch(unit_, p):
                    e.dma_start(aslot[:, p, :, :],
                                W[:, bass.ds(unit_ * UNIT + (part % 2) * 3 * D, UNIT)].rearrange("(k p) n -> p k n", p=P)
                                ).then_inc(ada_landed[p], 16)

                def product(unit_, p):
                    def stage(ins):
                        ins.then_inc(ach.sem, 1)
                        ach.add()
                        e.wait_ge(ach.sem, ach.value())

                    alanded[p].add(16)
                    e.wait_ge(alanded[p].sem, alanded[p].value())
                    w = aslot[:, p, :, :]
                    stage(e.tensor_tensor(w, w, cT[:, :].rearrange("p (k n) -> p k n", n=1).to_broadcast([P, DC, UNIT]),
                                          ALU.mult))
                    for half in (4, 2):
                        stage(e.tensor_tensor(w[:, 0:half, :], w[:, 0:half, :], w[:, half:2 * half, :], ALU.add))
                    stage(e.tensor_tensor(asum[:, bass.ds(unit_ * UNIT, UNIT)], w[:, 0, :], w[:, 1, :], ALU.add))

                fetch(0, 0)
                fetch(1, 1)
                with loop(e, 5, [(ach, 8), (alanded[0], 16), (alanded[1], 16)]) as i:
                    for p in range(2):
                        product(i * 2 + p, p)
                        fetch(i * 2 + (2 + p), p)
                for p in range(2):
                    product(10 + p, p)
                e.sem_inc(S["ada_done"], 1)

            w_split = Count(S["w_hi"])
            FFN_UNITS = [(2 * FH, DC), (8, FH)]

            def split_run(name, stretches, high, lands=None):
                u, at = marks[name]
                landed_ = [Count(x, n) for x, n in zip(w_landed, at)]

                def split(q, kc, n=16):
                    landed_[q].add(n)
                    e.wait_ge(landed_[q].sem, landed_[q].value())
                    e.sem_inc(S["pool_step"], 1)
                    w, hi = wring[:, q, 0:kc * UNIT], high[q][:, 0:kc * UNIT]
                    e.tensor_scalar(hi, w, 1.0, 0.0, ALU.mult, ALU.add).then_inc(w_split.sem, 1)
                    w_split.add()
                    e.wait_ge(w_split.sem, w_split.value())
                    e.sem_inc(S["pool_step"], 1)
                    e.tensor_tensor(wlo[:, q, 0:kc * UNIT], w, hi.bitcast(F32), ALU.subtract).then_inc(S["w_lo"], 1)

                for n, kc in stretches:
                    if lands:
                        for i, x in enumerate(lands):
                            split((u + i) % 2, kc, x)
                        return
                    with loop(e, n // 2, [(w_split, 2), (landed_[0], 16), (landed_[1], 16)]):
                        for p in range(2):
                            split((u + p) % 2, kc)
                    if n % 2:
                        split(u % 2, kc)
                    u += n

            split_run("w_in", [(9, DC)], whi_in)
            e.wait_ge(S["cT_ready"], 1)
            ada(0)
            e.wait_ge(S["sg_done"], 3)
            split_run("w_q", [(8, DC)], whi_q)

            e.wait_ge(S["ada_cols"], 1)
            chain(e.iota(iota16, [[1, TOPK]], base=0, channel_multiplier=0, allow_small_or_imprecise_dtypes=True))
            e.memset(small[:, 0:1], 0.0).then_inc(S["consts"], 1)
            e.wait_ge(S["sc_done"], 4 * TT)
            copied = Count(S["idx_copied"])
            landed = [Count(s) for s in row_landed]
            ready = Count(S["idx_ready"])
            us, vs = Count(S["u_used"]), Count(S["v_used"], RING)
            expert_u, expert_v = IN["expert_u"][0], IN["expert_v"][0]

            def gather(g, tables, parts):
                for dst, src in parts:
                    e.tensor_copy(dst, src).then_inc(copied.sem, 1)
                    copied.add()
                e.wait_ge(copied.sem, copied.value())
                e.sem_inc(S["pool_step"], 1)
                for s, table in zip(range(g, g + 4), tables):
                    e.indirect_dma_start(ring[:, s, :], None, table,
                                         bass.IndirectOffsetOnAxis(ap=cur[:, s:s + 1], axis=0)
                                         ).then_inc(landed[s].sem, 16)

            def after_mixed(g):
                e.wait_ge(us.sem, us.value(8 - (g // 2 + 2)))
                e.wait_ge(vs.sem, vs.value(8 - (g // 2 + 2)))

            ready.add()
            e.wait_ge(ready.sem, ready.value())
            for g in range(0, RING, 4):
                gather(g, [expert_u] * 4, [(cur[:, g:g + 4], idx_flat[:, g:g + 4])])
            us.add(RING)
            with loop(e, UNITS - 1, [(copied, 16), (us, RING), (vs, RING), (ready, 1)]) as n:
                ready.add()
                e.wait_ge(ready.sem, ready.value())
                for half in range(2):
                    for g in range(0, RING, 4):
                        after_mixed(g)
                        v0 = n * TOPK + (half * 8 + g // 2)
                        gather(g, [expert_u, expert_v] * 2,
                               [(cur[:, g:g + 4:2], idx_flat[:, bass.ds(v0 + TOPK, 2)]),
                                (cur[:, g + 1:g + 4:2], idx_flat[:, bass.ds(v0, 2)])])
                    us.add(RING // 2)
                    vs.add(RING // 2)
            for g in range(0, RING, 4):
                after_mixed(g)
                gather(g, [expert_v] * 4, [(cur[:, g:g + 4], idx_flat[:, (UNITS - 1) * TOPK + g:(UNITS - 1) * TOPK + g + 4])])
            e.wait_ge(S["h_ready"], 2)
            ada(1)
            e.wait_ge(S["norm_full"], 5)
            chain(e.memset(keep, 1.0))
            chain(e.affine_select(out=keep, in_=keep, compare_op=ALU.is_ge, fill=0.0, base=0,
                                  pattern=[[1, P]], channel_multiplier=-1))
            chain(e.memset(reset, 1.0))
            for t in range(TT):
                chain(e.memset(reset[:, t * P:t * P + 1], 0.0))
            e.memset(kd, 0.0).then_inc(S["consts"], 1)
            e.wait_ge(S["ada_cols"], 2)
            ada(2)

            e.wait_ge(S["ew_exp"], 3)
            e.wait_ge(S["amat_done"], 8)
            split_run("gla_out", [(4, DC)], whi_go)
            e.wait_ge(S["h_ready"], 5)
            split_run("ffn0", FFN_UNITS, whi_f)
            e.wait_ge(S["h_ready"], 6)
            chain(e.memset(cmask, 0.0))
            e.affine_select(out=cmask, in_=cmask, compare_op=ALU.is_ge, fill=MASKED, base=0,
                            pattern=[[-1, P]], channel_multiplier=1).then_inc(S["consts"], 1)
            split_run("mla_in", [(3, DC)], whi_m, lands=(16, 16, 32))
            e.wait_ge(S["norm_full"], 6)
            ada(3)
            e.wait_ge(S["ada_cols"], 4)
            split_run("mla_out", [(4, DC)], whi_m)
            e.wait_ge(S["h_ready"], 7)
            split_run("ffn1", FFN_UNITS, whi_f)

        @block.scalar
        def _(e):
            c = {n: Count(s) for n, s in S.items()}
            done, evacs = c["chunk_done"], Count(S["act_evac"], 4)
            st = {"u": 0, "norm": 0}

            def need(name, n):
                c[name].at = max(c[name].at, n)
                e.wait_ge(S[name], n)

            def inc(ins, name):
                ins.then_inc(S[name], 1)
                c[name].add()

            def own(ins, name):
                inc(ins, name)
                e.wait_ge(S[name], c[name].value())

            def squares(aps):
                for k, ap in enumerate(aps):
                    inc(e.activation(work[:, k, :], ap, ACT.Square), "sq_ready")

            def rsqrt(dst, log, src, dim):
                c["ms_ready"].at += 1
                e.wait_ge(S["ms_ready"], c["ms_ready"].at)
                own(e.activation(log, src, ACT.Ln, scale=1.0 / dim, bias=eps[:, 0:1]), "var_ready")
                inc(e.activation(dst, log, ACT.Exp, scale=-0.5), "std_ready")

            def root(dim=D):
                rsqrt(row[:, 2 * (st["norm"] % 2), :], row[:, 1, :], ps[:, 4, :], dim)
                st["norm"] += 1

            def hchunks():
                return [hT[:, k, :] for k in range(DC)]

            def units(n, evac, first=0):
                def one(base):
                    b = 2 * (st["u"] % 2)
                    st["u"] += 1
                    for j in range(2):
                        done.add()
                        e.wait_ge(done.sem, done.value())
                        evac(ps[:, b + j, :], base + j).then_inc(evacs.sem, 1)
                        evacs.add()
                if n // 2 > 1:
                    u0 = st["u"]
                    with loop(e, n // 2, [(done, 4), (evacs, 4)]) as i:
                        one(i * 4 + first)
                        one(i * 4 + (first + 2))
                    st["u"] = u0 + 2 * (n // 2)
                else:
                    for q in range(2 * (n // 2)):
                        one(first + 2 * q)
                if n % 2:
                    one(first + 2 * (n - 1))

            def copy_to(dst, scale=1.0, func=ACT.Copy):
                def evac(src, m):
                    where = dst[:, m, :] if isinstance(m, int) else dst[:, bass.ds(m, 1), :].rearrange("p a k -> p (a k)")
                    return e.activation(where, src, func, scale=scale)
                return evac

            def skip(n):
                done.add(2 * n)
                st["u"] += n

            def high_parts(dst, ready):
                for k in range(DC):
                    ready(k)
                    inc(e.activation(dst[:, k, :], nT[:, k, :], ACT.Copy), "nhi_ready")

            def high_shifted(shift):
                for k in range(DC):
                    need("norm_scaled", c["norm_scaled"].at + 1)
                    inc(e.activation(n_hi[:, k, :], nT[:, k, :], ACT.Identity, bias=mod[:, shift + k:shift + k + 1]),
                        "nhi_ready")

            def norm_chunks(full):
                def wait(k):
                    if k < DC - 1:
                        e.wait_ge(S["norm_chunk"], (full - 1) * (DC - 1) + k + 1)
                    else:
                        e.wait_ge(S["norm_full"], full)
                return wait

            e.sem_inc(S["act_evac"], 4)
            for k in range(DC):
                need("xtok_t", k + 1)
                inc(e.activation(hT[:, k, :], ps[:, 4 + k % 4, :], ACT.Copy), "hT_in")
            need("hT_in", DC)
            squares(hchunks())
            root()
            need("params_c", 1)
            high_parts(n_hi, norm_chunks(1))
            own(e.activation(cT[:], col("c_2", 0, DC), ACT.Silu), "cT_ready")
            copy = copy_to(z)
            gate = copy_to(z, func=ACT.Sigmoid)
            units(3, lambda src, m: (copy if m < 3 else gate)(src, m))
            units(6, copy_to(z), first=6)

            def head_norm(src, dst, g, b, func):
                for k in range(3):
                    need("gl_cen", c["gl_cen"].at + 1)
                    inc(e.activation(work[:, k, :], src[:, k, :], ACT.Square), "sq_ready")
                need("gl_var", c["gl_var"].at + 1)
                own(e.activation(gvar, ps[:, 5:8, :], ACT.Ln, bias=eps[:, 0:1]), "gl_veps")
                inc(e.activation(gvar, gvar, ACT.Exp, scale=-0.5), "gl_std")
                need("mix_scaled", c["mix_scaled"].at + 1)
                for k in range(3):
                    ins = e.activation(dst[:, k, :], src[:, k, :], func, scale=col(g, k), bias=col(b, k))
                inc(ins, "gl_norm")

            head_norm(cvA, mixT, "ln_a_g", "ln_a_b", ACT.Silu)
            head_norm(z[:, 15:18, :], z[:, 15:18, :], "ln_c_g", "ln_c_b", ACT.Identity)
            for t in range(TT):
                need("vt_t", t + 1)
                inc(e.activation(vtok[:, t, :], ps[:, 5 + t % 3, 0:MIX_C], ACT.Copy), "vt_ready")
            skip(4)
            need("h_ready", 1)
            squares(hchunks())
            root()
            high_parts(q_hi, norm_chunks(2))
            for i in range(2 * TT):
                need("ntok_t", i + 1)
                inc(e.activation(ntok[:, i // 2, (i % 2) * 512:(i % 2 + 1) * 512], ps[:, 5 + i % 2, :], ACT.Copy),
                    "ntok_ready")
            units(8, copy_to(qT))
            for q in range(4):
                need("keys_t", q + 1)
                inc(e.activation(keysT[:, 4 * q:4 * q + 4, :].rearrange("p a k -> p (a k)"), ps[:, 4 + q, :], ACT.Copy),
                    "keysT_ready")
            for t in range(TT):
                for q in range(4):
                    need("sc_done", 4 * t + q + 1)
                    u = HEADS * t + 2 * q
                    inc(e.activation(score[:, u:u + 2, :].rearrange("p a k -> p (a k)"), ps[:, 4 * (t % 2) + q, :],
                                     ACT.Copy), "sc_ready")
                    if t == 0 and q == 0:
                        e.wait_ge(S["sc_ready"], 1)
                        inc(e.activation(hs.rearrange("p a k -> p (a k)"), score[:, 0, :], ACT.Copy), "hs_ready")
            e.wait_ge(S["sc_ready"], c["sc_ready"].value())
            inc(e.activation(score[:, UNITS:UNITS + AHEAD, :], score[:, 0:AHEAD, :], ACT.Copy), "sc_ready")
            e.wait_ge(S["sc_ready"], c["sc_ready"].value())
            hsr, hst, cmx, gxp = c["hs_read"], c["hs_ready"], c["cand_max"], c["gexp"]
            used, xrd, gel = c["u_used"], c["x_ready"], c["gelu_ready"]
            cof, dgr, vus, axr = c["coef_ready"], c["diag_ready"], c["v_used"], c["acc_ready"]
            vus.at = RING
            e.sem_inc(S["v_used"], RING)

            def diagonals():
                cof.add()
                e.wait_ge(cof.sem, cof.value())
                for k in range(TOPK):
                    e.wait_ge(vus.sem, vus.value(TOPK - 1 - k))
                    e.activation(diag[:, k, :], ident[:], ACT.Copy, scale=coef[:, k:k + 1]).then_inc(dgr.sem, 1)
                    dgr.add()
                vus.add(TOPK)

            def head_scores(n):
                hst.add()
                if not (isinstance(n, int) and n == 0):
                    e.wait_ge(hsr.sem, hst.value(1))
                src = score[:, n, :] if isinstance(n, int) else score[:, bass.ds(n, 1), :].rearrange("p a k -> p (a k)")
                e.activation(hs.rearrange("p a k -> p (a k)"), src, ACT.Copy).then_inc(hst.sem, 1)

            def gate_exp():
                cmx.add()
                e.wait_ge(cmx.sem, cmx.value())
                e.activation(gcur, top_v[:, 2, :], ACT.Exp, bias=small[:, 1:2], accum_out=small[:, 2:3]).then_inc(gxp.sem, 1)
                gxp.add()

            def hidden():
                e.activation(gdots, dots, ACT.Gelu_apprx_tanh).then_inc(gel.sem, 1)
                gel.add()

            gate_exp()
            head_scores(1)
            gate_exp()
            acct = c["acc_t"]
            for count in (axr, acct, c["acc_added"]):
                e.sem_inc(count.sem, 1)
                count.at = 1

            def tokens(b):
                e.wait_ge(used.sem, used.value())
                src = ntok[:, b, :] if isinstance(b, int) else ntok[:, bass.ds(b, 1), :].rearrange("p a k -> p (a k)")
                e.activation(ps[:, 4:6, :].rearrange("p a k -> p (a k)"), src, ACT.Copy).then_inc(xrd.sem, 1)
                xrd.add()

            def head(n):
                head_scores(n + AHEAD)
                used.add(TOPK)
                e.wait_ge(used.sem, used.value())
                hidden()
                gate_exp()
                diagonals()

            def block_(b, last):
                with loop(e, HEADS - 1, [(hst, 1), (cmx, 1), (gxp, 1), (used, TOPK), (gel, 1), (cof, 1), (dgr, TOPK),
                                         (vus, TOPK)]) as h:
                    head(h + b * HEADS + 1)
                if not last:
                    tokens(b + 1)
                    head(b * HEADS + HEADS)
                e.wait_ge(acct.sem, acct.value())
                blk.add()
                e.wait_ge(blk.sem, blk.value())
                e.activation(acc_sb, ps[:, 6:8, :].rearrange("p a k -> p (a k)"), ACT.Copy).then_inc(axr.sem, 1)
                axr.add()
                acct.add()

            blk = c["block_summed"]
            e.wait_ge(S["hT_in"], 1)
            tokens(0)
            head(0)
            with loop(e, TT - 1, [(hst, 8), (cmx, 8), (gxp, 8), (used, PER_BLOCK), (xrd, 1), (gel, 8), (cof, 8),
                                  (dgr, PER_BLOCK), (vus, PER_BLOCK), (axr, 1), (acct, 1), (blk, 1)]) as b:
                block_(b, False)
            block_(TT - 1, True)
            need("pT_t", 1)
            inc(e.activation(pT, ps[:, 6:8, :], ACT.Copy), "pT_ready")
            units(4, copy_to(peT))
            need("h_ready", 2)
            squares(hchunks())
            root()
            units(4, copy_to(sgT, func=ACT.Sigmoid))
            need("h_ready", 3)
            squares(hchunks())
            root()
            need("h_ready", 4)
            squares(hchunks())
            root()

            need("glr_ready", 1)
            inc(e.activation(glrT[0:16, :], ps[0:16, 5, :], ACT.Copy), "glog_in")
            for h in range(GLA_H):
                need("glog_a", h + 1)
                own(e.activation(gtmp[:, h, :], ps[:, 4 + h, :], ACT.Abs, bias=col("gla_b_gate_2", h)), "a_ch")
            own(e.activation(gtmp2, gtmp, ACT.Exp, scale=-1.0), "a_ch")
            inc(e.activation(gtmp2, gtmp2, ACT.Ln, bias=1.0), "glog_l")
            q_or_k = (copy_to(gq, scale=GLA_DK ** -0.5), copy_to(gk))
            for q in range(2):
                for p in range(2):
                    for j in range(2):
                        done.add()
                        e.wait_ge(done.sem, done.value())
                        q_or_k[q](ps[:, 2 * (st["u"] % 2) + j, :], 2 * p + j).then_inc(evacs.sem, 1)
                        evacs.add()
                    st["u"] += 1
            need("dq_ready", 1)
            inc(e.activation(qsub, gtmp, ACT.Exp, scale=1.0 / 16), "dq_exp")
            for i in range(2):
                need("dk_ready", i + 1)
                n = 16 * (i + 1)
                inc(e.activation(kd_g(i % 2)[:, :, 0:n], kd_g(i % 2)[:, :, 0:n], ACT.Exp, scale=1.0 / 16), "dk_exp")
            with loop(e, 2, [(done, 4), (evacs, 4)]) as i:
                for p in range(2):
                    for j in range(2):
                        done.add()
                        e.wait_ge(done.sem, done.value())
                        e.activation(gvt[:, 2 * j:2 * j + 2, bass.ds(i * (2 * UNIT) + p * UNIT, UNIT)],
                                     ps[:, 2 * p + j, :].rearrange("p (a k) -> p a k", a=2), ACT.Copy
                                     ).then_inc(evacs.sem, 1)
                        evacs.add()
            st["u"] += 4
            for i in range(8):
                if i + 2 < 8:
                    need("dk_ready", i + 3)
                    n = 16 * (i + 3)
                    inc(e.activation(kd_g(i % 2)[:, :, 0:n], kd_g(i % 2)[:, :, 0:n], ACT.Exp, scale=1.0 / 16), "dk_exp")
                done.add()
                e.wait_ge(done.sem, done.value())
                e.activation(gr[:, i, :], ps[:, 2 * ((st["u"] + i // 2) % 2) + i % 2, :], ACT.Copy
                             ).then_inc(evacs.sem, 1)
                evacs.add()
            st["u"] += 4
            need("ew_ready", 1)
            own(e.activation(gtmp, gb, ACT.Exp, scale=1.0 / 16), "ew_exp")
            own(e.activation(elast, gsubs(gb)[:, :, P - 1], ACT.Exp, scale=1.0 / 16), "ew_exp")
            inc(e.activation(gtmp2, gtmp2, ACT.Exp, scale=1.0 / 16), "ew_exp")
            need("ada_done", 3)
            for h in range(GLA_H):
                need("kw_t", h + 1)
                inc(e.activation(kwt[:, 4 * h:4 * h + 4, :], ps[:, 4 + h, :].rearrange("p (a k) -> p a k", a=4), ACT.Copy),
                    "kw_tok")
            for i in range(16):
                t, h = divmod(i, GLA_H)
                need("o_done", i + 1)
                inc(e.activation(goT[:, 2 * h:2 * h + 2, t * P:(t + 1) * P],
                                 ps[:, 4 + i % 4, 0:2 * P].rearrange("p (a k) -> p a k", a=2), ACT.Copy), "o_evac")
                if i == 0:
                    e.wait_ge(evacs.sem, evacs.value())
                    inc(e.activation(gr[:, 0:4, :], gr[:, 0:4, :], ACT.Silu), "gr_ready")
                if i == 4:
                    inc(e.activation(gr[:, 4:8, :], gr[:, 4:8, :], ACT.Silu), "gr_ready")
            need("o_evac", 16)
            squares([goT[:, k, :] for k in range(DC)])
            rsqrt(gtmp2, gtmp, ps[:, 4:8, :], GLA_DV)
            high_parts(n_hi, lambda k: e.wait_ge(S["go_chunk"], k + 1))
            skip(4)

            def ffn(h):
                need("h_ready", h)
                squares(hchunks())
                root()
                dve = Count(S["dve_evac"], 4)
                dve.at = st["dve"]
                raw, hh = c["hid_raw"], c["hid_hi_ready"]
                high_shifted(48 * (h // 7) + 24)
                with loop(e, FH, [(done, 4), (evacs, 2), (dve, 2), (raw, 2), (hh, 2)]) as i:
                    for j in range(2):
                        done.add()
                        e.wait_ge(done.sem, done.value())
                        e.wait_ge(dve.sem, dve.value(1))
                        e.activation(gsil[:, j, :], ps[:, j, :], ACT.Silu).then_inc(evacs.sem, 1)
                        evacs.add()
                        dve.add()
                    done.add(2)
                    for j in range(2):
                        raw.add()
                        e.wait_ge(raw.sem, raw.value())
                        m = bass.ds(i * 2 + j, 1)
                        e.activation(hid_h[:, m, :].rearrange("p a k -> p (a k)"), hid[:, m, :].rearrange("p a k -> p (a k)"),
                                     ACT.Copy).then_inc(hh.sem, 1)
                        hh.add()
                done.add(16)
                st["dve"] = dve.at + 8

            st["dve"] = 4 + 8 + 8
            ffn(5)
            st["u"] += 22 + 8

            need("h_ready", 6)
            squares(hchunks())
            root()
            high_shifted(48)
            need("pos_in", 16)
            units(3, copy_to(cT6))
            e.wait_ge(evacs.sem, evacs.value())
            squares([cT6[:, k, :] for k in range(3)])
            root(384)
            squares([cT6[:, 3 + k, :] for k in range(2)])
            root(256)
            for m in range(4):
                for j in range(3):
                    done.add()
                    e.wait_ge(done.sem, done.value())
                    dst = qr[:, m, :] if j == 2 else qn[:, 2 * m + j, :]
                    e.activation(dst, ps[:, (3 * m + j) % 4, :], ACT.Copy).then_inc(evacs.sem, 1)
                    evacs.add()
            st["u"] += 4
            with loop(e, 4, [(done, 4), (evacs, 4)]) as i:
                for p in range(2):
                    b = 2 * ((st["u"] + p) % 2)
                    done.add()
                    e.wait_ge(done.sem, done.value())
                    e.activation(kn[:, bass.ds(i * 2 + p, 1), :].rearrange("p a k -> p (a k)"), ps[:, b, :], ACT.Copy
                                 ).then_inc(evacs.sem, 1)
                    evacs.add()
                    done.add()
                    e.wait_ge(done.sem, done.value())
                    e.activation(vt[:, :, bass.ds(i * 256 + p * VDIM, VDIM)],
                                 ps[:, b + 1, :].rearrange("p (a k) -> p a k", a=TT), ACT.Copy).then_inc(evacs.sem, 1)
                    evacs.add()
            st["u"] += 8
            need("angle_ready", 1)
            inc(e.activation(tri, rtmp, ACT.Sin), "trig_ready")

            SCALE = float(NOPE + ROPE) ** -0.5

            def evac_p(i):
                h, t = divmod(i, TT)
                need("att_t", i + 1)
                if t == 0 and h:
                    need("att_o", h)
                inc(e.activation(pTt[:, 0:t + 1, t * P:(t + 1) * P],
                                 ps[:, 2 + i % 2, 0:(t + 1) * P].rearrange("p (a k) -> p a k", k=P), ACT.Copy), "att_pt")

            def exp_p(i):
                n = (i % TT + 1) * P
                need("att_m", i + 1)
                if i >= 4:
                    need("att_t", i - 3)
                inc(e.activation(pp[:, i % 4, 0:n], sbank(i, n), ACT.Exp, scale=SCALE,
                                 bias=attsm[:, i % 4, 1:2], accum_out=attsm[:, i % 4, 2:3]), "att_p")

            exp_p(0)
            exp_p(1)
            for i in range(MLA_H * TT):
                if i + 2 < MLA_H * TT:
                    exp_p(i + 2)
                h, t = divmod(i, TT)
                evac_p(i)
                if t == 0 and h:
                    inc(e.activation(n_hi[:, h - 1, :], ps[:, 6 + (h - 1) % 2, :], ACT.Copy), "att_oh")
            need("att_o", MLA_H)
            inc(e.activation(n_hi[:, MLA_H - 1, :], ps[:, 6 + (MLA_H - 1) % 2, :], ACT.Copy), "att_oh")
            skip(4)
            st["dve"] += 8
            ffn(7)
            need("h_ready", 8)
            squares(hchunks())
            root()
            for i in range(2 * TT):
                need("fin_t", i + 1)
                inc(e.activation(o_tok[:, i // 2, (i % 2) * 512:(i % 2 + 1) * 512], ps[:, 5 + i % 3, :], ACT.Copy),
                    "fin_ready")

        @block.vector
        def _(e):
            c = {n: Count(s) for n, s in S.items()}
            done, evacs = c["chunk_done"], Count(S["dve_evac"], 4)
            st = {"u": 0, "norm": 0}

            def need(name, n):
                c[name].at = max(c[name].at, n)
                e.wait_ge(S[name], n)

            def inc(ins, name):
                ins.then_inc(S[name], 1)
                c[name].add()

            def own(ins, name="v_ch"):
                inc(ins, name)
                e.wait_ge(S[name], c[name].value())

            def bcast(ap, shape):
                return ap.to_broadcast(shape)

            def rstd_row():
                c["std_ready"].at += 1
                e.wait_ge(S["std_ready"], c["std_ready"].at)
                st["norm"] += 1
                return row[:, 2 * ((st["norm"] - 1) % 2), :]

            def rms(src, dst, gain, n, shift=None, signal="norm_full"):
                rstd = rstd_row()
                for k in range(n):
                    ins = e.scalar_tensor_tensor(out=dst[:, k, :], in0=src[:, k, :], scalar=gain(k), in1=rstd,
                                                 op0=ALU.mult, op1=ALU.mult)
                    if shift is None and k == n - 1:
                        own(ins, signal)
                    else:
                        inc(ins, "v_ch" if shift is not None else "norm_chunk")
                if shift is not None:
                    base = c["v_ch"].at - n
                    for k in range(n):
                        e.wait_ge(S["v_ch"], base + k + 1)
                        ins = e.tensor_scalar(dst[:, k, :], dst[:, k, :], shift(k), None, ALU.add)
                        if k < n - 1:
                            inc(ins, "norm_chunk")
                        else:
                            own(ins, signal)

            def low_parts(high):
                for k in range(DC):
                    need("nhi_ready", c["nhi_ready"].at + 1)
                    inc(e.tensor_tensor(n_lo[:, k, :], nT[:, k, :], high[:, k, :].bitcast(F32), ALU.subtract), "nlo_ready")

            def skip(n):
                done.add(2 * n)
                st["u"] += n

            def residual(units, gate=None):
                with loop(e, units // 2, [(done, 4), (evacs, 4)]) as i:
                    for p in range(2):
                        for j in range(2):
                            done.add()
                            e.wait_ge(done.sem, done.value())
                            m = i * 4 + (2 * p + j)
                            bank = ps[:, 2 * ((st["u"] + p) % 2) + j, :]
                            dst = hT[:, bass.ds(m, 1), :].rearrange("p a k -> p (a k)")
                            if gate is None:
                                ins = e.tensor_tensor(dst, bank, dst, ALU.add)
                            else:
                                ins = e.scalar_tensor_tensor(out=dst, in0=bank, scalar=mod[:, bass.ds(m + gate, 1)],
                                                             in1=dst, op0=ALU.mult, op1=ALU.add)
                            ins.then_inc(evacs.sem, 1)
                            evacs.add()
                st["u"] += units

            def h_done():
                e.wait_ge(evacs.sem, evacs.value())
                own(e.tensor_copy(mark[:], hT[:, 0, 0:1]), "h_ready")

            e.sem_inc(S["dve_evac"], 4)
            need("hT_in", DC)
            need("params_t", 1)
            own(e.tensor_copy(par[:, :, :].rearrange("p a k -> p (a k)"), ps[:, 4, 0:3 * P]), "params_c")
            need("ws_t", 1)
            own(e.tensor_copy(wsT.rearrange("p a k -> p (a k)")[:, 0:4 * P], ps[:, 5, :]))
            own(e.tensor_copy(wsT.rearrange("p a k -> p (a k)")[:, 4 * P:6 * P], ps[:, 6, 0:2 * P]))
            own(e.memset(wsT[64:128, :, 0:64], 0.0), "ws_ready")
            rms(hT, nT, lambda k: col("g_mix", k), DC)
            low_parts(n_hi)

            e.wait_ge(S["act_evac"], 4 + 6)
            need("consts", 1)
            own(e.tensor_tensor(padA[:, :, TAPS_A - 1:], z[:, 0:3, :], z[:, 3:6, :], ALU.mult))
            for k in range(3):
                inc(e.tensor_scalar(cvA[:, k, :], padA[:, k, 0:T], col("conv_a_w", k), col("conv_a_b", k),
                                    ALU.mult, ALU.add), "v_ch")
            for tap in range(1, TAPS_A):
                for k in range(3):
                    e.wait_ge(S["v_ch"], c["v_ch"].value(2))
                    inc(e.scalar_tensor_tensor(out=cvA[:, k, :], in0=padA[:, k, tap:tap + T],
                                               scalar=col("conv_a_w", 3 * tap + k), in1=cvA[:, k, :],
                                               op0=ALU.mult, op1=ALU.add), "v_ch")
            e.wait_ge(S["v_ch"], c["v_ch"].value())
            own(e.tensor_copy(mark[:], cvA[:, 0, 0:1]), "gl_src")

            def head_center(src):
                c["gl_mean"].at += 1
                e.wait_ge(S["gl_mean"], c["gl_mean"].at)
                for k in range(3):
                    own(e.tensor_tensor(src[:, k, :], src[:, k, :], ps[:, 5 + k, :], ALU.subtract), "gl_cen")

            def head_scale(src):
                c["gl_std"].at += 1
                e.wait_ge(S["gl_std"], c["gl_std"].at)
                own(e.tensor_tensor(src, src, gvar, ALU.mult), "mix_scaled")

            def short_conv():
                own(e.tensor_tensor(padB[:, :, TAPS_B - 1:], z[:, 8:10, :], z[:, 10:12, :], ALU.mult))
                yb = mixT[:, 3:5, :]
                for k in range(2):
                    own(e.tensor_scalar(yb[:, k, :], padB[:, k, 0:T], col("conv_b_w", k), None, ALU.mult))
                    for tap in range(1, TAPS_B):
                        own(e.scalar_tensor_tensor(out=yb[:, k, :], in0=padB[:, k, tap:tap + T],
                                                   scalar=col("conv_b_w", 2 * tap + k), in1=yb[:, k, :],
                                                   op0=ALU.mult, op1=ALU.add))
                own(e.tensor_tensor(yb, yb, z[:, 6:8, :], ALU.mult))

            head_center(cvA)
            e.wait_ge(S["act_evac"], 4 + 18)
            head_scale(cvA)
            own(e.tensor_copy(mark[:], z[:, 15, 0:1]), "gl_src")
            head_center(z[:, 15:18, :])
            short_conv()
            head_scale(z[:, 15:18, :])
            skip(9)
            need("bs_in", 96)
            for k in range(3):
                need("mix_ready", k + 1)
                for q in range(2):
                    rows_ = slice(64 * q, 64 * q + 64)
                    own(e.tensor_tensor(work[rows_, 3, :].rearrange("p (b i) -> p b i", b=TT),
                                        ps[rows_, 5 + q, :].rearrange("p (b i) -> p b i", b=TT),
                                        bsb[rows_, k:k + 1, :].to_broadcast([64, TT, P]), ALU.add))
                own(e.tensor_tensor(mixT[:, 5 + k, :], work[:, 3, :], z[:, 12 + k, :], ALU.mult), "sg_done")

            def modulation(part, bank=0):
                need("ada_cols", part + 1)
                m = mod[:, 24 * part:24 * part + 24]
                own(e.tensor_tensor(m, ps[:, bank, 0:24], col("ada_b_2", 24 * part, 24), ALU.add), "mod_ready")
                gain = col(("norm_mix_2", "norm_ffn_2")[part % 2], 8 * (part // 2), 8)
                own(e.scalar_tensor_tensor(out=gmod[:, part, :], in0=m[:, 8:16], scalar=1.0, in1=gain,
                                           op0=ALU.add, op1=ALU.mult))

            residual(4)
            h_done()

            rms(hT, nT, lambda k: col("g_ffn", k), DC)
            need("ntok_t", 2 * TT)
            low_parts(q_hi)
            modulation(0, bank=7)
            skip(8)
            need("consts", 2)
            used = c["u_used"]
            landed = [Count(s) for s in row_landed]
            hst, gxp = c["hs_ready"], c["gexp"]
            vch, mk, rdy = c["v_ch"], c["hs_read"], c["idx_ready"]
            cmx, gel, xrd, gat = c["cand_max"], c["gelu_ready"], c["x_ready"], c["gates_ready"]

            def signal(ins, count):
                ins.then_inc(count.sem, 1)
                count.add()
                e.wait_ge(count.sem, count.value())
                e.sem_inc(S["vector_step"], 1)

            def chain(ins):
                signal(ins, vch)

            def top16(values, a):
                chain(e.max(top_v[:, a, 0:8], values))
                chain(e.max_index(top_i[:, a, 0:8], top_v[:, a, 0:8], values))
                chain(e.match_replace(values, top_v[:, a, 0:8], values, -3e38))
                chain(e.max(top_v[:, a, 8:16], values))

            def topk(n):
                hst.add()
                e.wait_ge(hst.sem, hst.value())
                e.sem_inc(S["vector_step"], 1)
                for a in range(2):
                    top16(hs[:, a, :], a)
                    ins = e.max_index(top_i[:, a, 8:16], top_v[:, a, 8:16], hs[:, a, :])
                    if a == 0:
                        chain(ins)
                    else:
                        signal(ins, mk)
                chain(e.tensor_tensor(cand, top_v[:, 0, :].rearrange("p (a b) -> p a b", b=1).to_broadcast([P, TOPK, TOPK]),
                                      top_v[:, 1:2, :].to_broadcast([P, TOPK, TOPK]), ALU.add))
                flat = cand.rearrange("p a b -> p (a b)")
                top16(flat, 2)
                chain(e.max_index(top_i[:, 2, 8:16], top_v[:, 2, 8:16], flat))
                signal(e.tensor_scalar(small[:, 1:2], top_v[:, 2, 0:1], -1.0, None, ALU.mult), cmx)
                chain(e.tensor_scalar(pick_i[:, 0, :], top_i[:, 2, :], 4, None, ALU.logical_shift_right))
                chain(e.tensor_scalar(pick_i[:, 1, :], top_i[:, 2, :], TOPK - 1, None, ALU.bitwise_and))
                chain(e.tensor_copy(pick_f, pick_i))
                chain(e.tensor_copy(top_f, top_i[:, 0:2, :]))
                for a in range(2):
                    chain(e.tensor_tensor(onehot, pick_f[:, a, :].rearrange("p (a b) -> p a b", b=1).to_broadcast([P, TOPK, TOPK]),
                                          iota16.rearrange("p (a b) -> p a b", a=1).to_broadcast([P, TOPK, TOPK]),
                                          ALU.is_equal))
                    chain(e.tensor_tensor(onehot, onehot, top_f[:, a:a + 1, :].to_broadcast([P, TOPK, TOPK]), ALU.mult))
                    chain(e.tensor_reduce(ek[:, a, :], onehot, AX.X, ALU.add))
                where = bass.ds(n * TOPK, TOPK)
                signal(e.scalar_tensor_tensor(out=idx_flat[:, where], in0=ek[:, 0, :], scalar=float(KEYS), in1=ek[:, 1, :],
                                              op0=ALU.mult, op1=ALU.add), rdy)
                gxp.add()
                e.wait_ge(gxp.sem, gxp.value())
                chain(e.reciprocal(small[:, 3:4], small[:, 2:3]))
                chain(e.tensor_scalar(gates.rearrange("p n k -> p (n k)")[:, where], gcur, small[:, 3:4], None, ALU.mult))

            def u_row(s, k):
                landed[s].add(16)
                e.wait_ge(used.sem, used.value())
                e.wait_ge(landed[s].sem, landed[s].value())
                e.tensor_tensor_reduce(junk, ring[:, s, :], ps[:, 4:6, :].rearrange("p a k -> p (a k)"), 1.0, 0.0,
                                       ALU.mult, ALU.add, dots[:, k:k + 1]).then_inc(used.sem, 1)
                used.add()

            def coefs(n):
                gel.add()
                e.wait_ge(gel.sem, gel.value())
                e.wait_ge(dgr.sem, dgr.value())
                dgr.add(TOPK)
                signal(e.tensor_tensor(coef, gdots, gates.rearrange("p n k -> p (n k)")[:, bass.ds(n * TOPK, TOPK)],
                                       ALU.mult), c["coef_ready"])

            dgr = c["diag_ready"]
            v0 = vch.at
            topk(0)
            steps = vch.at - v0
            need("sc_ready", 4 * TT + 1)
            own(e.memset(zero, 0.0), "consts_v")
            topk(1)
            def u_mixed(n):
                for half in range(2):
                    for q in range(8):
                        u_row(2 * q, half * 8 + q)
                        landed[2 * q + 1].add(16)
                topk(n + AHEAD)
                coefs(n)

            def tokens():
                xrd.add()
                e.wait_ge(xrd.sem, xrd.value())

            def u_block(b, last):
                with loop(e, HEADS - 1, [(hst, 1), (gxp, 1), (mk, 1), (rdy, 1), (cmx, 1), (gel, 1), (used, TOPK),
                                         (vch, steps), (dgr, TOPK), (c["coef_ready"], 1)]
                          + [(l, 32) for l in landed]) as h:
                    u_mixed(h + b * HEADS + 1)
                if not last:
                    tokens()
                    u_mixed(b * HEADS + HEADS)
                c["acc_t"].add()
                e.wait_ge(c["acc_t"].sem, c["acc_t"].value())
                dst = hT[:, :, bass.ds(b * P, P)]
                signal(e.tensor_tensor(dst, ps[:, 2:4, :].rearrange("p a (c k) -> p (a c) k", k=P), dst, ALU.add),
                       c["acc_added"])

            c["acc_t"].at = c["acc_added"].at = 1
            tokens()
            for s in range(RING):
                u_row(s, s)
            topk(AHEAD)
            coefs(0)
            with loop(e, TT - 1, [(hst, 8), (gxp, 8), (mk, 8), (rdy, 8), (cmx, 8), (gel, 8), (xrd, 1), (used, PER_BLOCK),
                                  (vch, 8 * steps), (dgr, PER_BLOCK), (c["coef_ready"], 8), (c["acc_t"], 1),
                                  (c["acc_added"], 1)] + [(l, 256) for l in landed]) as b:
                u_block(b, False)
            u_block(TT - 1, True)
            for l in landed:
                l.add(16)
            own(e.tensor_copy(mark[:], hT[:, 0, 0:1]), "h_ready")
            rms(hT, nT, lambda k: col("g_ple", k), DC)
            done.add(8)
            for k in range(DC):
                e.wait_ge(S["act_evac"], 4 + 18 + 16 + 8 + k + 1)
                own(e.tensor_tensor(sgT[:, k, :], sgT[:, k, :], peT[:, k, :], ALU.mult))
                ins = e.tensor_tensor(hT[:, k, :], hT[:, k, :], sgT[:, k, :], ALU.add)
                own(ins, "h_ready" if k == DC - 1 else "v_ch")
            done.add(8)
            rms(hT, hT, lambda k: col("g_final", k), DC)
            own(e.tensor_copy(mark[:], hT[:, 0, 0:1]), "h_ready")

            def modulated(layer, k):
                rms(hT, nT, lambda m: gmod[:, 2 * layer + k, m:m + 1], DC,
                    shift=lambda m: mod[:, 48 * layer + 24 * k + m:48 * layer + 24 * k + m + 1])

            def modulated_parts(layer, k):
                rstd = rstd_row()
                for m in range(DC):
                    inc(e.scalar_tensor_tensor(out=nT[:, m, :], in0=hT[:, m, :], scalar=gmod[:, 2 * layer + k, m:m + 1],
                                               in1=rstd, op0=ALU.mult, op1=ALU.mult), "norm_scaled")
                need("norm_scaled", c["norm_scaled"].at)
                for m in range(DC):
                    need("nhi_ready", c["nhi_ready"].at + 1)
                    s_ = 48 * layer + 24 * k + m
                    inc(e.scalar_tensor_tensor(out=n_lo[:, m, :], in0=nT[:, m, :], scalar=mod[:, s_:s_ + 1],
                                               in1=n_hi[:, m, :].bitcast(F32), op0=ALU.add, op1=ALU.subtract), "nlo_ready")

            modulated(0, 0)
            for h in range(GLA_H):
                need("a_ch", h + 1)
                own(e.tensor_scalar(gb[:, h, :], ps[:, 4 + h, :], col("gla_b_gate_2", h), 0.0, ALU.add, ALU.min), "glog_v")
            modulation(1)
            need("glog_l", 1)
            need("consts", 3)
            own(e.tensor_tensor(gtmp, gb, gtmp2, ALU.subtract))
            for h in range(GLA_H):
                own(e.tensor_tensor_scan(gb[:, h, :], reset, gtmp[:, h, :], 0.0, ALU.mult, ALU.add))
            runs = gb.rearrange("p h (i s) -> p (h i) s", s=GLA_SUB)
            own(e.tensor_tensor(gtmp.rearrange("p h (i s) -> p (h i) s", s=GLA_SUB), runs,
                                runs[:, :, 8:9].to_broadcast([P, 4 * T // GLA_SUB, GLA_SUB]), ALU.subtract), "dq_ready")
            gbg, gkg = gsubs(gb), gsubs(gk)

            def k_diff(i):
                n = 16 * (i + 1)
                if i >= 2:
                    need("amat_done", i - 1)
                own(e.tensor_tensor(kd_g(i % 2)[:, :, 0:n], gbg[:, :, 16 * i + 8:16 * i + 9].to_broadcast([P, GLA_G, n]),
                                    gbg[:, :, 0:n], ALU.subtract), "dk_ready")

            k_diff(0)
            k_diff(1)
            e.wait_ge(S["act_evac"], 4 + 50)
            need("dq_exp", 1)
            own(e.tensor_tensor(qsub, qsub, gq, ALU.mult), "q_sub")
            for i in range(8):
                n = 16 * (i + 1)
                need("dk_exp", i + 1)
                own(e.tensor_tensor(kd_g(i % 2)[:, :, 0:n], kd_g(i % 2)[:, :, 0:n], gkg[:, :, 0:n], ALU.mult), "k_sub")
                if i + 2 < 8:
                    k_diff(i + 2)
            skip(12)
            own(e.tensor_tensor(gsubs(gtmp2), gbg[:, :, P - 1:P].to_broadcast([P, GLA_G, P]), gbg, ALU.subtract), "ew_ready")
            need("ew_exp", 3)
            own(e.tensor_tensor(gq, gq, gtmp, ALU.mult), "ew_done")
            own(e.tensor_tensor(gtmp2, gtmp2, gk, ALU.mult), "kw_ready")
            need("amat_done", 8)
            for h in range(GLA_H):
                own(e.tensor_tensor(amat[:, 4 * h:4 * h + 4, :], ps[:, 4 + h, :].rearrange("p (a k) -> p a k", a=4),
                                    keep.rearrange("p (a k) -> p a k", a=1).to_broadcast([P, 4, P]), ALU.mult), "a_ready")
            for i in range(16):
                t, h = divmod(i, GLA_H)
                need("o_evac", i + 1)
                src = ps[:, 4 + i % 4, 2 * P:4 * P]
                if t == 0:
                    ins = e.tensor_copy(state[:, h, :], src)
                elif t < TT - 1:
                    ins = e.scalar_tensor_tensor(out=state[:, h, :], in0=state[:, h, :],
                                                 scalar=elast[:, h * TT + t:h * TT + t + 1], in1=src,
                                                 op0=ALU.mult, op1=ALU.add)
                else:
                    break
                own(ins, "s_new")
            modulation(2)
            need("gr_ready", 2)
            need("ms_ready", st["norm"] + 1)
            for k in range(DC):
                inc(e.scalar_tensor_tensor(out=goT[:, k, :], in0=goT[:, k, :], scalar=col("gla_g_out_2", k % 2),
                                           in1=gr[:, k, :], op0=ALU.mult, op1=ALU.mult), "v_ch")
            c["std_ready"].at += 1
            e.wait_ge(S["std_ready"], c["std_ready"].at)
            need("v_ch", c["v_ch"].at)
            for h in range(GLA_H):
                for k in (2 * h, 2 * h + 1):
                    inc(e.tensor_tensor(goT[:, k, :], goT[:, k, :], gtmp2[:, h, :], ALU.mult), "go_chunk")
            need("go_chunk", DC)
            low_parts(n_hi)
            residual(4, gate=16)
            h_done()

            def ffn(layer):
                modulated_parts(layer, 1)
                raw, hh = c["hid_raw"], c["hid_hi_ready"]
                act = Count(S["act_evac"], st["act"])
                with loop(e, FH, [(done, 4), (evacs, 2), (act, 2), (raw, 2), (hh, 2)]) as i:
                    done.add(2)
                    for j in range(2):
                        act.add()
                        e.wait_ge(act.sem, act.value())
                        done.add()
                        e.wait_ge(done.sem, done.value())
                        e.tensor_tensor(hid[:, bass.ds(i * 2 + j, 1), :].rearrange("p a k -> p (a k)"), ps[:, 2 + j, :],
                                        gsil[:, j, :], ALU.mult).then_inc(raw.sem, 1)
                        raw.add()
                        e.wait_ge(raw.sem, raw.value())
                        e.sem_inc(evacs.sem, 1)
                        evacs.add()
                    for j in range(2):
                        hh.add()
                        e.wait_ge(hh.sem, hh.value())
                        m = bass.ds(i * 2 + j, 1)
                        e.tensor_tensor(hid_l[:, m, :].rearrange("p a k -> p (a k)"), hid[:, m, :].rearrange("p a k -> p (a k)"),
                                        hid_h[:, m, :].bitcast(F32).rearrange("p a k -> p (a k)"), ALU.subtract
                                        ).then_inc(S["hid_ready"], 1)
                st["act"] = act.at
                with loop(e, 2, [(done, 8), (evacs, 4)]) as i:
                    for half in range(2):
                        done.add(2)
                        for j in range(2):
                            done.add()
                            e.wait_ge(done.sem, done.value())
                            m = i * 4 + (2 * half + j)
                            dst = hT[:, bass.ds(m, 1), :].rearrange("p a k -> p (a k)")
                            e.scalar_tensor_tensor(out=dst, in0=ps[:, 2 * half + j, :],
                                                   scalar=mod[:, bass.ds(m + (48 * layer + 40), 1)], in1=dst,
                                                   op0=ALU.mult, op1=ALU.add).then_inc(evacs.sem, 1)
                            evacs.add()
                st["u"] += 30
                h_done()

            st["act"] = 4 + 18 + 16 + 16 + 24
            ffn(0)

            modulated_parts(1, 0)
            need("pos_in", 16)
            own(e.tensor_copy(ang, pos_i))
            own(e.tensor_scalar(ang, ang, col("inv_freq"), None, ALU.mult))
            for q, turn in ((0, 0.25), (1, 0.0)):
                n_, r_ = rtmp[:, q, :], tri[:, q, :]
                own(e.tensor_scalar(n_, ang, float(1 / (2 * np.pi)), turn, ALU.mult, ALU.add))
                own(e.tensor_scalar(n_, n_, ROUND, None, ALU.add))
                own(e.tensor_scalar(n_, n_, ROUND, None, ALU.subtract))
                own(e.scalar_tensor_tensor(out=r_, in0=n_, scalar=-PI2_A, in1=ang, op0=ALU.mult, op1=ALU.add))
                own(e.scalar_tensor_tensor(out=r_, in0=n_, scalar=-PI2_B, in1=r_, op0=ALU.mult, op1=ALU.add))
                own(e.scalar_tensor_tensor(out=r_, in0=n_, scalar=-PI2_C, in1=r_, op0=ALU.mult, op1=ALU.add))
                own(e.tensor_scalar(r_, r_, float(turn * 2 * np.pi), PI_IN, ALU.add, ALU.min))
                own(e.tensor_scalar(n_, r_, -PI_IN, None, ALU.max))
            own(e.tensor_copy(mark[:], ang[:, 0:1]), "angle_ready")
            e.wait_ge(S["act_evac"], st["act"] + 6)
            rms(cT6, cT6, lambda k: col("mla_g_q_2", k), 3)
            rms(cT6[:, 3:5, :], cT6[:, 3:5, :], lambda k: col("mla_g_kv_2", k), 2)
            e.wait_ge(S["act_evac"], st["act"] + 6 + 12 + 16)
            st["act"] += 34
            need("trig_ready", 1)
            for r in range(5):
                x = cT6[:, 5, :] if r == 4 else qr[:, r, :]
                need("rot_done", r + 1)
                own(e.tensor_tensor(rtmp[:, 0, :], ps[:, 4 + r % 4, :], tri[:, 1, :], ALU.mult), "rope_read")
                own(e.tensor_tensor(x, x, tri[:, 0, :], ALU.mult))
                own(e.tensor_tensor(x, x, rtmp[:, 0, :], ALU.add), "rope_ready")
            need("consts", 4)
            SCALE = float(NOPE + ROPE) ** -0.5

            def peak(i):
                t = i % TT
                n = (t + 1) * P
                b = sbank(i, T)
                need("att_s", i + 1)
                own(e.tensor_tensor(b[:, t * P:n], b[:, t * P:n], cmask, ALU.add))
                own(e.tensor_reduce(attsm[:, i % 4, 0:1], b[:, 0:n], AX.X, ALU.max))
                own(e.tensor_scalar(attsm[:, i % 4, 1:2], attsm[:, i % 4, 0:1], -SCALE, None, ALU.mult), "att_m")

            def low_out(h):
                need("att_oh", h + 1)
                own(e.tensor_tensor(n_lo[:, h, :], ps[:, 6 + h % 2, :], n_hi[:, h, :].bitcast(F32), ALU.subtract), "att_oe")

            peak(0)
            peak(1)
            for i in range(MLA_H * TT):
                if i + 2 < MLA_H * TT:
                    peak(i + 2)
                n = (i % TT + 1) * P
                need("att_p", i + 1)
                own(e.reciprocal(attsm[:, i % 4, 3:4], attsm[:, i % 4, 2:3]))
                own(e.tensor_scalar(pp[:, i % 4, 0:n], pp[:, i % 4, 0:n], attsm[:, i % 4, 3:4], None, ALU.mult), "att_n")
                if i > TT and i % TT == 1:
                    low_out(i // TT - 1)
            low_out(MLA_H - 1)
            skip(3 + 4 + 8)
            modulation(3)
            done.add(4)
            residual(4, gate=48 + 16)
            h_done()
            ffn(1)
            rms(hT, nT, lambda k: col("final_norm_2", k), DC)


_INS = ["x", "p", "g_mix", "w_in", "conv_a_w", "conv_a_b", "ln_a_g", "ln_a_b", "conv_b_w", "ln_c_g", "ln_c_b", "w_s",
        "b_s", "w_out", "g_ffn", "w_q", "sub_keys", "expert_u", "expert_v", "g_ple", "w_pe", "w_pg", "g_final",
        "c_2", "positions_2", "ada_w_2", "ada_b_2", "norm_mix_2", "norm_ffn_2", "gla_w_in_2", "gla_w_gate_2",
        "gla_b_gate_2", "gla_g_out_2", "gla_w_out_2", "mla_w_in_2", "mla_g_q_2", "mla_w_q_up_2", "mla_g_kv_2",
        "mla_w_kv_up_2", "mla_w_out_2", "ffn_w_in_2", "ffn_w_out_2", "final_norm_2"]


def kernel(**inputs):
    import numpy as _np
    import concourse.bacc as _bacc
    from concourse import mybir as _mybir
    from concourse.bass_utils import run_bass_kernel_spmd as _run

    nc = _bacc.Bacc("TRN2", target_bir_lowering=False, num_devices=1)
    given = {name: _np.ascontiguousarray(inputs[name]) for name in _INS}
    freq = _np.float32(10000.0) ** (-_np.arange(0, ROPE, 2, dtype=_np.float32) / _np.float32(ROPE))
    given["inv_freq"] = _np.tile(_np.repeat(freq, 2), 2).astype(_np.float32).reshape(1, P)
    arrays, args = {}, {}
    for name, a in given.items():
        arrays[f"in_{name}_dram"] = a
        args[name] = nc.dram_tensor(f"in_{name}_dram", a.shape, _mybir.dt.from_np(a.dtype), kind="ExternalInput").ap()
    out = nc.dram_tensor("out_0_dram", (1, T, D), F32, kind="ExternalOutput").ap()
    build(nc, args, out)
    r = _run(nc, [arrays], core_ids=[0])
    return r.results[0]["out_0_dram"]
```
